# Optimizing a Trainium2 kernel written in Bass

```python
import jax, jax.numpy as jnp
from jax import lax
import numpy as np
import math

D_MODEL = 1024
BATCH = 1
SEQ = 512
DEPTH = 1

POOL_WINDOWS = (2, 4, 8, 16)
POOL_GROUPS = len(POOL_WINDOWS)
POOL_WIDTH = D_MODEL
POOL_GROUP = POOL_WIDTH // POOL_GROUPS
SGU_CHUNK = 128
SGU_WIDTH = D_MODEL
SGU_HEADS = 8
SGU_HEAD_DIM = SGU_WIDTH // SGU_HEADS
N_BRANCHES = 2
IN_WIDTH = POOL_WIDTH + 2 * SGU_WIDTH + N_BRANCHES * D_MODEL
D_FF = 2816
CONV_WIDTH = 3
PLE_DIM = 256
EPS = 1e-6


def rmsnorm(x, g):
    xf = x.astype(jnp.float32)
    y = xf * lax.rsqrt(jnp.mean(xf * xf, axis=-1, keepdims=True) + EPS)
    return (y * g.astype(jnp.float32)).astype(x.dtype)

def pool_mixer(h, w_pool, pool_scale):
    T = h.shape[1]
    hf = h.astype(jnp.float32)
    c = jnp.cumsum(hf, axis=1)
    t = jnp.arange(T)
    outs = []
    for gi, w in enumerate(POOL_WINDOWS):
        sl = slice(gi * POOL_GROUP, (gi + 1) * POOL_GROUP)
        cg = c[..., sl]
        prev = jnp.pad(cg, ((0, 0), (w, 0), (0, 0)))[:, :T]
        cnt = jnp.minimum(t + 1, w).astype(jnp.float32)[None, :, None]
        outs.append((cg - prev) / cnt - hf[..., sl])
    pooled = jnp.stack(outs, axis=2).astype(h.dtype)
    y = jnp.einsum('btgc,gcd->btgd', pooled, w_pool)
    return y.reshape(h.shape) * pool_scale

def spatial_gating(z_uv, sgu_norm, w_spatial, b_spatial):
    B, T, _ = z_uv.shape
    z = jax.nn.gelu(z_uv, approximate=False)
    u, v = z[..., :SGU_WIDTH], z[..., SGU_WIDTH:]
    v = rmsnorm(v, sgu_norm)
    nc = T // SGU_CHUNK
    v = v.reshape(B, nc, SGU_CHUNK, SGU_HEADS, SGU_HEAD_DIM)
    mask = jnp.tril(jnp.ones((SGU_CHUNK, SGU_CHUNK), dtype=w_spatial.dtype))
    ws = w_spatial * mask[None]
    mixed = jnp.einsum('hts,bnshd->bnthd', ws, v)
    mixed = mixed + jnp.transpose(b_spatial)[None, None, :, :, None]
    return u * mixed.reshape(B, T, SGU_WIDTH)

def conv_ffn(h, w_up, conv_w, conv_b, w_down):
    T = h.shape[1]
    up = h @ w_up
    up_pad = jnp.pad(up, ((0, 0), (CONV_WIDTH - 1, 0), (0, 0)))
    conv = conv_b
    for k in range(CONV_WIDTH):
        conv = conv + conv_w[k] * up_pad[:, k:k + T]
    a, b = conv[..., :D_FF], conv[..., D_FF:]
    return (jax.nn.gelu(a, approximate=False) * b) @ w_down

def first_inputs(seed: int = 0) -> dict:
    key = jax.random.key(seed)
    ks = jax.random.split(key, 24)
    f32 = jnp.float32
    L, D = DEPTH, D_MODEL

    def nrm(k, shape, scale):
        return jax.random.normal(k, shape, f32) * scale

    def gain(k, shape):
        return 1.0 + 0.05 * jax.random.normal(k, shape, f32)

    return {
        "x": nrm(ks[0], (BATCH, SEQ, D), 1.0),
        "p": nrm(ks[1], (DEPTH, BATCH, SEQ, PLE_DIM), 1.0),
        "mix_norm": gain(ks[2], (L, D)),
        "w_in": nrm(ks[3], (L, D, IN_WIDTH), D ** -0.5),
        "w_pool": nrm(ks[4], (L, POOL_GROUPS, POOL_GROUP, POOL_GROUP), POOL_GROUP ** -0.5),
        "pool_scale": gain(ks[5], (L, POOL_WIDTH)),
        "sgu_norm": gain(ks[6], (L, SGU_WIDTH)),
        "w_spatial": nrm(ks[7], (L, SGU_HEADS, SGU_CHUNK, SGU_CHUNK), 0.5 * SGU_CHUNK ** -0.5),
        "b_spatial": gain(ks[8], (L, SGU_HEADS, SGU_CHUNK)),
        "w_branch_a": nrm(ks[9], (L, POOL_WIDTH, D), POOL_WIDTH ** -0.5),
        "w_branch_b": nrm(ks[10], (L, SGU_WIDTH, D), SGU_WIDTH ** -0.5),
        "w_out": nrm(ks[11], (L, D, D), D ** -0.5),
        "ffn_norm": gain(ks[12], (L, D)),
        "w_up": nrm(ks[13], (L, D, 2 * D_FF), D ** -0.5),
        "conv_w": nrm(ks[14], (L, CONV_WIDTH, 2 * D_FF), CONV_WIDTH ** -0.5),
        "conv_b": nrm(ks[15], (L, 2 * D_FF), 0.02),
        "w_down": nrm(ks[16], (L, D_FF, D), D_FF ** -0.5),
        "ple_norm": gain(ks[17], (L, D)),
        "w_ple_gate": nrm(ks[18], (L, D, D), D ** -0.5),
        "w_ple": nrm(ks[19], (L, PLE_DIM, D), PLE_DIM ** -0.5),
        "final_norm": gain(ks[20], (D,)),
    }

def first_block(x, p, mix_norm, w_in, w_pool, pool_scale, sgu_norm, w_spatial, b_spatial,
              w_branch_a, w_branch_b, w_out, ffn_norm, w_up, conv_w, conv_b, w_down,
              ple_norm, w_ple_gate, w_ple, final_norm):
    o_uv = POOL_WIDTH
    o_gate = POOL_WIDTH + 2 * SGU_WIDTH
    for i in range(DEPTH):
        h = rmsnorm(x, mix_norm[i])
        z = h @ w_in[i]
        z_pool = z[..., :o_uv]
        z_uv = z[..., o_uv:o_gate]
        z_gate = z[..., o_gate:]
        y_a = pool_mixer(z_pool, w_pool[i], pool_scale[i]) @ w_branch_a[i]
        y_b = spatial_gating(z_uv, sgu_norm[i], w_spatial[i], b_spatial[i]) @ w_branch_b[i]
        gates = jax.nn.sigmoid(z_gate.astype(jnp.float32)).astype(x.dtype)
        g_a, g_b = gates[..., :D_MODEL], gates[..., D_MODEL:]
        x = x + (g_a * y_a + g_b * y_b) @ w_out[i]
        h = rmsnorm(x, ffn_norm[i])
        x = x + conv_ffn(h, w_up[i], conv_w[i], conv_b[i], w_down[i])
        gate = jax.nn.sigmoid((rmsnorm(x, ple_norm[i]) @ w_ple_gate[i]).astype(jnp.float32)).astype(x.dtype)
        x = x + gate * (p[i] @ w_ple[i])
    return rmsnorm(x, final_norm)


DEPTH_2 = 2

N_MIXERS = 2
A_HEADS = 16
A_KV_HEADS = 2
A_HEAD_DIM = 64
WINDOW = 128
BLOCK = 128
NUM_BUCKETS = 32
MAX_DISTANCE = 128
B_HEADS = 16
Q_LORA = 256
KV_LORA = 128
QK_NOPE = 64
QK_ROPE = 32
V_DIM = 64
ROPE_BASE = 10000.0
NEG = -1e30

N_A_LAYERS = (DEPTH_2 + 1) // 2
N_B_LAYERS = DEPTH_2 // 2
A_IN_COLS = (A_HEADS + 2 * A_KV_HEADS) * A_HEAD_DIM
B_IN_COLS = Q_LORA + KV_LORA + QK_ROPE


def rmsnorm_2(x, g):
    xf = x.astype(jnp.float32)
    y = xf * lax.rsqrt(jnp.mean(xf * xf, axis=-1, keepdims=True) + EPS)
    return (y * g.astype(jnp.float32)).astype(x.dtype)

def swiglu(h, wg, wu, wd):
    return (jax.nn.silu(h @ wg) * (h @ wu)) @ wd

def t5_bucket(dist):
    n = jnp.maximum(dist, 0)
    max_exact = NUM_BUCKETS // 2
    large = max_exact + (jnp.log(jnp.maximum(n, 1).astype(jnp.float32) / max_exact)
                         / math.log(MAX_DISTANCE / max_exact)
                         * (NUM_BUCKETS - max_exact)).astype(jnp.int32)
    large = jnp.minimum(large, NUM_BUCKETS - 1)
    return jnp.where(n < max_exact, n, large)

def apply_rope(t, pos):
    half = QK_ROPE // 2
    inv_freq = ROPE_BASE ** (-jnp.arange(0, QK_ROPE, 2, dtype=jnp.float32) / QK_ROPE)
    ang = pos.astype(jnp.float32)[..., None] * inv_freq
    cos = jnp.cos(ang)[:, :, None, :]
    sin = jnp.sin(ang)[:, :, None, :]
    t1, t2 = t[..., :half].astype(jnp.float32), t[..., half:].astype(jnp.float32)
    return jnp.concatenate([t1 * cos - t2 * sin, t2 * cos + t1 * sin], axis=-1).astype(t.dtype)

def band(t, nb):
    B = t.shape[0]
    rest = t.shape[2:]
    pad = jnp.zeros((B, BLOCK) + rest, t.dtype)
    tp = jnp.concatenate([pad, t], axis=1).reshape((B, nb + 1, BLOCK) + rest)
    return jnp.concatenate([tp[:, :-1], tp[:, 1:]], axis=2)

def sliding_window_attention(h, pos, rel_bias, w_in, q_gain, k_gain, sinks, w_out):
    B, S, _ = h.shape
    nb = S // BLOCK
    G = A_HEADS // A_KV_HEADS
    qkv = h @ w_in
    q, k, v = jnp.split(qkv, [A_HEADS * A_HEAD_DIM, (A_HEADS + A_KV_HEADS) * A_HEAD_DIM], axis=-1)
    q = rmsnorm_2(q.reshape(B, S, A_HEADS, A_HEAD_DIM), q_gain)
    k = rmsnorm_2(k.reshape(B, S, A_KV_HEADS, A_HEAD_DIM), k_gain)
    v = v.reshape(B, S, A_KV_HEADS, A_HEAD_DIM)
    q = q.reshape(B, nb, BLOCK, A_KV_HEADS, G, A_HEAD_DIM)
    kb, vb = band(k, nb), band(v, nb)
    posb = band(pos, nb)
    scale = A_HEAD_DIM ** -0.5
    scores = jnp.einsum('bnqkgd,bnskd->bnkgqs', q, kb).astype(jnp.float32) * scale
    dist = pos.reshape(B, nb, BLOCK)[..., :, None] - posb[..., None, :]
    bias = rel_bias[t5_bucket(dist)].astype(jnp.float32)
    bias = bias.reshape(B, nb, BLOCK, 2 * BLOCK, A_KV_HEADS, G).transpose(0, 1, 4, 5, 2, 3)
    scores = scores + bias
    qi = jnp.arange(BLOCK)[:, None] + BLOCK
    si = jnp.arange(2 * BLOCK)[None, :]
    rel = qi - si
    blk = jnp.arange(nb)[:, None, None]
    valid = (rel >= 0) & (rel < WINDOW) & (blk * BLOCK + si - BLOCK >= 0)
    scores = jnp.where(valid[None, :, None, None], scores, NEG)
    sink = sinks.astype(jnp.float32).reshape(A_KV_HEADS, G)[None, None, :, :, None, None]
    m = jnp.maximum(jnp.max(scores, axis=-1, keepdims=True), sink)
    p = jnp.exp(scores - m)
    denom = jnp.sum(p, axis=-1, keepdims=True) + jnp.exp(sink - m)
    probs = (p / denom).astype(v.dtype)
    o = jnp.einsum('bnkgqs,bnskd->bnqkgd', probs, vb).reshape(B, S, A_HEADS * A_HEAD_DIM)
    return o @ w_out

def latent_attention(h, pos, w_in, q_norm, kv_norm, w_uq, w_ukv, q_gain, k_gain, w_out):
    B, S, _ = h.shape
    nb = S // BLOCK
    dqk = QK_NOPE + QK_ROPE
    c = h @ w_in
    c_q, c_kv, k_rope = jnp.split(c, [Q_LORA, Q_LORA + KV_LORA], axis=-1)
    q = (rmsnorm_2(c_q, q_norm) @ w_uq).reshape(B, S, B_HEADS, dqk)
    kv = (rmsnorm_2(c_kv, kv_norm) @ w_ukv).reshape(B, S, B_HEADS, QK_NOPE + V_DIM)
    k_nope, v = jnp.split(kv, [QK_NOPE], axis=-1)
    k = jnp.concatenate(
        [k_nope, jnp.broadcast_to(k_rope[:, :, None, :], (B, S, B_HEADS, QK_ROPE))], axis=-1)
    q = rmsnorm_2(q, q_gain)
    k = rmsnorm_2(k, k_gain)
    q = jnp.concatenate([q[..., :QK_NOPE], apply_rope(q[..., QK_NOPE:], pos)], axis=-1)
    k = jnp.concatenate([k[..., :QK_NOPE], apply_rope(k[..., QK_NOPE:], pos)], axis=-1)
    scale = dqk ** -0.5
    qb = q.reshape(B, nb, BLOCK, B_HEADS, dqk).transpose(1, 0, 2, 3, 4)
    key_idx = jnp.arange(S)

    def attend(args):
        q_blk, n = args
        s = jnp.einsum('bqhd,bshd->bhqs', q_blk, k).astype(jnp.float32) * scale
        q_idx = n * BLOCK + jnp.arange(BLOCK)
        s = jnp.where(key_idx[None, :] <= q_idx[:, None], s, NEG)
        p = jax.nn.softmax(s, axis=-1).astype(v.dtype)
        return jnp.einsum('bhqs,bshd->bqhd', p, v)

    o = lax.map(attend, (qb, jnp.arange(nb)))
    o = o.transpose(1, 0, 2, 3, 4).reshape(B, S, B_HEADS * V_DIM)
    return o @ w_out

def second_inputs(seed: int = 0) -> dict:
    key = jax.random.key(seed)
    ks = jax.random.split(key, 32)
    f32 = jnp.float32

    def w(k, shape, fan_in):
        return jax.random.normal(k, shape, f32) * (fan_in ** -0.5)

    def gain(k, shape):
        return 1.0 + 0.05 * jax.random.normal(k, shape, f32)

    x = jax.random.normal(ks[0], (BATCH, SEQ, D_MODEL), f32)
    offsets = jax.random.randint(ks[1], (BATCH, 1), 0, 64, dtype=jnp.int32)
    positions = (jnp.arange(SEQ, dtype=jnp.int32)[None, :] + offsets).astype(jnp.int32)
    return {
        "x": x,
        "positions": positions,
        "rel_bias": 0.5 * jax.random.normal(ks[2], (NUM_BUCKETS, A_HEADS), f32),
        "ffn_norm1": gain(ks[3], (DEPTH_2, D_MODEL)),
        "ffn1_wg": w(ks[4], (DEPTH_2, D_MODEL, D_FF), D_MODEL),
        "ffn1_wu": w(ks[5], (DEPTH_2, D_MODEL, D_FF), D_MODEL),
        "ffn1_wd": w(ks[6], (DEPTH_2, D_FF, D_MODEL), D_FF),
        "mix_norm": gain(ks[7], (DEPTH_2, D_MODEL)),
        "ffn_norm2": gain(ks[8], (DEPTH_2, D_MODEL)),
        "ffn2_wg": w(ks[9], (DEPTH_2, D_MODEL, D_FF), D_MODEL),
        "ffn2_wu": w(ks[10], (DEPTH_2, D_MODEL, D_FF), D_MODEL),
        "ffn2_wd": w(ks[11], (DEPTH_2, D_FF, D_MODEL), D_FF),
        "a_w_in": w(ks[12], (N_A_LAYERS, D_MODEL, A_IN_COLS), D_MODEL),
        "a_q_gain": gain(ks[13], (N_A_LAYERS, A_HEAD_DIM)),
        "a_k_gain": gain(ks[14], (N_A_LAYERS, A_HEAD_DIM)),
        "a_sinks": jax.random.normal(ks[15], (N_A_LAYERS, A_HEADS), f32),
        "a_w_out": w(ks[16], (N_A_LAYERS, A_HEADS * A_HEAD_DIM, D_MODEL), A_HEADS * A_HEAD_DIM),
        "b_w_in": w(ks[17], (N_B_LAYERS, D_MODEL, B_IN_COLS), D_MODEL),
        "b_q_norm": gain(ks[18], (N_B_LAYERS, Q_LORA)),
        "b_kv_norm": gain(ks[19], (N_B_LAYERS, KV_LORA)),
        "b_w_uq": w(ks[20], (N_B_LAYERS, Q_LORA, B_HEADS * (QK_NOPE + QK_ROPE)), Q_LORA),
        "b_w_ukv": w(ks[21], (N_B_LAYERS, KV_LORA, B_HEADS * (QK_NOPE + V_DIM)), KV_LORA),
        "b_q_gain": gain(ks[22], (N_B_LAYERS, QK_NOPE + QK_ROPE)),
        "b_k_gain": gain(ks[23], (N_B_LAYERS, QK_NOPE + QK_ROPE)),
        "b_w_out": w(ks[24], (N_B_LAYERS, B_HEADS * V_DIM, D_MODEL), B_HEADS * V_DIM),
    }

def second_block(x, positions, rel_bias, ffn_norm1, ffn1_wg, ffn1_wu, ffn1_wd, mix_norm,
              ffn_norm2, ffn2_wg, ffn2_wu, ffn2_wd, a_w_in, a_q_gain, a_k_gain, a_sinks,
              a_w_out, b_w_in, b_q_norm, b_kv_norm, b_w_uq, b_w_ukv, b_q_gain, b_k_gain,
              b_w_out):
    for i in range(DEPTH_2):
        x = x + 0.5 * swiglu(rmsnorm_2(x, ffn_norm1[i]), ffn1_wg[i], ffn1_wu[i], ffn1_wd[i])
        h = rmsnorm_2(x, mix_norm[i])
        j = i // N_MIXERS
        if i % N_MIXERS == 0:
            x = x + sliding_window_attention(h, positions, rel_bias, a_w_in[j], a_q_gain[j],
                                             a_k_gain[j], a_sinks[j], a_w_out[j])
        else:
            x = x + latent_attention(h, positions, b_w_in[j], b_q_norm[j], b_kv_norm[j],
                                     b_w_uq[j], b_w_ukv[j], b_q_gain[j], b_k_gain[j], b_w_out[j])
        x = x + 0.5 * swiglu(rmsnorm_2(x, ffn_norm2[i]), ffn2_wg[i], ffn2_wu[i], ffn2_wd[i])
    return x


def setup_inputs(seed=0):
    out = dict(first_inputs(seed))
    for name, value in second_inputs(seed + 1).items():
        if name != "x":
            out[name + "_2"] = value
    return out


def reference(
    x, p, mix_norm, w_in, w_pool, pool_scale, sgu_norm, w_spatial, b_spatial, w_branch_a,
    w_branch_b, w_out, ffn_norm, w_up, conv_w, conv_b, w_down, ple_norm, w_ple_gate, w_ple,
    final_norm, positions_2, rel_bias_2, ffn_norm1_2, ffn1_wg_2, ffn1_wu_2, ffn1_wd_2,
    mix_norm_2, ffn_norm2_2, ffn2_wg_2, ffn2_wu_2, ffn2_wd_2, a_w_in_2, a_q_gain_2, a_k_gain_2,
    a_sinks_2, a_w_out_2, b_w_in_2, b_q_norm_2, b_kv_norm_2, b_w_uq_2, b_w_ukv_2, b_q_gain_2,
    b_k_gain_2, b_w_out_2,
):
    x = first_block(
        x, p, mix_norm, w_in, w_pool, pool_scale, sgu_norm, w_spatial, b_spatial, w_branch_a,
        w_branch_b, w_out, ffn_norm, w_up, conv_w, conv_b, w_down, ple_norm, w_ple_gate, w_ple,
        final_norm,
    )
    return second_block(
        x, positions_2, rel_bias_2, ffn_norm1_2, ffn1_wg_2, ffn1_wu_2, ffn1_wd_2, mix_norm_2,
        ffn_norm2_2, ffn2_wg_2, ffn2_wu_2, ffn2_wd_2, a_w_in_2, a_q_gain_2, a_k_gain_2,
        a_sinks_2, a_w_out_2, b_w_in_2, b_q_norm_2, b_kv_norm_2, b_w_uq_2, b_w_ukv_2,
        b_q_gain_2, b_k_gain_2, b_w_out_2,
    )


_drawn_inputs = setup_inputs


def setup_inputs(seed=0):
    import zlib

    import numpy as np

    out = dict(_drawn_inputs(seed))
    spreads = {}
    factors = {'sgu_norm': 8.0,
     'b_spatial': 3.188,
     'conv_b': 3.411,
     'ple_norm': 6.614,
     'a_q_gain_2': 6.822,
     'a_k_gain_2': 6.367,
     'a_sinks_2': 3.137,
     'b_q_norm_2': 8.0,
     'b_kv_norm_2': 5.158,
     'b_q_gain_2': 8.0,
     'b_k_gain_2': 7.998}
    for name, (base, spread) in spreads.items():
        noise = np.random.default_rng([zlib.crc32(name.encode()), seed]).standard_normal(out[name].shape)
        drawn = base * np.exp(spread * noise) if base else spread * noise
        out[name] = __import__('jax').numpy.asarray(drawn.astype(out[name].dtype))
    for name, factor in factors.items():
        out[name] = (out[name] * factor).astype(out[name].dtype)
    return out
```

```python
import math
from contextlib import ExitStack

import numpy as np
import concourse.bass as bass
from concourse import mybir

F32 = mybir.dt.float32
F32R = mybir.dt.float32r
BF16 = mybir.dt.bfloat16
I32 = mybir.dt.int32
ALU = mybir.AluOpType
ACT = mybir.ActivationFunctionType
AX = mybir.AxisListType

T, D, DFF = 512, 1024, 2816
EPS = 1e-6
NEG = -1e30
AH, BH = 16, 16
ROPE_HALF = 16
LOWEST = -3.0e38


def bucket_bounds():
    def bucket(n):
        if n < 16:
            return n
        return min(31, 16 + int(math.log(n / 16) / math.log(8) * 16))
    return [min(n for n in range(200) if bucket(n) >= k) for k in range(1, 32)]


class Queue:

    def __init__(self, engine, sem):
        self.e, self.sem, self.n, self.seen = engine, sem, 0, {}

    def wait(self, *after):
        for tok in after:
            if tok is None:
                continue
            if isinstance(tok, list):
                self.wait(*tok)
                continue
            sem, v = tok
            if self.seen.get(sem.name, 0) < v:
                self.seen[sem.name] = v
                self.e.wait_ge(sem, v)

    def add(self, fn, *after, signal=True):
        self.wait(*after)
        ins = fn(self.e)
        if not signal:
            return None
        self.n += 1
        ins.then_inc(self.sem, 1)
        return (self.sem, self.n)

    def dma(self, sem, out, in_, *after):
        self.wait(*after)
        sem[1] += 16
        self.e.dma_start(out, in_).then_inc(sem[0], 16)
        return (sem[0], sem[1])


class Ring:

    def __init__(self, views):
        self.views, self.free, self.i = views, [[] for _ in views], -1

    def take(self):
        self.i = (self.i + 1) % len(self.views)
        was, self.free[self.i] = self.free[self.i], []
        return self.i, self.views[self.i], was

    def part(self, k):
        other = Ring(self.views[-k:])
        other.free = self.free[-k:]
        self.views, self.free, self.i = self.views[:-k], self.free[:-k], -1
        return other

    def join(self, other):
        self.views, self.free = self.views + other.views, self.free + other.free

    def done(self, i, *toks):
        self.free[i] += [t for t in toks if t is not None]


def program(nc, a, out):
    ctx = ExitStack()
    with ctx:
        build(nc, a, out, ctx)


def build(nc, a, out, ctx):
    def sb(name, shape, dt=F32):
        return ctx.enter_context(nc.sbuf_tensor(name, shape, dt))

    def sem(name):
        return ctx.enter_context(nc.semaphore(name))

    ctx.enter_context(nc.allow_non_contiguous_dma(reason="a few short columns"))
    PE, AC, DV, PO, SP = (Queue(e, sem(n)) for e, n in ((nc.tensor, "s_pe"), (nc.scalar, "s_act"), (nc.vector, "s_dve"),
                                                        (nc.gpsimd, "s_pool"), (nc.sync, "s_sp")))

    X = sb("X", [128, 8, T])
    Hh, Hl = sb("Hh", [128, 8, T], F32R), sb("Hl", [128, 8, T], F32R)
    Ph, Pl = sb("Ph", [128, 16, T], F32R), sb("Pl", [128, 16, T], F32R)
    M = sb("M", [128, 8, T])
    RAW = sb("RAW", [128, 2, 2048])
    Wh, Wl = sb("Wh", [128, 3, 2048], F32R), sb("Wl", [128, 3, 2048], F32R)
    NT = 4
    TMP = sb("TMP", [128, NT, 528])
    Z = sb("Z", [128, 2048])
    WS = sb("WS", [128, 2, T], F32R)
    ident, ones = sb("ident", [128, 128]), sb("ones", [128, 128])
    identb, maskb = sb("identb", [128, 128], BF16), sb("maskb", [128, 128], BF16)
    P0, P1, P2 = sb("P0", [128, 99]), sb("P1", [128, 88]), sb("P2", [128, 88])
    rb2 = sb("rb2", [128, 48])
    drb3 = sb("drb3", [128, 48], BF16)
    pki = sb("pki", [128, 384], I32)
    pkf = sb("pkf", [128, 384])
    krt = sb("krt", [128, 128])
    rope = M[:, 6, :].rearrange("p (a b) -> p a b", a=8)
    sm = sb("sm", [128, 320])
    ropt = sb("ropt", [128, 8, 64])
    smi = sb("smi", [128, 4], I32)

    BANK = [ctx.enter_context(nc.psum_tensor(f"bank{i}", [128, 512], F32)) for i in range(8)]
    banks = Ring([b[:, :] for b in BANK])

    eps = sm[:, 0:1]
    posf = sm[:, 1:5]
    gq_a, gk_a, gq_b, gk_b = sm[:, 5:6], sm[:, 6:7], sm[:, 7:8], sm[:, 8:9]
    rinv = sm[:, 16:32]
    sinkc = sm[:, 32:48]
    invf = sm[:, 48:64]
    grow_q, grow_k = sm[:, 64:96], sm[:, 96:128]
    st4, rs4 = sm[:, 128:132], sm[:, 132:136]
    kr2 = sm[:, 136:140]
    lo = sm[:, 9:10]
    mneg, sums, small = sm[:, 160:192], sm[:, 192:224], sm[:, 224:320]

    cs = {n: [sem("d_" + n), 0] for n in ("x", "par", "par1", "par2", "sm", "pos", "pos2", "rb", "ws", "p", "fill",
                                         "bw", "out", "bs0", "bs1", "pscr")}
    raws = [[sem(f"d_raw{i}"), 0] for i in range(2)]

    BS = nc.dram_tensor("bias_scratch", (16, 4, 128, 256), F32, kind="Internal").ap()
    PS = nc.dram_tensor("pos_scratch", (T + 128,), I32, kind="Internal").ap()

    def f(ap):
        return ap.bitcast(F32)

    def consts():
        z = PO.add(lambda e: e.memset(ident[:, :], 0.0))
        o = PO.add(lambda e: e.memset(ones[:, :], 1.0))
        PO.add(lambda e: e.memset(eps, EPS))
        PO.add(lambda e: e.memset(gq_b, 1.0))
        PO.add(lambda e: e.memset(gk_b, 1.0))
        tid = PO.add(lambda e: e.affine_select(out=ident[:, :], in_=ident[:, :], compare_op=ALU.not_equal, fill=1.0,
                                               base=0, pattern=[[-1, 128]], channel_multiplier=1), z)
        b0 = PO.add(lambda e: e.memset(identb[:, :], 0.0))
        PO.add(lambda e: e.affine_select(out=identb[:, :], in_=identb[:, :], compare_op=ALU.not_equal, fill=1.0,
                                         base=0, pattern=[[-1, 128]], channel_multiplier=1), b0)
        b1 = PO.add(lambda e: e.memset(maskb[:, :], 0.0))
        tmb = PO.add(lambda e: e.affine_select(out=maskb[:, :], in_=maskb[:, :], compare_op=ALU.is_ge, fill=NEG,
                                               base=0, pattern=[[-1, 128]], channel_multiplier=1), b1)
        for t in range(16):
            PO.add(lambda e, t=t: e.memset(rinv[:, t:t + 1], float(np.float32(1.0) / np.float32(t + 1))))
            PO.add(lambda e, t=t: e.memset(invf[:, t:t + 1],
                                           float(np.float32(10000.0) ** np.float32(-2.0 * t / 32))))
        tc = PO.add(lambda e: e.memset(TMP[:, :, 0:16], 0.0))
        return tc

    t_const = consts()

    PARS = [("mix_norm", 8), ("pool_scale", 8), ("sgu_norm", 8), ("ffn_norm", 8), ("ple_norm", 8), ("final_norm", 8),
            ("ffn_norm1_2", 16), ("mix_norm_2", 16), ("ffn_norm2_2", 16), ("b_q_norm_2", 2), ("b_kv_norm_2", 1)]
    col = {}
    stage = M[:, 7, :]

    def flat(ap):
        n = len(ap.shape)
        if n == 1:
            return ap
        names = "abcd"[:n]
        return ap.rearrange(" ".join(names) + " -> (" + " ".join(names) + ")")

    def parameters():
        r = 0
        tok = None
        for name, n in PARS:
            col[name] = r
            tok = SP.dma(cs["par"], stage[r:r + n, 0:128], flat(a[name]).rearrange("(c p) -> c p", p=128))
            r += n
        cb = flat(a["conv_b"]).rearrange("(c p) -> c p", p=128)
        cw = a["conv_w"][0].rearrange("k (c p) -> (k c) p", p=128)
        SP.dma(cs["par"], stage[0:44, 128:256], cb)
        SP.dma(cs["par"], stage[44:88, 128:256], cw[0:44, :])
        tok = SP.dma(cs["par"], stage[0:88, 256:384], cw[44:132, :])
        bi, bank, was = banks.take()
        PE.wait(was, t_const, tok)
        for i, (n, d) in enumerate(((99, P0), (88, P1), (88, P2))):
            tk = PE.add(lambda e, i=i, n=n: e.transpose(bank[:, 128 * i:128 * i + n], stage[0:n, 128 * i:128 * i + 128],
                                                        ident[0:n, 0:n]))
        for i, (n, d) in enumerate(((99, P0), (88, P1), (88, P2))):
            t = DV.add(lambda e, i=i, n=n, d=d: e.tensor_copy(d[:, :], bank[:, 128 * i:128 * i + n]), tk)
        banks.done(bi, t)
        return t

    def gain(name, c, base=0):
        return P0[:, col[name] + base + c:col[name] + base + c + 1]

    def convp(k, c):
        r = 44 * (k + 1) + c
        return P1[:, r:r + 1] if r < 88 else P2[:, r - 88:r - 87]

    tiles = []

    def square(src, k, c0, w=256):
        return [(0, k, w, src[:, c0:c0 + w])]

    def plan():
        win = a["w_in"][0]
        for i in range(4):
            tiles.append(("pool", i, square(win, 8, 256 * i)))
        tiles.append(("wpool", 0, [(0, 8, 256, a["w_pool"][0].rearrange("g c d -> (g c) d"))]))
        for i in range(4):
            tiles.append(("wa", i, square(a["w_branch_a"][0], 8, 256 * i)))
            tiles.append(("ga", i, square(win, 8, 3072 + 256 * i)))
        for i in range(4):
            tiles.append(("v", i, square(win, 8, 2048 + 256 * i)))
        for i in range(4):
            tiles.append(("u", i, square(win, 8, 1024 + 256 * i)))
        for i in range(4):
            tiles.append(("wb", i, square(a["w_branch_b"][0], 8, 256 * i)))
            tiles.append(("gb", i, square(win, 8, 4096 + 256 * i)))
        for i in range(4):
            tiles.append(("wo", i, square(a["w_out"][0], 8, 256 * i)))
        plan_ffn("f", a["w_up"][0], a["w_up"][0], DFF, a["w_down"][0])
        tiles.append(("ple", 0, [(0, 2, 1024, a["w_ple"][0])]))
        for i in range(4):
            tiles.append(("pg", i, square(a["w_ple_gate"][0], 8, 256 * i)))
        plan_ffn("s0", a["ffn1_wg_2"][0], a["ffn1_wu_2"][0], 0, a["ffn1_wd_2"][0])
        wi = a["a_w_in_2"][0]
        tiles.append(("akv", 0, square(wi, 8, 1024)))
        for i in range(4):
            tiles.append(("aq", i, square(wi, 8, 256 * i)))
        for i in range(4):
            tiles.append(("ao", i, square(a["a_w_out_2"][0], 8, 256 * i)))
        plan_ffn("s1", a["ffn2_wg_2"][0], a["ffn2_wu_2"][0], 0, a["ffn2_wd_2"][0])
        plan_ffn("s2", a["ffn1_wg_2"][1], a["ffn1_wu_2"][1], 0, a["ffn1_wd_2"][1])
        wi = a["b_w_in_2"][0]
        tiles.append(("bq", 0, square(wi, 8, 0)))
        tiles.append(("bkv", 0, square(wi, 8, 256, 160)))
        for g in range(4):
            tiles.append(("bg", g, [(0, 2, 384, a["b_w_uq_2"][0][:, 384 * g:384 * g + 384]),
                                    (768, 1, 512, a["b_w_ukv_2"][0][:, 512 * g:512 * g + 512])]))
        for i in range(4):
            tiles.append(("bo", i, square(a["b_w_out_2"][0], 8, 256 * i)))
        plan_ffn("s3", a["ffn2_wg_2"][1], a["ffn2_wu_2"][1], 0, a["ffn2_wd_2"][1])

    THIRDS = ((0, 8), (8, 8), (16, 6))

    def plan_ffn(tag, wa, wb, off, wd):
        for h, (c0, n) in enumerate(THIRDS):
            for j in range(n // 2):
                tiles.append((tag + "a", (h, j), square(wa, 8, 128 * c0 + 256 * j)))
                tiles.append((tag + "b", (h, j), square(wb, 8, off + 128 * c0 + 256 * j)))
            for i in range(4):
                tiles.append((tag + "d", (h, i), [(0, n, 256, wd[128 * c0:128 * (c0 + n), 256 * i:256 * i + 256])]))

    plan()
    NW = len(tiles)
    landed, halves, split, used = {}, {}, {}, {}
    state = {"dma": 0, "split": 0, "use": 0}

    def size(n):
        return max(o + k * w for o, k, w, _ in tiles[n][2])

    def load_tile():
        n = state["dma"]
        if n >= NW:
            return
        state["dma"] += 1
        for o, k, w, src in tiles[n][2]:
            dst = RAW[:, n % 2, o:o + k * w].rearrange("p (k w) -> p k w", k=k)
            landed[n] = SP.dma(raws[n % 2], dst, src.rearrange("(k p) w -> p k w", p=128), split.get(n - 2))

    def split_tile():
        n = state["split"]
        if n >= NW:
            return
        state["split"] += 1
        s, z = n % 3, size(n)
        parts = [(0, z // 2), (z // 2, z)]
        ta = [AC.add(lambda e, x=x, y=y: e.activation(Wh[:, s, x:y], RAW[:, n % 2, x:y], ACT.Copy),
                     landed[n], used.get(n - 3)) for x, y in parts]
        td = [DV.add(lambda e, x=x, y=y: e.tensor_tensor(Wl[:, s, x:y], RAW[:, n % 2, x:y], f(Wh[:, s, x:y]),
                                                         ALU.subtract), t, used.get(n - 3))
              for (x, y), t in zip(parts, ta)]
        split[n] = td

    def next_tile(name, i):
        n = state["use"]
        assert tiles[n][0:2] == (name, i), (tiles[n][0:2], name, i)
        state["use"] += 1
        while state["split"] <= min(n + 2, NW - 1):
            split_tile()
            load_tile()
        s = n % 3
        views = []
        for o, k, w, _ in tiles[n][2]:
            views.append(tuple(W[:, s, o:o + k * w].rearrange("p (k w) -> p k w", k=k) for W in (Wh, Wl)))
        PE.wait(split[n])
        return n, views

    def tile_used(n, tok):
        used[n] = tok

    def mm3(o, lh, ll, rh, rl, start, stop):
        PE.add(lambda e: e.matmul(o, ll, rh, start=start, stop=False), signal=False)
        PE.add(lambda e: e.matmul(o, lh, rl, start=False, stop=False), signal=False)
        return PE.add(lambda e: e.matmul(o, lh, rh, start=False, stop=stop), signal=stop)

    hready = [[] for _ in range(8)]
    pready = [[] for _ in range(16)]

    def form_a(views, K, src, ready, base=0, m=2, kw=0):
        res = []
        wh, wl = views
        for c in range(m):
            bi, bank, was = banks.take()
            PE.wait(was)
            for k in range(K):
                PE.wait(ready[base + k])
                cc = slice((kw + c) * 128, (kw + c + 1) * 128)
                t = mm3(bank, wh[:, k, cc], wl[:, k, cc], src[0][:, base + k, :], src[1][:, base + k, :],
                        k == 0, k == K - 1)
            res.append((bi, bank, t))
        return res

    H, P = (Hh, Hl), (Ph, Pl)

    def pair(dst, c, src_tok, view, *was):
        h = AC.add(lambda e: e.activation(dst[0][:, c, :], view, ACT.Copy), src_tok, *was)
        l = DV.add(lambda e: e.tensor_tensor(dst[1][:, c, :], view, f(dst[0][:, c, :]), ALU.subtract), h, *was)
        return [h, l]

    xt = [[] for _ in range(8)]
    SQ = TMP[:, NT - 1, 16:528]
    tmps = Ring([TMP[:, i, :] for i in range(NT - 1)])
    nstate = {"sq": None, "read": []}

    def stats(c):
        if c == 0:
            nstate["sq"] = AC.add(lambda e: e.activation(SQ, X[:, c, :], ACT.Square), xt[c], nstate["read"])
            return
        ti, tv, was = tmps.take()
        v = tv[:, 16:528]
        s = AC.add(lambda e: e.activation(v, X[:, c, :], ACT.Square), xt[c], was)
        nstate["sq"] = PO.add(lambda e: e.tensor_tensor(SQ, SQ, v, ALU.add), s, nstate["sq"])
        tmps.done(ti, nstate["sq"])

    def rstd():
        bi, bank, was = banks.take()
        PE.wait(was, nstate["sq"])
        for n in range(4):
            t = PE.add(lambda e, n=n: e.matmul(bank[:, n:n + 1], SQ[:, 128 * n:128 * n + 128], ones[:, 0:1],
                                               start=True, stop=True))
        t2 = AC.add(lambda e: e.activation(st4, bank[:, 0:4], ACT.Sqrt, bias=eps, scale=1.0 / D), t)
        nstate["read"] = [t]
        t3 = DV.add(lambda e: e.reciprocal(rs4, st4), t2)
        ti, tv, w2 = tmps.take()
        v = tv[:, 16:528]
        DV.wait(t3)
        for n in range(4):
            t4 = DV.add(lambda e, n=n: e.tensor_scalar(v[:, 128 * n:128 * n + 128], ident[:, :], rs4[:, n:n + 1], None,
                                                       ALU.mult), w2)
        t5 = PE.add(lambda e: e.matmul(bank, ones[:, :], v, start=True, stop=True), t4)
        tmps.done(ti, t5)
        return bi, bank, t5

    def norm(name, base=0):
        bi, bank, tr = rstd()
        pe = (PE.sem, PE.n)
        for c in range(8):
            ti, tv, was = tmps.take()
            v = tv[:, 16:528]
            t = DV.add(lambda e, c=c: e.scalar_tensor_tensor(v, X[:, c, :], gain(name, c, base), bank, ALU.mult,
                                                             ALU.mult), tr, xt[c], was)
            hready[c] = pair(H, c, t, v, pe)
            tmps.done(ti, *hready[c])
        banks.done(bi, t)

    def add_x(c, bank, tok, factor):
        t = DV.add(lambda e: e.scalar_tensor_tensor(X[:, c, :], bank, factor, X[:, c, :], ALU.mult, ALU.add),
                   tok, xt[c])
        xt[c] = [t]
        return t

    def ffn(tag, kind):
        pe0 = None
        for h, (c0, n) in enumerate(THIRDS):
            base = 8 * (h % 2)
            for j in range(n // 2):
                extra(2)
                na, va = next_tile(tag + "a", (h, j))
                ra = form_a(va[0], 8, H, hready)
                tile_used(na, ra[1][2])
                acts = []
                for c in range(2):
                    cc = c0 + 2 * j + c
                    bi, bank, t = ra[c]
                    if kind == "conv":
                        v, toks, ti = conv(cc, bank, t, bi)
                        t2 = AC.add(lambda e, v=v: e.activation(v, v, ACT.Gelu), toks)
                        acts.append((v, t2, ti))
                    else:
                        ti, tv, was = tmps.take()
                        v = tv[:, 16:528]
                        t2 = AC.add(lambda e, v=v, bank=bank: e.activation(v, bank, ACT.Silu), t, was)
                        banks.done(bi, t2)
                        acts.append((v, t2, ti))
                nb, vb = next_tile(tag + "b", (h, j))
                rb = form_a(vb[0], 8, H, hready)
                tile_used(nb, rb[1][2])
                for c in range(2):
                    cc = c0 + 2 * j + c
                    bi, bank, t = rb[c]
                    v, t2, ti = acts[c]
                    if kind == "conv":
                        w, toks, tj = conv(22 + cc, bank, t, bi)
                        t3 = DV.add(lambda e, v=v, w=w: e.tensor_tensor(v, v, w, ALU.mult), toks, t2)
                        tmps.done(tj, t3)
                    else:
                        t3 = DV.add(lambda e, v=v, bank=bank: e.tensor_tensor(v, v, bank, ALU.mult), t, t2)
                        banks.done(bi, t3)
                    q = base + 2 * j + c
                    pready[q] = pair(P, q, t3, v, pfree[q])
                    tmps.done(ti, *pready[q])
            for i in range(4):
                extra(1)
                nd, vd = next_tile(tag + "d", (h, i))
                rd = form_a(vd[0], n, P, pready, base=base)
                tile_used(nd, rd[1][2])
                for c in range(2):
                    bi, bank, t = rd[c]
                    banks.done(bi, add_x(2 * i + c, bank, t, 1.0 if kind == "conv" else 0.5))
                    if h == 2:
                        stats(2 * i + c)
            for q in range(16):
                pfree[q] = [(PE.sem, PE.n)] if base <= q < base + 8 else pfree[q]

    pfree = [[] for _ in range(16)]

    def conv(cc, bank, t, bi):
        ti, tv, was = tmps.take()
        v = tv[:, 16:528]
        t1 = AC.add(lambda e: e.activation(v, bank, ACT.Identity, bias=convp(-1, cc), scale=convp(2, cc)), t, was)
        t2 = DV.add(lambda e: e.scalar_tensor_tensor(v[:, 1:T], bank[:, 0:T - 1], convp(1, cc), v[:, 1:T], ALU.mult,
                                                     ALU.add), t1)
        t3 = DV.add(lambda e: e.scalar_tensor_tensor(v[:, 2:T], bank[:, 0:T - 2], convp(0, cc), v[:, 2:T], ALU.mult,
                                                     ALU.add), t2)
        banks.done(bi, t3)
        return v, [t3], ti

    extras = []

    def extra(n):
        for _ in range(n):
            if extras:
                extras.pop(0)()

    bstate = {}
    BND = [LOWEST] + [float(b) for b in bucket_bounds()]

    def bias_consts():
        rows = Z[:, 0:128].rearrange("p (n k) -> p n k", n=4)
        was = bstate["t"]
        for k in range(32):
            t = PO.add(lambda e, k=k: e.memset(rows[:, :, k:k + 1], BND[k]), was)
        t1 = DV.add(lambda e: e.tensor_tensor(Z[:, 0:128], Z[:, 0:128], ident[:, :], ALU.mult), t, was)
        t1 = DV.add(lambda e: e.tensor_reduce(lo, Z[:, 0:128], AX.X, ALU.add), t1)
        tz = PO.add(lambda e: e.memset(rb2[:, 16:32], 0.0))
        rb = a["rel_bias_2"]
        for n in range(4):
            SP.dma(cs["rb"], rb2[32 * n:32 * n + 32, 0:16], rb)
            t = SP.dma(cs["rb"], rb2[32 * n + 1:32 * n + 32, 16:32], rb[0:31, :], tz)
        d = rb2[:, 32:48]
        t = DV.add(lambda e: e.tensor_tensor(d, rb2[:, 0:16], rb2[:, 16:32], ALU.subtract), t)
        for j in range(3):
            part = drb3[:, :].rearrange("p (h j) -> p h j", j=3)[:, :, j]
            t = DV.add(lambda e, part=part: e.tensor_copy(part, d), t)
            if j < 2:
                t = DV.add(lambda e, part=part: e.tensor_tensor(d, d, part, ALU.subtract), t)
        bstate["drb"] = t
        for n in range(4):
            SP.dma(cs["pos2"], pki[32 * n:32 * n + 32, 0:255],
                   PS[1 + 128 * n:256 + 128 * n].rearrange("(o n) -> o n", o=1).broadcast_to([32, 255]),
                   bstate["pos"])
            t = SP.dma(cs["pos2"], pki[32 * n:32 * n + 32, 256:384],
                       PS[128 + 128 * n:256 + 128 * n].rearrange("(o n) -> o n", o=1).broadcast_to([32, 128]))
        DV.add(lambda e: e.tensor_copy(pkf[:, 0:255], pki[:, 0:255]), t)
        bstate["pk"] = DV.add(lambda e: e.tensor_copy(pkf[:, 256:384], pki[:, 256:384]), t)
        bstate["t"] = bstate["t"] + [bstate["pk"]]

    def plan_bias():
        acc = Z[:, :].rearrange("p (h n u) -> p h n u", h=16, n=4)
        GU = 32
        Gv = M[:, 0:4, :].rearrange("p a b -> p (a b)").bitcast(BF16).rearrange("p (q u) -> p q u", q=128)
        pk_t = pkf[:, :]
        for ch in range(4):
            def compare(ch=ch):
                keys = bass.AP(pk_t.tensor, pk_t.offset + GU * ch, [list(pk_t.ap[0]), [1, 128], [1, GU]])
                qs = pkf[:, 256:384].unsqueeze(2).broadcast_to([128, 128, GU])
                bstate["G"] = DV.add(lambda e: e.scalar_tensor_tensor(Gv, keys, lo, qs, ALU.add, ALU.is_le),
                                     bstate["pk"], bstate.get("gread"), bstate["t"], bstate["mfree"])
            extras.append(compare)
            for n in range(4):
                for v in range(4):
                    def step(ch=ch, n=n, v=v):
                        bi, bank, was = banks.take()
                        PE.wait(was, bstate["G"], bstate["drb"])
                        rows = slice(32 * n, 32 * n + 32)
                        for w in range(8):
                            t = PE.add(lambda e, w=w: e.matmul(bank[:, 48 * w:48 * w + 48], Gv[rows, :, 8 * v + w],
                                                               drb3[rows, :], start=True, stop=True))
                        bstate["gread"] = t
                        src = bank[:, 0:384].rearrange("p (u h j) -> p h u j", u=8, j=3)
                        t = DV.add(lambda e: e.tensor_reduce(acc[:, :, n, 8 * v:8 * v + 8], src, AX.X, ALU.add),
                                   t, bstate.get("bw"), bstate["t"])
                        banks.done(bi, t)
                        bstate["acc"] = t
                    extras.append(step)

            def write(ch=ch):
                for h in range(16):
                    dst = bass.AP(BS.tensor, h * 4 * 128 * 256 + 1 + GU * ch, [[257, 128], [128 * 256, 4], [1, GU]])
                    bstate["bw"] = SP.dma(cs["bw"], dst, acc[:, h, :, :], bstate["acc"], bstate["fill"])
            extras.append(write)

    for i in range(2):
        load_tile()
    tx = SP.dma(cs["x"], M[:, 0:7, :].rearrange("p a b -> p (a b)")[:, 0:3072].rearrange("p (n d) -> p n d", n=3),
                a["x"][0, 0:384, :].rearrange("(n p) d -> p n d", p=128))
    tx = SP.dma(cs["x"], Z[:, 0:1024], a["x"][0, 384:512, :])
    t_par = parameters()
    xm = M[:, 0:6, :].rearrange("p a b -> p (a b)").rearrange("p (n d) -> p n d", n=3)
    for c in range(8):
        bi, bank, was = banks.take()
        PE.wait(was, tx, t_const)
        for n in range(4):
            src = xm[:, n, 128 * c:128 * c + 128] if n < 3 else Z[:, 128 * c:128 * c + 128]
            t = PE.add(lambda e, n=n, src=src, bank=bank: e.transpose(bank[:, 128 * n:128 * n + 128], src, ident[:, :]))
        xt[c] = [DV.add(lambda e, c=c, bank=bank: e.tensor_copy(X[:, c, :], bank), t)]
        banks.done(bi, *xt[c])
        stats(c)
    t_x_in = t
    wsp = Z[:, 0:1024].rearrange("p (h s) -> p h s", h=8)
    bsp = Z[:, 1024:2048].rearrange("p (h t) -> p h t", h=8)
    t_ws = SP.dma(cs["ws"], wsp, a["w_spatial"][0].rearrange("h t s -> t h s"), t_x_in)
    t_ws = SP.dma(cs["ws"], Z[:, 1024:2048],
                  flat(a["b_spatial"]).rearrange("(o n) -> o n", o=1).broadcast_to([128, 1024]))
    pos = flat(a["positions_2"])
    SP.wait(t_const)
    SP.dma(cs["sm"], smi[:, :], pos.rearrange("(n p) -> p n", p=128))
    SP.dma(cs["sm"], sinkc, a["a_sinks_2"].broadcast_to([128, 16]))
    for k, (name, w, d) in enumerate((("a_q_gain_2", 64, gq_a), ("a_k_gain_2", 64, gk_a))):
        gcol = flat(a[name]).rearrange("(n o) -> n o", o=1)
        SP.dma(cs["sm"], d[0:64, :], gcol)
        SP.dma(cs["sm"], d[64:128, :], gcol)
    for name, d, row in (("b_q_gain_2", gq_b, grow_q), ("b_k_gain_2", gk_b, grow_k)):
        SP.dma(cs["sm"], d[0:64, :], flat(a[name]).rearrange("(n o) -> n o", o=1)[0:64, :])
        t_sm = SP.dma(cs["sm"], row, a[name][:, 64:96].broadcast_to([128, 32]))
    SP.dma(cs["pscr"], PS[0:128], pos[0:128])
    bstate["pos"] = SP.dma(cs["pscr"], PS[128:640], pos)
    t_g1 = t_sm
    bstate["posf"] = t_posf = DV.add(lambda e: e.tensor_copy(posf, smi[:, :]), t_sm)

    def trig():
        TWO_PI = 2 * math.pi
        c1 = float(np.float32(6.28125))
        c2 = float(np.float32(TWO_PI - c1))
        c3 = float(np.float32(TWO_PI - c1 - c2))
        MAGIC = 12582912.0
        ang, kk, r, t_ = rope[:, 0, :], rope[:, 1, :], rope[:, 2, :], rope[:, 3, :]
        sn, cn = rope[:, 4, :], rope[:, 5, :]
        tk = None
        DV.wait(t_const, t_posf, t_sm)
        for n in range(4):
            tk = DV.add(lambda e, n=n: e.tensor_scalar(ang[:, 16 * n:16 * n + 16], invf, posf[:, n:n + 1], None,
                                                       ALU.mult))
        tk = DV.add(lambda e: e.tensor_scalar(kk, ang, 1.0 / TWO_PI, None, ALU.mult), tk)
        tk = DV.add(lambda e: e.tensor_scalar(kk, kk, MAGIC, None, ALU.add), tk)
        tk = DV.add(lambda e: e.tensor_scalar(kk, kk, -MAGIC, None, ALU.add), tk)
        tk = DV.add(lambda e: e.scalar_tensor_tensor(r, kk, -c1, ang, ALU.mult, ALU.add), tk)
        tk = DV.add(lambda e: e.scalar_tensor_tensor(r, kk, -c2, r, ALU.mult, ALU.add), tk)
        tk = DV.add(lambda e: e.scalar_tensor_tensor(r, kk, -c3, r, ALU.mult, ALU.add), tk)
        PI = float(np.nextafter(np.float32(math.pi), np.float32(0)))
        tk = DV.add(lambda e: e.tensor_scalar(r, r, PI, -PI, ALU.min, ALU.max), tk)
        ts = AC.add(lambda e: e.activation(sn, r, ACT.Sin), tk)
        tk = DV.add(lambda e: e.tensor_scalar(t_, r, -1.0, None, ALU.mult), tk)
        tk = DV.add(lambda e: e.tensor_tensor(t_, t_, r, ALU.max), tk)
        tk = DV.add(lambda e: e.tensor_scalar(t_, t_, -1.0, math.pi / 2, ALU.mult, ALU.add), tk)
        tc = AC.add(lambda e: e.activation(cn, t_, ACT.Sin), tk)
        DV.wait(ts, tc)

    def tables():
        sn, cn = rope[:, 4, :], rope[:, 5, :]
        tk = None
        for row, base in ((grow_q, 0), (grow_k, 4)):
            dst = ropt[:, base:base + 4, :]
            for j, (g, tr) in enumerate(((0, cn), (16, sn), (16, cn), (0, sn))):
                for n in range(4):
                    tk = DV.add(lambda e, j=j, g=g, tr=tr, n=n, dst=dst, row=row: e.tensor_tensor(
                        dst[:, j, 16 * n:16 * n + 16], tr[:, 16 * n:16 * n + 16], row[:, g:g + 16], ALU.mult))
        return tk



    split_tile()
    load_tile()
    split_tile()
    load_tile()
    DV.wait(t_par)
    norm("mix_norm")
    trig()
    t_rope = tables()

    for g in range(4):
        w = 2 << g
        n, v = next_tile("pool", g)
        r = form_a(v[0], 8, H, hready)
        tile_used(n, r[1][2])
        for c in range(2):
            bi, bank, t = r[c]
            i0, z0, w0 = tmps.take()
            i1, z1, w1 = tmps.take()
            i2, z2, w2 = tmps.take()
            tz = AC.add(lambda e, z0=z0, bank=bank: e.activation(z0[:, 16:528], bank, ACT.Copy), t, w0)
            src, dsts = z0, [z1, z2]
            tk, k, q = tz, 1, 0
            while k < w:
                d = dsts[q % 2]
                tk = DV.add(lambda e, d=d, src=src, k=k: e.tensor_tensor(d[:, 16:528], src[:, 16:528],
                                                                         src[:, 16 - k:528 - k], ALU.add),
                            tk, w1, w2)
                src, k, q = d, 2 * k, q + 1
            tk = DV.add(lambda e, s=src, w=w: e.scalar_tensor_tensor(s[:, 16:16 + w], s[:, 16:16 + w], float(w),
                                                                     rinv[:, 0:w], ALU.mult, ALU.mult), tk)
            tk = DV.add(lambda e, s=src, w=w, z0=z0: e.scalar_tensor_tensor(s[:, 16:528], s[:, 16:528], 1.0 / w,
                                                                            z0[:, 16:528], ALU.mult, ALU.subtract), tk)
            banks.done(bi, tz)
            q = 2 * g + c
            pready[q] = pair(P, q, tk, src[:, 16:528])
            for i in (i0, i1, i2):
                tmps.done(i, *pready[q])
    n, v = next_tile("wpool", 0)
    wh, wl = v[0]
    for g in range(4):
        r = form_a((wh[:, 2 * g:2 * g + 2, :], wl[:, 2 * g:2 * g + 2, :]), 2, P, pready, base=2 * g)
        for c in range(2):
            bi, bank, t = r[c]
            q = 8 + 2 * g + c
            s = gain("pool_scale", 2 * g + c)
            h = AC.add(lambda e, q=q, bank=bank, s=s: e.activation(Ph[:, q, :], bank, ACT.Copy, scale=s), t)
            l = DV.add(lambda e, q=q, bank=bank, s=s: e.scalar_tensor_tensor(
                Pl[:, q, :], bank, s, f(Ph[:, q, :]), ALU.mult, ALU.subtract), h)
            pready[q] = [h, l]
            banks.done(bi, h, l)
    tile_used(n, r[1][2])
    t_pool = r[1][2]

    def gated(ta, tg, src, ready, base, finish):
        for i in range(4):
            na, va = next_tile(ta, i)
            ra = form_a(va[0], 8, src, ready, base=base)
            tile_used(na, ra[1][2])
            ng, vg = next_tile(tg, i)
            rg = form_a(vg[0], 8, H, hready)
            tile_used(ng, rg[1][2])
            for c in range(2):
                bg, bankg, tgk = rg[c]
                ba, banka, tak = ra[c]
                ti, tv, was = tmps.take()
                v = tv[:, 16:528]
                s = AC.add(lambda e, v=v, b=bankg: e.activation(v, b, ACT.Sigmoid), tgk, was)
                banks.done(bg, s)
                t = finish(2 * i + c, v, banka, [s, tak])
                banks.done(ba, t)
                tmps.done(ti, t)

    mt = [None] * 8

    def fin_a(c, v, bank, toks):
        mt[c] = DV.add(lambda e: e.tensor_tensor(M[:, c, :], v, bank, ALU.mult), *toks)
        return mt[c]

    gated("wa", "ga", P, pready, 8, fin_a)
    t_free8 = (PE.sem, PE.n)

    vh, vl = (W[:, 0:8, :].rearrange("p a b -> p (a b)").rearrange("p (n d) -> p n d", n=4) for W in (Ph, Pl))
    ssv = small[:, 0:16].rearrange("p (n i) -> p n i", n=4)
    vtok = []
    for i in range(4):
        n, v = next_tile("v", i)
        wh, wl = v[0]
        for half in range(2):
            bi, bank, was = banks.take()
            PE.wait(was)
            for q in range(2):
                b = 2 * half + q
                for k in range(8):
                    t = mm3(bank[:, 256 * q:256 * q + 256], Hh[:, k, 128 * b:128 * b + 128],
                            Hl[:, k, 128 * b:128 * b + 128], wh[:, k, :], wl[:, k, :], k == 0, k == 7)
            ti, tv, w0 = tmps.take()
            tj, tw, w1 = tmps.take()
            vv, ww = tv[:, 16:528], tw[:, 16:528]
            tg = AC.add(lambda e, vv=vv, bank=bank: e.activation(vv, bank, ACT.Gelu), t, w0)
            banks.done(bi, tg)
            hh = vh[:, 2 * half:2 * half + 2, 256 * i:256 * i + 256]
            ll = vl[:, 2 * half:2 * half + 2, 256 * i:256 * i + 256]
            v3 = vv.rearrange("p (q d) -> p q d", q=2)
            h = AC.add(lambda e, hh=hh, v3=v3: e.activation(hh, v3, ACT.Copy), tg, t_pool)
            l = DV.add(lambda e, ll=ll, v3=v3, hh=hh: e.tensor_tensor(ll, v3, f(hh), ALU.subtract), h)
            for q in range(2):
                s = AC.add(lambda e, q=q, i=i, half=half, vv=vv, ww=ww: e.activation(
                    ww[:, 256 * q:256 * q + 256], vv[:, 256 * q:256 * q + 256], ACT.Square,
                    accum_out=ssv[:, 2 * half + q, i:i + 1]), tg, w1)
            vtok += [h, l]
            tmps.done(ti, l, s)
            tmps.done(tj, s)
        tile_used(n, t)
    ssum, srt, rv = small[:, 16:20], small[:, 20:24], small[:, 24:28]
    t = DV.add(lambda e: e.tensor_reduce(ssum, ssv, AX.X, ALU.add), s)
    t = AC.add(lambda e: e.activation(srt, ssum, ACT.Sqrt, bias=eps, scale=1.0 / 1024), t)
    t_rv = DV.add(lambda e: e.reciprocal(rv, srt), t)

    t_m = PO.add(lambda e: e.affine_select(out=wsp, in_=wsp, compare_op=ALU.is_ge, fill=0.0, base=0,
                                           pattern=[[0, 8], [-1, 128]], channel_multiplier=1), t_ws)
    for half in range(2):
        bi, bank, was = banks.take()
        PE.wait(was, t_m)
        for q in range(4):
            t = PE.add(lambda e, q=q, half=half, bank=bank: e.transpose(bank[:, 128 * q:128 * q + 128],
                                                                        wsp[:, 4 * half + q, :], ident[:, :]))
        t_wsT = DV.add(lambda e, half=half, bank=bank: e.tensor_copy(Z[:, 512 * half:512 * half + 512], bank), t)
        banks.done(bi, t_wsT)

    t_ws_used = None
    for i in range(4):
        n, v = next_tile("u", i)
        r = form_a(v[0], 8, H, hready)
        tile_used(n, r[1][2])
        for c in range(2):
            h = 2 * i + c
            bi, bank, t = r[c]
            i0, z0, w0 = tmps.take()
            i1, z1, w1 = tmps.take()
            uu, tt = z0[:, 16:528], z1[:, 16:528]
            tu = AC.add(lambda e, uu=uu, bank=bank: e.activation(uu, bank, ACT.Gelu), t, w0)
            banks.done(bi, tu)
            DV.wait(t_wsT, t_rv)
            for q in range(4):
                ts = DV.add(lambda e, q=q, h=h, tt=tt: e.tensor_scalar(
                    tt[:, 128 * q:128 * q + 128], wsp[:, h, :], rv[:, q:q + 1], None, ALU.mult), w1)
            th = AC.add(lambda e, tt=tt: e.activation(WS[:, 0, :], tt, ACT.Copy), ts, t_ws_used)
            tl = DV.add(lambda e, tt=tt: e.tensor_tensor(WS[:, 1, :], tt, f(WS[:, 0, :]), ALU.subtract), th,
                        t_ws_used)
            bj, bk, was = banks.take()
            PE.wait(was, th, tl, vtok)
            for q in range(4):
                sl = slice(128 * q, 128 * q + 128)
                hc = slice(128 * h, 128 * h + 128)
                t = mm3(bk[:, sl], vh[:, q, hc], vl[:, q, hc], WS[:, 0, sl], WS[:, 1, sl], True, True)
            t_ws_used = t
            i2, z2, w2 = tmps.take()
            mx = z2[:, 16:528]
            bb = bsp[:, h, :].unsqueeze(1).broadcast_to([128, 4, 128])
            t1 = DV.add(lambda e, h=h, mx=mx, bk=bk, bb=bb: e.scalar_tensor_tensor(
                mx.rearrange("p (n t) -> p n t", n=4), bk.rearrange("p (n t) -> p n t", n=4), gain("sgu_norm", h), bb,
                ALU.mult, ALU.add), t, w2)
            banks.done(bj, t1)
            t2 = DV.add(lambda e, uu=uu, mx=mx: e.tensor_tensor(mx, mx, uu, ALU.mult), t1, tu)
            pready[8 + h] = pair(P, 8 + h, t2, mx, t_free8)
            tmps.done(i0, t2)
            tmps.done(i1, tl)
            tmps.done(i2, *pready[8 + h])
    bstate["t"] = [(DV.sem, DV.n), (PE.sem, PE.n), (AC.sem, AC.n)]
    t_vused = (PE.sem, PE.n)

    def fin_b(c, v, bank, toks):
        t = DV.add(lambda e: e.tensor_tensor(v, v, bank, ALU.mult), *toks)
        t2 = DV.add(lambda e: e.tensor_tensor(M[:, c, :], M[:, c, :], v, ALU.add), t, mt[c])
        pready[c] = pair(P, c, t2, M[:, c, :], t_vused)
        return t2

    gated("wb", "gb", P, pready, 8, fin_b)
    for i in range(4):
        n, v = next_tile("wo", i)
        r = form_a(v[0], 8, P, pready)
        tile_used(n, r[1][2])
        for c in range(2):
            bi, bank, t = r[c]
            banks.done(bi, add_x(2 * i + c, bank, t, 1.0))
            stats(2 * i + c)
    for q in range(16):
        pfree[q] = [(PE.sem, PE.n)]

    t_f = DV.add(lambda e: e.memset(M[:, 0:4, :], NEG), (PE.sem, PE.n), (AC.sem, AC.n), (DV.sem, DV.n))
    for h in range(16):
        for q in range(1):
            bstate["fill"] = SP.dma(cs["fill"], BS[h].rearrange("n p s -> p n s"),
                                    M[:, 0:2, :].rearrange("p a b -> p (a b)").rearrange("p (n s) -> p n s", n=4), t_f)
    bias_consts()
    norm("ffn_norm")
    ffn("f", "conv")

    pm = M[:, 4:6, :].rearrange("p a b -> p (a b)").rearrange("p (n d) -> p n d", n=4)
    t_p = SP.dma(cs["p"], pm, a["p"][0, 0].rearrange("(n p) d -> p n d", p=128), bstate["t"])
    for c in range(2):
        bi, bank, was = banks.take()
        PE.wait(was, t_p)
        for n in range(4):
            t = PE.add(lambda e, n=n, c=c, bank=bank: e.transpose(bank[:, 128 * n:128 * n + 128],
                                                                  pm[:, n, 128 * c:128 * c + 128], ident[:, :]))
        pready[c] = pair(P, c, t, bank, pfree[c])
        banks.done(bi, *pready[c])
    t_pm = (PE.sem, PE.n)
    n, v = next_tile("ple", 0)
    for c in range(8):
        r = form_a(v[0], 2, P, pready, m=1, kw=c)
        bi, bank, t = r[0]
        mt[c] = AC.add(lambda e, c=c, bank=bank: e.activation(M[:, c, :], bank, ACT.Copy), t, t_pm, bstate["fill"])
        banks.done(bi, mt[c])
    tile_used(n, t)
    for q in range(16):
        pfree[q] = [(PE.sem, PE.n)]
    norm("ple_norm")
    for i in range(4):
        extra(1)
        n, v = next_tile("pg", i)
        r = form_a(v[0], 8, H, hready)
        tile_used(n, r[1][2])
        for c in range(2):
            cc = 2 * i + c
            bi, bank, t = r[c]
            ti, tv, was = tmps.take()
            v_ = tv[:, 16:528]
            s = AC.add(lambda e, v=v_, b=bank: e.activation(v, b, ACT.Sigmoid), t, was)
            banks.done(bi, s)
            t1 = DV.add(lambda e, v=v_, cc=cc: e.tensor_tensor(v, v, M[:, cc, :], ALU.mult), s, mt[cc])
            t2 = DV.add(lambda e, v=v_, cc=cc: e.tensor_tensor(X[:, cc, :], X[:, cc, :], v, ALU.add), t1, xt[cc])
            xt[cc] = [t2]
            tmps.done(ti, t2)
            stats(cc)
    bi, bank, tr = rstd()
    for c in range(8):
        xt[c] = [DV.add(lambda e, c=c, bank=bank: e.scalar_tensor_tensor(
            X[:, c, :], X[:, c, :], gain("final_norm", c), bank, ALU.mult, ALU.mult), tr, xt[c])]
        if c == 7:
            banks.done(bi, *xt[c])
        stats(c)

    def mul3(o, x, y):
        return lambda e: e.tensor_tensor(o, x, y, ALU.mult)

    def rsqrt_small(dst, src, n, *after):
        t = AC.add(lambda e: e.activation(dst, src, ACT.Sqrt, bias=eps, scale=1.0 / n), *after)
        return DV.add(lambda e: e.reciprocal(dst, dst), t)

    def scaled_pair(dst, rows, bank, t, scale, *was):
        h = AC.add(lambda e: e.activation(dst[0], bank, ACT.Copy, scale=scale), t, *was)
        l = DV.add(lambda e: e.scalar_tensor_tensor(dst[1], bank, scale, f(dst[0]), ALU.mult, ALU.subtract), h, *was)
        return [h, l]

    def turn(src, rows):
        bi, bank, was = banks.take()
        PE.wait(was)
        for n in range(4):
            t = PE.add(lambda e, n=n: e.transpose(bank[0:rows, 128 * n:128 * n + 128], src(n), ident[:, :]))
        return bi, bank, t

    def proj_b(W, c0, w, n_t, b0, stride, K, src=H):
        bi, bank, was = banks.take()
        PE.wait(was)
        for q in range(n_t):
            b = b0 + q
            for k in range(K):
                PE.wait(src[2][k])
                t = mm3(bank[:, stride * q:stride * q + w], src[0][:, k, 128 * b:128 * b + 128],
                        src[1][:, k, 128 * b:128 * b + 128], W[0][:, k, c0:c0 + w], W[1][:, k, c0:c0 + w],
                        k == 0, k == K - 1)
        return bi, bank, t

    def now():
        return [(q.sem, q.n) for q in (PE, AC, DV, PO) if q.n]

    def out_proj(name, src, ready, base):
        for i in range(4):
            n, v = next_tile(name, i)
            r = form_a(v[0], 8, src, ready, base=base)
            tile_used(n, r[1][2])
            for c in range(2):
                bi, bank, t = r[c]
                banks.done(bi, add_x(2 * i + c, bank, t, 1.0))
                stats(2 * i + c)

    def mflat(a0, a1):
        return M[:, a0:a1, :].rearrange("p a b -> p (a b)")

    def attend_a():
        free0 = now()
        qt = mflat(0, 2).rearrange("p (n d) -> p n d", n=4)
        SS = [mflat(2, 4).rearrange("p (n s) -> p n s", n=4), mflat(4, 6).rearrange("p (n s) -> p n s", n=4)]
        kd = mflat(6, 8).rearrange("p (n g u d) -> p n g u d", n=4, g=2, u=2)
        ot = mflat(6, 8).rearrange("p (n d) -> p n d", n=4)
        BR = [Z[:, 0:1024].rearrange("p (n s) -> p n s", n=4), Z[:, 1024:2048].rearrange("p (n s) -> p n s", n=4)]
        vA = [W[:, 2, :].rearrange("p (n d) -> p n d", n=4) for W in P]
        QT = [(Ph[:, 3, :], Pl[:, 3, :]), (WS[:, 0, :], WS[:, 1, :])]
        t_neg = [PO.add(lambda e, b=b: e.memset(b[:, 0, 0:128], NEG), bstate["bw"], free0) for b in BR]
        Hs = (Hh, Hl, hready)
        AC.wait(free0)
        DV.wait(free0)

        n_, v_ = next_tile("akv", 0)
        ssk, rk = small[:, 0:8], small[:, 8:16]
        got = []
        vt = []
        for half in range(2):
            bi, bank, t = proj_b(v_[0], 0, 256, 2, 2 * half, 256, 8, Hs)
            bv = bank.rearrange("p (n g d) -> p n g d", n=2, g=4)
            ti, tv, was = tmps.take()
            sq = tv[:, 16:272].rearrange("p (n g d) -> p n g d", n=2, g=2)
            t1 = AC.add(lambda e, sq=sq, bv=bv: e.activation(sq, bv[:, :, 0:2, :], ACT.Square), t, was)
            t2 = DV.add(lambda e, half=half, tv=tv: e.tensor_reduce(
                ssk[:, 4 * half:4 * half + 4], tv[:, 16:272].rearrange("p (m d) -> p m d", d=64), AX.X, ALU.add), t1)
            tmps.done(ti, t2)
            b3 = bank.rearrange("p (n d) -> p n d", n=2)[:, :, 128:256]
            h = AC.add(lambda e, half=half, b3=b3: e.activation(vA[0][:, 2 * half:2 * half + 2, :], b3, ACT.Copy), t)
            l = DV.add(lambda e, half=half, b3=b3: e.tensor_tensor(
                vA[1][:, 2 * half:2 * half + 2, :], b3, f(vA[0][:, 2 * half:2 * half + 2, :]), ALU.subtract), h)
            vt += [h, l]
            got.append((bi, bv, t))
        tile_used(n_, t)
        tr = rsqrt_small(rk, ssk, 64, t2)
        rk4 = rk.rearrange("p (n g) -> p n g", n=4)
        for half in range(2):
            bi, bv, t = got[half]
            for u in range(2):
                tk = DV.add(lambda e, half=half, u=u, bv=bv: e.tensor_tensor(
                    kd[:, 2 * half:2 * half + 2, :, u, :], bv[:, :, 0:2, :],
                    rk4[:, 2 * half:2 * half + 2, :].unsqueeze(3).broadcast_to([128, 2, 2, 64]), ALU.mult), tr)
            banks.done(bi, tk, *vt)
        KT = []
        for g in range(2):
            PE.wait(tk)
            bi, bank, t = turn(lambda n, g=g: kd[:, n, g, :, :].rearrange("p u d -> p (u d)"), 128)
            kt = (Ph[:, g, :], Pl[:, g, :])
            toks = scaled_pair(kt, 128, bank, t, gk_a)
            banks.done(bi, *toks)
            KT.append((kt, toks))
        t_kd = t

        qfree = [[], []]
        sfree = [[], []]
        bfree = [[], []]
        pt_free = [[], []]
        oready = []
        otfree = [t_kd]
        heads = []

        def q_group(g):
            n_, v_ = next_tile("aq", g)
            ssq, rq = small[:, 16:32], small[:, 32:48]
            got = []
            for half in range(2):
                bi, bank, t = proj_b(v_[0], 0, 256, 2, 2 * half, 256, 8, Hs)
                ti, tv, was = tmps.take()
                sq = tv[:, 16:528]
                t1 = AC.add(lambda e, sq=sq, bank=bank: e.activation(sq, bank, ACT.Square), t, was)
                t2 = DV.add(lambda e, half=half, sq=sq: e.tensor_reduce(
                    ssq[:, 8 * half:8 * half + 8], sq.rearrange("p (m d) -> p m d", d=64), AX.X, ALU.add), t1)
                tmps.done(ti, t2)
                got.append((bi, bank, t))
            tile_used(n_, t)
            tr = rsqrt_small(rq, ssq, 64, t2)
            for half in range(2):
                bi, bank, t = got[half]
                tk = DV.add(lambda e, half=half, bank=bank: e.tensor_tensor(
                    qt[:, 2 * half:2 * half + 2, :].rearrange("p n (m d) -> p (n m) d", d=64),
                    bank.rearrange("p (m d) -> p m d", d=64),
                    rq[:, 8 * half:8 * half + 8].unsqueeze(2).broadcast_to([128, 8, 64]), ALU.mult), tr,
                    bstate.get("qt_read"))
                banks.done(bi, tk)
            return tk

        def load_bias(h):
            b = BR[h % 2]
            SP.dma(cs[f"bs{h % 2}"], b[:, 1:4, :], BS[h, 1:4].rearrange("n q s -> q n s"), bfree[h % 2], t_neg,
                   bstate["bw"])
            return SP.dma(cs[f"bs{h % 2}"], b[:, 0, 128:256], BS[h, 0, :, 128:256], bfree[h % 2])

        bias_t = {0: load_bias(0), 1: load_bias(1)}

        def scores(h):
            r, hp = h % 2, (h // 2) % 2
            qv, qtok = heads[h // 2]
            kt, ktok = KT[h // 8]
            rows = slice(64 * r, 64 * r + 64)
            PE.wait(qtok, ktok)
            S = SS[h % 2]
            bt = bias_t[h]
            for m in range(2):
                bi, bank, was = banks.take()
                PE.wait(was)
                for n in (2 * m, 2 * m + 1):
                    o = 256 * (n % 2)
                    ql = [x[rows, 128 * n:128 * n + 128] for x in qv]
                    if n == 0:
                        for z in range(2):
                            t = mm3(bank[:, 128 * z:128 * z + 128], ql[0], ql[1], kt[0][rows, 0:128],
                                    kt[1][rows, 0:128], True, True)
                    else:
                        ks = slice(128 * (n - 1), 128 * (n + 1))
                        t = mm3(bank[:, o:o + 256], ql[0], ql[1], kt[0][rows, ks], kt[1][rows, ks], True, True)
                t1 = DV.add(lambda e, m=m, bank=bank, h=h: e.scalar_tensor_tensor(
                    S[:, 2 * m:2 * m + 2, :], bank.rearrange("p (n s) -> p n s", n=2), 0.125,
                    BR[h % 2][:, 2 * m:2 * m + 2, :], ALU.mult, ALU.add), t, bt, sfree[h % 2], t_neg)
                banks.done(bi, t1)
            bfree[h % 2] = [t1]
            if r == 1:
                qfree[hp] = [t]
            if h + 2 < 16:
                bias_t[h + 2] = load_bias(h + 2)
            x = 16 * (h % 3)
            mx, nm, sm_, es = (small[:, 48 + x + 4 * i:52 + x + 4 * i] for i in range(4))
            t2 = DV.add(lambda e: e.tensor_reduce(mx, S, AX.X, ALU.max), t1)
            t3 = DV.add(lambda e: e.tensor_scalar(nm, mx, sinkc[:, h:h + 1], -1.0, ALU.max, ALU.mult), t2)
            for n in range(4):
                t4 = AC.add(lambda e, n=n: e.activation(S[:, n, :], S[:, n, :], ACT.Exp, bias=nm[:, n:n + 1],
                                                        accum_out=sm_[:, n:n + 1]), t3)
            t5 = AC.add(lambda e: e.activation(es, nm, ACT.Exp, bias=sinkc[:, h:h + 1]), t4)
            return t5

        def turns(h, te):
            S = SS[h % 2]
            slot = 4 + 2 * (h % 2)
            toks = []
            for m in range(2):
                bi, bank, was = banks.take()
                PE.wait(was, te)
                for i in range(4):
                    b = 4 * m + i
                    t = PE.add(lambda e, i=i, b=b, bank=bank: e.transpose(
                        bank[:, 128 * i:128 * i + 128], S[:, b // 2, 128 * (b % 2):128 * (b % 2) + 128], ident[:, :]))
                pr = pair(P, slot + m, t, bank, pt_free[h % 2])
                banks.done(bi, *pr)
                toks += pr
            sfree[h % 2] = [t]
            return toks

        def values(h, toks):
            slot = 4 + 2 * (h % 2)
            kv = h // 8
            bi, bank, was = banks.take()
            PE.wait(was, toks, vt)
            for n in range(4):
                js = [j for j in (n - 1, n) if j >= 0]
                for j in js:
                    b = 2 * n + (j - n + 1)
                    c, o = slot + b // 4, 128 * (b % 4)
                    t = mm3(bank[:, 64 * n:64 * n + 64], Ph[:, c, o:o + 128], Pl[:, c, o:o + 128],
                            vA[0][:, j, 64 * kv:64 * kv + 64], vA[1][:, j, 64 * kv:64 * kv + 64],
                            j == js[0], j == n)
            pt_free[h % 2] = [t]
            x = 16 * (h % 3)
            sm_, es = small[:, 56 + x:60 + x], small[:, 60 + x:64 + x]
            t1 = DV.add(lambda e: e.tensor_tensor(sm_, sm_, es, ALU.add), toks)
            t1 = DV.add(lambda e: e.reciprocal(sm_, sm_), t1)
            hl = h % 4
            t2 = DV.add(lambda e: e.tensor_tensor(ot[:, :, 64 * hl:64 * hl + 64],
                                                  bank[:, 0:256].rearrange("p (n d) -> p n d", n=4),
                                                  sm_.unsqueeze(2).broadcast_to([128, 4, 64]), ALU.mult),
                        t1, t, otfree[0])
            banks.done(bi, t2)
            return t2

        for i in range(16 + 2):
            if i < 16:
                if i % 4 == 0:
                    tq = q_group(i // 4)
                if i % 2 == 0:
                    hp = (i // 2) % 2
                    PE.wait(tq)
                    bi, bank, t = turn(lambda n, hp=hp: qt[:, n, 128 * hp:128 * hp + 128], 128)
                    bstate["qt_read"] = t
                    toks = scaled_pair(QT[hp], 128, bank, t, gq_a, qfree[hp])
                    banks.done(bi, *toks)
                    heads.append((QT[hp], toks))
                ex = scores(i)
                if i == 0:
                    exps = {}
                exps[i] = ex
            if 1 <= i <= 16:
                pts = turns(i - 1, exps[i - 1])
                prev = pts
                exps[("p", i - 1)] = pts
            if i >= 2:
                h = i - 2
                to = values(h, exps[("p", h)])
                if h % 4 == 3:
                    g = h // 4
                    for hp in range(2):
                        PE.wait(to)
                        bi, bank, t = turn(lambda n, hp=hp: ot[:, n, 128 * hp:128 * hp + 128], 128)
                        q = 8 + 2 * g + hp
                        pready[q] = pair(P, q, t, bank)
                        banks.done(bi, *pready[q])
                    otfree[0] = t
        out_proj("ao", P, pready, 8)
        for q in range(16):
            pfree[q] = now()

    def attend_b():
        free0 = now()
        AC.wait(free0)
        DV.wait(free0)
        PO.wait(free0)
        Hs = (Hh, Hl, hready)
        cq = mflat(0, 2).rearrange("p (n d) -> p n d", n=4)
        ck = mflat(2, 3).rearrange("p (n d) -> p n d", n=4)
        kr = krt[:, :].rearrange("p (n d) -> p n d", n=4)
        ssq, ssc = small[:, 0:4], small[:, 4:8]
        rq, rc = small[:, 8:12], small[:, 12:16]
        nq, vq = next_tile("bq", 0)
        got, gok = [], []
        for half in range(2):
            bi, bank, t = proj_b(vq[0], 0, 256, 2, 2 * half, 256, 8, Hs)
            ti, tv, was = tmps.take()
            for q in range(2):
                t1 = AC.add(lambda e, q=q, half=half, tv=tv, bank=bank: e.activation(
                    tv[:, 16 + 256 * q:272 + 256 * q], bank[:, 256 * q:256 * q + 256], ACT.Square,
                    accum_out=ssq[:, 2 * half + q:2 * half + q + 1]), t, was)
            tmps.done(ti, t1)
            got.append((bi, bank, t))
        tile_used(nq, t)
        nk, vk = next_tile("bkv", 0)
        for half in range(2):
            bi, bank, t = proj_b(vk[0], 0, 160, 2, 2 * half, 160, 8, Hs)
            ti, tv, was = tmps.take()
            for q in range(2):
                AC.add(lambda e, q=q, half=half, tv=tv, bank=bank: e.activation(
                    tv[:, 16 + 160 * q:144 + 160 * q], bank[:, 160 * q:160 * q + 128], ACT.Square,
                    accum_out=ssc[:, 2 * half + q:2 * half + q + 1]), t, was)
                AC.add(lambda e, q=q, half=half, tv=tv, bank=bank: e.activation(
                    tv[:, 144 + 160 * q:176 + 160 * q], bank[:, 160 * q + 128:160 * q + 160], ACT.Square,
                    accum_out=kr2[:, 2 * half + q:2 * half + q + 1]))
                t1 = AC.add(lambda e, q=q, half=half, bank=bank: e.activation(
                    kr[:, 2 * half + q, :], bank[:, 160 * q + 128:160 * q + 160], ACT.Copy))
            tmps.done(ti, t1)
            gok.append((bi, bank, t))
        tile_used(nk, t)
        t_kr = t1
        ta = rsqrt_small(rq, ssq, 256, t1)
        tb = rsqrt_small(rc, ssc, 128, t1)
        for half in range(2):
            for (bi, bank, t), w, wd, dst, r in ((got[half], 256, 256, cq, rq), (gok[half], 160, 128, ck, rc)):
                for q in range(2):
                    n = 2 * half + q
                    tk = DV.add(lambda e, q=q, n=n, w=w, wd=wd, dst=dst, r=r, bank=bank: e.tensor_scalar(
                        dst[:, n, :], bank[:, w * q:w * q + wd], r[:, n:n + 1], None, ALU.mult), ta, tb)
                banks.done(bi, tk, t_kr)
        PE.wait(tk)
        cready = []
        for c in range(3):
            srcv = (lambda n, c=c: cq[:, n, 128 * c:128 * c + 128]) if c < 2 else (lambda n: ck[:, n, :])
            bi, bank, t = turn(srcv, 128)
            s = gain("b_q_norm_2", c) if c < 2 else gain("b_kv_norm_2", 0)
            toks = scaled_pair((Ph[:, c, :], Pl[:, c, :]), 128, bank, t, s)
            banks.done(bi, *toks)
            cready.append(toks)
        t_c = t
        Cq = (Ph, Pl, cready)
        Ck = (Ph[:, 2:3, :], Pl[:, 2:3, :], cready[2:3])

        qt = mflat(0, 3).rearrange("p (n h d) -> p n h d", n=4, h=4)
        kt = mflat(3, 6).rearrange("p (n h d) -> p n h d", n=4, h=4)
        ot = mflat(6, 8).rearrange("p (n d) -> p n d", n=4)
        vB = [W[:, 3:5, :].rearrange("p a b -> p (a b)").rearrange("p (n h d) -> p n h d", n=4, h=4) for W in P]
        QK = [((Ph[:, 5, :], Pl[:, 5, :]), (Ph[:, 6, :], Pl[:, 6, :])),
              ((Ph[:, 7, :], Pl[:, 7, :]), (Ph[:, 8, :], Pl[:, 8, :]))]
        ER = Ring([Z[:, 512 * i:512 * i + 512] for i in range(4)])
        PT = Ring([9, 10, 11, 12])
        sc = 96 ** -0.5
        st = {"v": [], "qk": [t_c], "o": [], "last": None}
        qkfree = [[], []]
        sq16, sk16, rq16, rk16 = (small[:, 16 * i:16 * i + 16] for i in range(1, 5))

        def group(g):
            n_, v_ = next_tile("bg", g)
            gq, gk = [], []
            vts = []
            for b in range(4):
                bi, bank, t = proj_b(v_[0], 0, 384, 1, b, 384, 2, Cq)
                gq.append((bi, bank, t))
                ti, tv, was = tmps.take()
                t1 = AC.add(lambda e: e.activation(tv[:, 16:400], bank[:, 0:384], ACT.Square), t, was)
                t2 = DV.add(lambda e: e.tensor_reduce(
                    sq16[:, 4 * b:4 * b + 4], tv[:, 16:400].rearrange("p (h d) -> p h d", h=4), AX.X, ALU.add), t1)
                tmps.done(ti, t2)
            ta = rsqrt_small(rq16, sq16, 96, t2)
            for b in range(4):
                bi, bank, t = gq[b]
                tq = DV.add(lambda e: e.tensor_tensor(
                    qt[:, b, :, :], bank[:, 0:384].rearrange("p (h d) -> p h d", h=4),
                    rq16[:, 4 * b:4 * b + 4].unsqueeze(2).broadcast_to([128, 4, 96]), ALU.mult), ta, st["qk"])
                banks.done(bi, tq)
            for b in range(4):
                bi, bank, t = proj_b(v_[1], 0, 512, 1, b, 512, 1, Ck)
                gk.append((bi, bank, t))
                ti, tv, was = tmps.take()
                bv = bank.rearrange("p (h d) -> p h d", h=4)
                t1 = AC.add(lambda e: e.activation(
                    tv[:, 16:272].rearrange("p (h d) -> p h d", h=4), bv[:, :, 0:64], ACT.Square), t, was)
                t2 = DV.add(lambda e: e.tensor_reduce(
                    sk16[:, 4 * b:4 * b + 4], tv[:, 16:272].rearrange("p (h d) -> p h d", h=4), AX.X, ALU.add), t1)
                tmps.done(ti, t2)
                t2 = DV.add(lambda e: e.tensor_scalar(sk16[:, 4 * b:4 * b + 4], sk16[:, 4 * b:4 * b + 4],
                                                      kr2[:, b:b + 1], None, ALU.add), t2)
                h = AC.add(lambda e: e.activation(vB[0][:, b, :, :], bv[:, :, 64:128], ACT.Copy), t, st["v"])
                l = DV.add(lambda e: e.tensor_tensor(vB[1][:, b, :, :], bv[:, :, 64:128], f(vB[0][:, b, :, :]),
                                                     ALU.subtract), h, st["v"])
                vts += [h, l]
            tile_used(n_, t)
            tb = rsqrt_small(rk16, sk16, 96, t2)
            for b in range(4):
                bi, bank, t = gk[b]
                tk = DV.add(lambda e: e.tensor_tensor(
                    kt[:, b, :, 0:64], bank.rearrange("p (h d) -> p h d", h=4)[:, :, 0:64],
                    rk16[:, 4 * b:4 * b + 4].unsqueeze(2).broadcast_to([128, 4, 64]), ALU.mult), tb, st["qk"])
                banks.done(bi, tk, *vts)
                tk = DV.add(lambda e: e.tensor_tensor(
                    kt[:, b, :, 64:96], kr[:, b, :].unsqueeze(1).broadcast_to([128, 4, 32]),
                    rk16[:, 4 * b:4 * b + 4].unsqueeze(2).broadcast_to([128, 4, 32]), ALU.mult), tb, t_kr)
            done = []
            for E, tens, base, t0 in ((DV, qt, 0, tq), (PO, kt, 4, tk)):
                i0, z0, w0 = tmps.take()
                i1, z1, w1 = tmps.take()
                tmp = [z0[:, 16:272], z0[:, 272:528], z1[:, 16:272], z1[:, 272:528]]
                tmp = [x.rearrange("p (n h d) -> p n h d", n=4, h=4) for x in tmp]
                x, y = tens[:, :, :, 64:80], tens[:, :, :, 80:96]
                tab = [ropt[:, base + j, :].rearrange("p (n d) -> p n d", n=4).unsqueeze(2)
                       .broadcast_to([128, 4, 4, 16]) for j in range(4)]
                for o, i, j in ((0, x, 0), (1, y, 1), (2, y, 2), (3, x, 3)):
                    t = E.add(mul3(tmp[o], i, tab[j]), t0, w0, w1, t_rope)
                t = E.add(lambda e, x=x, tmp=tmp: e.tensor_tensor(x, tmp[0], tmp[1], ALU.subtract), t)
                t = E.add(lambda e, y=y, tmp=tmp: e.tensor_tensor(y, tmp[2], tmp[3], ALU.add), t)
                tmps.done(i0, t)
                tmps.done(i1, t)
                done.append(t)
            return done, vts

        def head_qk(h, done):
            hl, s = h % 4, h % 2
            PE.wait(done)
            res = []
            for src, dst, gcol in ((qt, QK[s][0], gq_b), (kt, QK[s][1], gk_b)):
                bi, bank, t = turn(lambda n, src=src: src[:, n, hl, :], 96)
                toks = scaled_pair([d[0:96, :] for d in dst], 96, bank[0:96, :], t, gcol[0:96, :], qkfree[s], t_g1)
                banks.done(bi, *toks)
                res += toks
            if hl == 3:
                st["qk"] = [t]
            return res

        def scores(h, n, ready):
            s = h % 2
            (qh, ql), (kh, kl) = QK[s]
            L = 128 * (n + 1)
            bi, bank, was = banks.take()
            PE.wait(was, ready)
            qs = slice(128 * n, 128 * n + 128)
            PE.add(lambda e: e.matmul(bank[:, 0:L], ql[0:96, qs], kh[0:96, 0:L], start=True, stop=False), signal=False)
            PE.add(lambda e: e.matmul(bank[:, 0:L], qh[0:96, qs], kl[0:96, 0:L], start=False, stop=False),
                   signal=False)
            PE.add(lambda e: e.matmul(bank[:, 0:L], qh[0:96, qs], kh[0:96, 0:L], start=False, stop=False),
                   signal=False)
            t = PE.add(lambda e: e.matmul(bank[:, 128 * n:L], identb[:, :], maskb[:, :], start=False, stop=True))
            if n == 3:
                qkfree[s] = [t]
            x = (h % 4) * 4 + n
            mx = mneg[:, x:x + 1]
            nm = mneg[:, 16 + x:17 + x]
            t1 = DV.add(lambda e: e.tensor_reduce(mx, bank[:, 0:L], AX.X, ALU.max), t)
            t1 = DV.add(lambda e: e.tensor_scalar(nm, mx, -sc, None, ALU.mult), t1)
            ei, E, w = ER.take()
            y = (h % 8) * 4 + n
            t2 = AC.add(lambda e: e.activation(E[:, 0:L], bank[:, 0:L], ACT.Exp, bias=nm, scale=sc,
                                               accum_out=sums[:, y:y + 1]), t1, w)
            banks.done(bi, t2)
            return ei, E, t2

        def turns(n, ei, E, te):
            L = 128 * (n + 1)
            bi, bank, was = banks.take()
            PE.wait(was, te)
            for j in range(n + 1):
                t = PE.add(lambda e, j=j: e.transpose(bank[:, 128 * j:128 * j + 128], E[:, 128 * j:128 * j + 128],
                                                      ident[:, :]))
            ER.done(ei, t)
            pi, slot, w = PT.take()
            hh = AC.add(lambda e: e.activation(Ph[:, slot, 0:L], bank[:, 0:L], ACT.Copy), t, w)
            ll = DV.add(lambda e: e.tensor_tensor(Pl[:, slot, 0:L], bank[:, 0:L], f(Ph[:, slot, 0:L]), ALU.subtract),
                        hh, w)
            banks.done(bi, hh, ll)
            return pi, slot, [hh, ll]

        obank, obanks = {}, banks.part(2)

        def values(h, n, pi, slot, toks, vts):
            hl = h % 4
            if n == 0:
                obank[h] = obanks.take()
            bi, bank, was = obank[h]
            PE.wait(was, toks, vts)
            for j in range(n + 1):
                sl = slice(128 * j, 128 * j + 128)
                t = mm3(bank[:, 64 * n:64 * n + 64], Ph[:, slot, sl], Pl[:, slot, sl], vB[0][:, j, hl, :],
                        vB[1][:, j, hl, :], j == 0, j == n)
            PT.done(pi, t)
            if n == 3:
                y = (h % 8) * 4
                t1 = DV.add(lambda e: e.reciprocal(sums[:, y:y + 4], sums[:, y:y + 4]), toks)
                t2 = DV.add(lambda e: e.tensor_tensor(ot[:, :, 64 * hl:64 * hl + 64],
                                                      bank[:, 0:256].rearrange("p (n d) -> p n d", n=4),
                                                      sums[:, y:y + 4].unsqueeze(2).broadcast_to([128, 4, 64]),
                                                      ALU.mult), t1, t, st["o"])
                obanks.done(bi, t2)
                if hl == 3:
                    st["v"] = [t]
                return t2
            return None

        for g in range(4):
            done, vts = group(g)
            items = [(4 * g + hl, n) for hl in range(4) for n in range(4)]
            sco, tur = {}, {}
            for i in range(16 + 2):
                if i < 16:
                    h, n = items[i]
                    if n == 0:
                        qk = head_qk(h, done)
                    sco[i] = scores(h, n, qk)
                if 1 <= i <= 16:
                    tur[i - 1] = turns(items[i - 1][1], *sco.pop(i - 1))
                if i >= 2:
                    h, n = items[i - 2]
                    to = values(h, n, *tur.pop(i - 2), vts)
            for hp in range(2):
                PE.wait(to)
                bi, bank, t = turn(lambda n: ot[:, n, 128 * hp:128 * hp + 128], 128)
                oready[2 * g + hp] = pair(H, 2 * g + hp, t, bank)
                banks.done(bi, *oready[2 * g + hp])
            st["o"] = [t]
        banks.join(obanks)
        out_proj("bo", H, oready, 0)
        for q in range(16):
            pfree[q] = now()

    oready = [[] for _ in range(8)]

    bstate["mfree"] = now()
    plan_bias()
    norm("ffn_norm1_2", 0)
    ffn("s0", "glu")
    while extras:
        extra(1)
    norm("mix_norm_2", 0)
    attend_a()
    norm("ffn_norm2_2", 0)
    ffn("s1", "glu")
    norm("ffn_norm1_2", 8)
    ffn("s2", "glu")
    norm("mix_norm_2", 8)
    attend_b()
    norm("ffn_norm2_2", 8)
    ffn("s3", "glu")

    om = M[:, :, :].rearrange("p a b -> p (a b)").rearrange("p (n d) -> p n d", n=4)
    t_free = [(AC.sem, AC.n), (PE.sem, PE.n), (DV.sem, DV.n)]
    for n in range(4):
        for half in range(2):
            bi, bank, was = banks.take()
            PE.wait(was)
            for q in range(4):
                c = 4 * half + q
                t = PE.add(lambda e, n=n, c=c, q=q, bank=bank: e.transpose(
                    bank[:, 128 * q:128 * q + 128], X[:, c, 128 * n:128 * n + 128], ident[:, :]), xt[c])
            eng, put = ((DV, lambda e, o, b: e.tensor_copy(o, b)),
                        (AC, lambda e, o, b: e.activation(o, b, ACT.Copy)))[half]
            t1 = eng.add(lambda e, n=n, half=half, bank=bank, put=put: put(e, om[:, n, 512 * half:512 * half + 512],
                                                                           bank), t, t_free)
            banks.done(bi, t1)
            t_out = SP.dma(cs["out"], out[0, 128 * n:128 * n + 128, 512 * half:512 * half + 512],
                           om[:, n, 512 * half:512 * half + 512], t1)
    SP.wait(t_out, bstate["bw"], bstate.get("fill"), bstate["pos"])


INS = ['x', 'p', 'mix_norm', 'w_in', 'w_pool', 'pool_scale', 'sgu_norm', 'w_spatial', 'b_spatial', 'w_branch_a',
       'w_branch_b', 'w_out', 'ffn_norm', 'w_up', 'conv_w', 'conv_b', 'w_down', 'ple_norm', 'w_ple_gate', 'w_ple',
       'final_norm', 'positions_2', 'rel_bias_2', 'ffn_norm1_2', 'ffn1_wg_2', 'ffn1_wu_2', 'ffn1_wd_2', 'mix_norm_2',
       'ffn_norm2_2', 'ffn2_wg_2', 'ffn2_wu_2', 'ffn2_wd_2', 'a_w_in_2', 'a_q_gain_2', 'a_k_gain_2', 'a_sinks_2',
       'a_w_out_2', 'b_w_in_2', 'b_q_norm_2', 'b_kv_norm_2', 'b_w_uq_2', 'b_w_ukv_2', 'b_q_gain_2', 'b_k_gain_2',
       'b_w_out_2']


def kernel(**inputs):
    import numpy as _np
    import concourse.bacc as _bacc
    from concourse import mybir as _mybir
    from concourse.bass_utils import run_bass_kernel_spmd as _run

    nc = _bacc.Bacc("TRN2", target_bir_lowering=False, num_devices=1, dynamic_dma_scratch_size=1024)
    arrays, args = {}, {}
    for name in INS:
        v = _np.ascontiguousarray(inputs[name])
        arrays[f"in_{name}"] = v
        args[name] = nc.dram_tensor(f"in_{name}", v.shape, _mybir.dt.from_np(v.dtype), kind="ExternalInput").ap()
    out = nc.dram_tensor("out_0", (1, T, D), F32, kind="ExternalOutput").ap()
    program(nc, args, out)
    r = _run(nc, [arrays], core_ids=[0])
    return r.results[0]["out_0"]
```

```python
import math
from contextlib import ExitStack

import numpy as np
import concourse.bass as bass
from concourse import mybir

F32 = mybir.dt.float32
F32R = mybir.dt.float32r
BF16 = mybir.dt.bfloat16
I32 = mybir.dt.int32
ALU = mybir.AluOpType
ACT = mybir.ActivationFunctionType
AX = mybir.AxisListType

T, D, DFF = 512, 1024, 2816
EPS = 1e-6
NEG = -1e30
AH, BH = 16, 16
ROPE_HALF = 16
LOWEST = -3.0e38


def bucket_bounds():
    def bucket(n):
        if n < 16:
            return n
        return min(31, 16 + int(math.log(n / 16) / math.log(8) * 16))
    return [min(n for n in range(200) if bucket(n) >= k) for k in range(1, 32)]


class Queue:

    def __init__(self, engine, sem):
        self.e, self.sem, self.n, self.seen = engine, sem, 0, {}

    def wait(self, *after):
        for tok in after:
            if tok is None:
                continue
            if isinstance(tok, list):
                self.wait(*tok)
                continue
            sem, v = tok
            if self.seen.get(sem.name, 0) < v:
                self.seen[sem.name] = v
                self.e.wait_ge(sem, v)

    def add(self, fn, *after, signal=True):
        self.wait(*after)
        ins = fn(self.e)
        if not signal:
            return None
        self.n += 1
        ins.then_inc(self.sem, 1)
        return (self.sem, self.n)

    def dma(self, sem, out, in_, *after):
        self.wait(*after)
        sem[1] += 16
        self.e.dma_start(out, in_).then_inc(sem[0], 16)
        return (sem[0], sem[1])


class Ring:

    def __init__(self, views):
        self.views, self.free, self.i = views, [[] for _ in views], -1

    def take(self):
        self.i = (self.i + 1) % len(self.views)
        was, self.free[self.i] = self.free[self.i], []
        return self.i, self.views[self.i], was

    def part(self, k):
        other = Ring(self.views[-k:])
        other.free = self.free[-k:]
        self.views, self.free, self.i = self.views[:-k], self.free[:-k], -1
        return other

    def join(self, other):
        self.views, self.free = self.views + other.views, self.free + other.free

    def done(self, i, *toks):
        self.free[i] += [t for t in toks if t is not None]


def program(nc, a, out):
    ctx = ExitStack()
    with ctx:
        build(nc, a, out, ctx)


def build(nc, a, out, ctx):
    def sb(name, shape, dt=F32):
        return ctx.enter_context(nc.sbuf_tensor(name, shape, dt))

    def sem(name):
        return ctx.enter_context(nc.semaphore(name))

    ctx.enter_context(nc.allow_non_contiguous_dma(reason="a few short columns"))
    PE, AC, DV, PO, SP = (Queue(e, sem(n)) for e, n in ((nc.tensor, "s_pe"), (nc.scalar, "s_act"), (nc.vector, "s_dve"),
                                                        (nc.gpsimd, "s_pool"), (nc.sync, "s_sp")))

    X = sb("X", [128, 8, T])
    Hh, Hl = sb("Hh", [128, 8, T], F32R), sb("Hl", [128, 8, T], F32R)
    Ph, Pl = sb("Ph", [128, 16, T], F32R), sb("Pl", [128, 16, T], F32R)
    M = sb("M", [128, 8, T])
    RAW = sb("RAW", [128, 2, 2048])
    Wh, Wl = sb("Wh", [128, 3, 2048], F32R), sb("Wl", [128, 3, 2048], F32R)
    NT = 4
    TMP = sb("TMP", [128, NT, 528])
    Z = sb("Z", [128, 2048])
    WS = sb("WS", [128, 2, T], F32R)
    ident, ones = sb("ident", [128, 128]), sb("ones", [128, 128])
    identb, maskb = sb("identb", [128, 128], BF16), sb("maskb", [128, 128], BF16)
    P0, P1, P2 = sb("P0", [128, 99]), sb("P1", [128, 88]), sb("P2", [128, 88])
    rb2 = sb("rb2", [128, 48])
    drb3 = sb("drb3", [128, 48], BF16)
    pki = sb("pki", [128, 384], I32)
    pkf = sb("pkf", [128, 384])
    krt = sb("krt", [128, 128])
    rope = M[:, 6, :].rearrange("p (a b) -> p a b", a=8)
    sm = sb("sm", [128, 320])
    ropt = sb("ropt", [128, 8, 64])
    smi = sb("smi", [128, 4], I32)

    BANK = [ctx.enter_context(nc.psum_tensor(f"bank{i}", [128, 512], F32)) for i in range(8)]
    banks = Ring([b[:, :] for b in BANK])

    eps = sm[:, 0:1]
    posf = sm[:, 1:5]
    gq_a, gk_a, gq_b, gk_b = sm[:, 5:6], sm[:, 6:7], sm[:, 7:8], sm[:, 8:9]
    rinv = sm[:, 16:32]
    sinkc = sm[:, 32:48]
    invf = sm[:, 48:64]
    grow_q, grow_k = sm[:, 64:96], sm[:, 96:128]
    st4, rs4 = sm[:, 128:132], sm[:, 132:136]
    kr2 = sm[:, 136:140]
    lo = sm[:, 9:10]
    mneg, sums, small = sm[:, 160:192], sm[:, 192:224], sm[:, 224:320]

    cs = {n: [sem("d_" + n), 0] for n in ("x", "par", "par1", "par2", "sm", "pos", "pos2", "rb", "ws", "p", "fill",
                                         "bw", "out", "bs0", "bs1", "pscr")}
    raws = [[sem(f"d_raw{i}"), 0] for i in range(2)]

    BS = nc.dram_tensor("bias_scratch", (16, 4, 128, 256), F32, kind="Internal").ap()
    PS = nc.dram_tensor("pos_scratch", (T + 128,), I32, kind="Internal").ap()

    def f(ap):
        return ap.bitcast(F32)

    def consts():
        z = PO.add(lambda e: e.memset(ident[:, :], 0.0))
        o = PO.add(lambda e: e.memset(ones[:, :], 1.0))
        PO.add(lambda e: e.memset(eps, EPS))
        PO.add(lambda e: e.memset(gq_b, 1.0))
        PO.add(lambda e: e.memset(gk_b, 1.0))
        tid = PO.add(lambda e: e.affine_select(out=ident[:, :], in_=ident[:, :], compare_op=ALU.not_equal, fill=1.0,
                                               base=0, pattern=[[-1, 128]], channel_multiplier=1), z)
        b0 = PO.add(lambda e: e.memset(identb[:, :], 0.0))
        PO.add(lambda e: e.affine_select(out=identb[:, :], in_=identb[:, :], compare_op=ALU.not_equal, fill=1.0,
                                         base=0, pattern=[[-1, 128]], channel_multiplier=1), b0)
        b1 = PO.add(lambda e: e.memset(maskb[:, :], 0.0))
        tmb = PO.add(lambda e: e.affine_select(out=maskb[:, :], in_=maskb[:, :], compare_op=ALU.is_ge, fill=NEG,
                                               base=0, pattern=[[-1, 128]], channel_multiplier=1), b1)
        for t in range(16):
            PO.add(lambda e, t=t: e.memset(rinv[:, t:t + 1], float(np.float32(1.0) / np.float32(t + 1))))
            PO.add(lambda e, t=t: e.memset(invf[:, t:t + 1],
                                           float(np.float32(10000.0) ** np.float32(-2.0 * t / 32))))
        tc = PO.add(lambda e: e.memset(TMP[:, :, 0:16], 0.0))
        return tc

    t_const = consts()

    PARS = [("mix_norm", 8), ("pool_scale", 8), ("sgu_norm", 8), ("ffn_norm", 8), ("ple_norm", 8), ("final_norm", 8),
            ("ffn_norm1_2", 16), ("mix_norm_2", 16), ("ffn_norm2_2", 16), ("b_q_norm_2", 2), ("b_kv_norm_2", 1)]
    col = {}
    stage = M[:, 7, :]

    def flat(ap):
        n = len(ap.shape)
        if n == 1:
            return ap
        names = "abcd"[:n]
        return ap.rearrange(" ".join(names) + " -> (" + " ".join(names) + ")")

    def parameters():
        r = 0
        tok = None
        for name, n in PARS:
            col[name] = r
            tok = SP.dma(cs["par"], stage[r:r + n, 0:128], flat(a[name]).rearrange("(c p) -> c p", p=128))
            r += n
        cb = flat(a["conv_b"]).rearrange("(c p) -> c p", p=128)
        cw = a["conv_w"][0].rearrange("k (c p) -> (k c) p", p=128)
        SP.dma(cs["par"], stage[0:44, 128:256], cb)
        SP.dma(cs["par"], stage[44:88, 128:256], cw[0:44, :])
        tok = SP.dma(cs["par"], stage[0:88, 256:384], cw[44:132, :])
        bi, bank, was = banks.take()
        PE.wait(was, t_const, tok)
        for i, (n, d) in enumerate(((99, P0), (88, P1), (88, P2))):
            tk = PE.add(lambda e, i=i, n=n: e.transpose(bank[:, 128 * i:128 * i + n], stage[0:n, 128 * i:128 * i + 128],
                                                        ident[0:n, 0:n]))
        for i, (n, d) in enumerate(((99, P0), (88, P1), (88, P2))):
            t = DV.add(lambda e, i=i, n=n, d=d: e.tensor_copy(d[:, :], bank[:, 128 * i:128 * i + n]), tk)
        banks.done(bi, t)
        return t

    def gain(name, c, base=0):
        return P0[:, col[name] + base + c:col[name] + base + c + 1]

    def convp(k, c):
        r = 44 * (k + 1) + c
        return P1[:, r:r + 1] if r < 88 else P2[:, r - 88:r - 87]

    tiles = []

    def square(src, k, c0, w=256):
        return [(0, k, w, src[:, c0:c0 + w])]

    def rows4(src, i):
        return [(0, 2, 1024, src[256 * i:256 * i + 256, :])]

    def plan():
        win = a["w_in"][0]
        for i in range(4):
            tiles.append(("pool", i, square(win, 8, 256 * i)))
        tiles.append(("wpool", 0, [(0, 8, 256, a["w_pool"][0].rearrange("g c d -> (g c) d"))]))
        for i in range(4):
            tiles.append(("wa", i, square(a["w_branch_a"][0], 8, 256 * i)))
            tiles.append(("ga", i, square(win, 8, 3072 + 256 * i)))
        for i in range(4):
            tiles.append(("v", i, square(win, 8, 2048 + 256 * i)))
        for i in range(4):
            tiles.append(("u", i, square(win, 8, 1024 + 256 * i)))
        for i in range(4):
            tiles.append(("wb", i, square(a["w_branch_b"][0], 8, 256 * i)))
            tiles.append(("gb", i, square(win, 8, 4096 + 256 * i)))
        for i in range(4):
            tiles.append(("wo", i, square(a["w_out"][0], 8, 256 * i)))
        plan_ffn("f", a["w_up"][0], a["w_up"][0], DFF, a["w_down"][0])
        tiles.append(("ple", 0, [(0, 2, 1024, a["w_ple"][0])]))
        for i in range(4):
            tiles.append(("pg", i, square(a["w_ple_gate"][0], 8, 256 * i)))
        plan_ffn("s0", a["ffn1_wg_2"][0], a["ffn1_wu_2"][0], 0, a["ffn1_wd_2"][0])
        wi = a["a_w_in_2"][0]
        tiles.append(("akv", 0, square(wi, 8, 1024)))
        for name, i in (("aq", 0), ("aq", 1), ("aq", 2), ("ao", 0), ("aq", 3), ("ao", 1), ("ao", 2), ("ao", 3)):
            tiles.append((name, i, square(wi, 8, 256 * i) if name == "aq" else rows4(a["a_w_out_2"][0], i)))
        plan_ffn("s1", a["ffn2_wg_2"][0], a["ffn2_wu_2"][0], 0, a["ffn2_wd_2"][0])
        plan_ffn("s2", a["ffn1_wg_2"][1], a["ffn1_wu_2"][1], 0, a["ffn1_wd_2"][1])
        wi = a["b_w_in_2"][0]
        tiles.append(("bq", 0, square(wi, 8, 0)))
        tiles.append(("bkv", 0, square(wi, 8, 256, 160)))
        for name, g in (("bg", 0), ("bg", 1), ("bo", 0), ("bg", 2), ("bo", 1), ("bg", 3), ("bo", 2), ("bo", 3)):
            tiles.append((name, g, rows4(a["b_w_out_2"][0], g) if name == "bo" else
                          [(0, 2, 384, a["b_w_uq_2"][0][:, 384 * g:384 * g + 384]),
                           (768, 1, 512, a["b_w_ukv_2"][0][:, 512 * g:512 * g + 512])]))
        plan_ffn("s3", a["ffn2_wg_2"][1], a["ffn2_wu_2"][1], 0, a["ffn2_wd_2"][1])

    THIRDS = ((0, 8), (8, 8), (16, 6))

    def plan_ffn(tag, wa, wb, off, wd):
        for h, (c0, n) in enumerate(THIRDS):
            for j in range(n // 2):
                tiles.append((tag + "a", (h, j), square(wa, 8, 128 * c0 + 256 * j)))
                tiles.append((tag + "b", (h, j), square(wb, 8, off + 128 * c0 + 256 * j)))
            for i in range(4):
                tiles.append((tag + "d", (h, i), [(0, n, 256, wd[128 * c0:128 * (c0 + n), 256 * i:256 * i + 256])]))

    plan()
    NW = len(tiles)
    landed, halves, split, used = {}, {}, {}, {}
    state = {"dma": 0, "split": 0, "use": 0}

    def size(n):
        return max(o + k * w for o, k, w, _ in tiles[n][2])

    def load_tile():
        n = state["dma"]
        if n >= NW:
            return
        state["dma"] += 1
        for o, k, w, src in tiles[n][2]:
            dst = RAW[:, n % 2, o:o + k * w].rearrange("p (k w) -> p k w", k=k)
            landed[n] = SP.dma(raws[n % 2], dst, src.rearrange("(k p) w -> p k w", p=128), split.get(n - 2))

    def split_tile():
        n = state["split"]
        if n >= NW:
            return
        state["split"] += 1
        s, z = n % 3, size(n)
        parts = [(0, z // 2), (z // 2, z)]
        ta = [AC.add(lambda e, x=x, y=y: e.activation(Wh[:, s, x:y], RAW[:, n % 2, x:y], ACT.Copy),
                     landed[n], used.get(n - 3)) for x, y in parts]
        td = [DV.add(lambda e, x=x, y=y: e.tensor_tensor(Wl[:, s, x:y], RAW[:, n % 2, x:y], f(Wh[:, s, x:y]),
                                                         ALU.subtract), t, used.get(n - 3))
              for (x, y), t in zip(parts, ta)]
        split[n] = td

    def next_tile(name, i, ahead=2):
        n = state["use"]
        assert tiles[n][0:2] == (name, i), (tiles[n][0:2], name, i)
        state["use"] += 1
        assert n + ahead - 3 < 0 or n + ahead - 3 in used
        while state["split"] <= min(n + ahead, NW - 1):
            split_tile()
            load_tile()
        s = n % 3
        views = []
        for o, k, w, _ in tiles[n][2]:
            views.append(tuple(W[:, s, o:o + k * w].rearrange("p (k w) -> p k w", k=k) for W in (Wh, Wl)))
        PE.wait(split[n])
        return n, views

    def tile_used(n):
        used[n] = (PE.sem, PE.n)

    def mm3(o, lh, ll, rh, rl, start, stop):
        PE.add(lambda e: e.matmul(o, ll, rh, start=start, stop=False), signal=False)
        PE.add(lambda e: e.matmul(o, lh, rl, start=False, stop=False), signal=False)
        return PE.add(lambda e: e.matmul(o, lh, rh, start=False, stop=stop), signal=stop)

    hready = [[] for _ in range(8)]
    pready = [[] for _ in range(16)]

    def form_a(views, K, src, ready, base=0, m=2, kw=0, ring=None, scaled=None,
               wide=False):
        res = []
        wh, wl = views
        if wide:
            got = [(ring or banks).take() for _ in range(m)]
            last = [None] * m
            for k0, k1 in ((0, K - 2), (K - 2, K)):
                for c in range(m):
                    PE.wait(got[c][2])
                    cc = slice((kw + c) * 128, (kw + c + 1) * 128)
                    for k in range(k0, k1):
                        PE.wait(ready[base + k])
                        last[c] = mm3(got[c][1], wh[:, k, cc], wl[:, k, cc], src[0][:, base + k, :],
                                      src[1][:, base + k, :], k == 0, k == K - 1)
            return [(got[c][0], got[c][1], last[c]) for c in range(m)]
        for c in range(m):
            bi, bank, was = (ring or banks).take()
            PE.wait(was)
            for k in range(K):
                PE.wait(ready[base + k])
                cc = slice((kw + c) * 128, (kw + c + 1) * 128)
                t = mm3(bank, wh[:, k, cc], wl[:, k, cc], src[0][:, base + k, :], src[1][:, base + k, :],
                        k == 0, k == K - 1)
            res.append((bi, bank, t))
            norm_step()
        if scaled is not None:
            assert not nstate["todo"]
            res = [(bi, bank, DV.add(lambda e, bank=bank: e.tensor_tensor(bank, bank, scaled, ALU.mult), t,
                                     nstate["R"])) for bi, bank, t in res]
        return res

    def norm_step():
        if nstate["todo"]:
            nstate["todo"].pop(0)()

    H, P = (Hh, Hl), (Ph, Pl)

    def pair(dst, c, src_tok, view, *was):
        h = AC.add(lambda e: e.activation(dst[0][:, c, :], view, ACT.Copy), src_tok, *was)
        l = DV.add(lambda e: e.tensor_tensor(dst[1][:, c, :], view, f(dst[0][:, c, :]), ALU.subtract), h, *was)
        return [h, l]

    xt = [[] for _ in range(8)]
    SQ = TMP[:, NT - 1, 16:528]
    tmps = Ring([TMP[:, i, :] for i in range(NT - 1)])
    bstate = {"nt": None}
    nstate = {"sq": None, "read": [], "rs": None, "todo": [], "R": None, "hread": None, "rst": None}

    nt = sb("nt", [128, 32])

    def rsqrt_small(dst, src, n, *after):
        w = dst.shape[1]
        v, u = nt[:, 0:w], nt[:, 16:16 + w]
        t = DV.add(lambda e: e.tensor_scalar(v, src, 1.0 / n, EPS, ALU.mult, ALU.add), bstate["nt"], *after)
        t = DV.add(lambda e: e.tensor_scalar(u.bitcast(I32), v.bitcast(I32), 1, None, ALU.logical_shift_right), t)
        t = DV.add(lambda e: e.tensor_scalar(dst.bitcast(I32), u.bitcast(I32), -1.0, float(0x5F3759DF), ALU.mult,
                                             ALU.add), t)
        for _ in range(3):
            t = DV.add(lambda e: e.tensor_tensor(u, dst, dst, ALU.mult), t)
            t = DV.add(lambda e: e.scalar_tensor_tensor(u, u, -0.5, v, ALU.mult, ALU.mult), t)
            t = DV.add(lambda e: e.scalar_tensor_tensor(dst, u, 1.5, dst, ALU.add, ALU.mult), t)
        bstate["nt"] = t
        return t

    def stats(c):
        if c == 0:
            nstate["sq"] = AC.add(lambda e: e.activation(SQ, X[:, c, :], ACT.Square), xt[c], nstate["read"])
            xt[c] = xt[c] + [nstate["sq"]]
            return
        ti, tv, was = tmps.take()
        v = tv[:, 16:528]
        s = AC.add(lambda e: e.activation(v, X[:, c, :], ACT.Square), xt[c], was)
        xt[c] = xt[c] + [s]
        nstate["sq"] = PO.add(lambda e: e.tensor_tensor(SQ, SQ, v, ALU.add), s, nstate["sq"])
        tmps.done(ti, nstate["sq"])

    def h_pair(c, name, base=0):
        g = gain(name, c, base)
        h = AC.add(lambda e: e.activation(Hh[:, c, :], X[:, c, :], ACT.Copy, scale=g), xt[c], nstate["hread"])
        l = DV.add(lambda e: e.scalar_tensor_tensor(Hl[:, c, :], X[:, c, :], g, f(Hh[:, c, :]), ALU.mult,
                                                    ALU.subtract), h, nstate["hread"])
        xt[c] = xt[c] + [h]
        hready[c] = [h, l]

    def h_read():
        nstate["hread"] = (PE.sem, PE.n)

    def rs_columns():
        bi, bank, was = banks.take()
        PE.wait(was, nstate["sq"])
        for n in range(4):
            t = PE.add(lambda e, n=n: e.matmul(bank[:, n:n + 1], SQ[:, 128 * n:128 * n + 128], ones[:, 0:1],
                                               start=True, stop=True))
        nstate["read"] = [t]
        t3 = rsqrt_small(rs4, bank[:, 0:4], D, t, nstate["rs"])
        banks.done(bi, t3)
        return t3

    def rs_diagonal(t3):
        ti, tv, w2 = tmps.take()
        v = tv[:, 16:528]
        DV.wait(t3)
        for n in range(4):
            t4 = DV.add(lambda e, n=n: e.tensor_scalar(v[:, 128 * n:128 * n + 128], ident[:, :], rs4[:, n:n + 1], None,
                                                       ALU.mult), w2)
        nstate["rs"] = t4
        return ti, v, t4

    def rs_spread(ti, v, t4):
        bi, bank, was = banks.take()
        PE.wait(was)
        t5 = PE.add(lambda e: e.matmul(bank, ones[:, :], v, start=True, stop=True), t4)
        tmps.done(ti, t5)
        return bi, bank, t5

    def rstd():
        return rs_spread(*rs_diagonal(rs_columns()))

    def norm_begin(R, *was):
        part = {}

        def first():
            part["d"] = rs_diagonal(rs_columns())

        def second():
            bi, bank, t = rs_spread(*part["d"])
            nstate["R"] = AC.add(lambda e: e.activation(R, bank, ACT.Copy), t, *was)
            banks.done(bi, nstate["R"])
        nstate["rs"] = now()
        nstate["todo"] = [first, second]

    def norm_begin_rows():
        def first():
            nstate["rst"] = rs_columns()
        nstate["rs"] = now()
        nstate["todo"] = [first]

    def now():
        return [(q.sem, q.n) for q in (PE, AC, DV, PO) if q.n]

    def norm(name, base=0):
        bi, bank, tr = rstd()
        pe = (PE.sem, PE.n)
        for c in range(8):
            ti, tv, was = tmps.take()
            v = tv[:, 16:528]
            t = DV.add(lambda e, c=c: e.scalar_tensor_tensor(v, X[:, c, :], gain(name, c, base), bank, ALU.mult,
                                                             ALU.mult), tr, xt[c], was)
            hready[c] = pair(H, c, t, v, pe)
            tmps.done(ti, *hready[c])
        banks.done(bi, t)

    def add_x(c, bank, tok, factor):
        t = DV.add(lambda e: e.scalar_tensor_tensor(X[:, c, :], bank, factor, X[:, c, :], ALU.mult, ALU.add),
                   tok, xt[c])
        xt[c] = [t]
        return t

    def ffn(tag, kind, after=None, after_base=0):
        for h, (c0, n) in enumerate(THIRDS):
            base = 8 * (h % 2)
            for j in range(n // 2):
                extra(4)
                na, va = next_tile(tag + "a", (h, j))
                ra = form_a(va[0], 8, H, hready, scaled=RF)
                tile_used(na)
                acts = []
                for c in range(2):
                    cc = c0 + 2 * j + c
                    bi, bank, t = ra[c]
                    if kind == "conv":
                        v, toks, ti = conv(cc, bank, t, bi)
                        t2 = AC.add(lambda e, v=v: e.activation(v, v, ACT.Gelu), toks)
                        acts.append((v, t2, ti))
                    else:
                        ti, tv, was = tmps.take()
                        v = tv[:, 16:528]
                        t2 = AC.add(lambda e, v=v, bank=bank: e.activation(v, bank, ACT.Silu), t, was)
                        banks.done(bi, t2)
                        acts.append((v, t2, ti))
                nb, vb = next_tile(tag + "b", (h, j))
                rb = form_a(vb[0], 8, H, hready, scaled=RF)
                tile_used(nb)
                for c in range(2):
                    cc = c0 + 2 * j + c
                    bi, bank, t = rb[c]
                    v, t2, ti = acts[c]
                    if kind == "conv":
                        w, toks, tj = conv(22 + cc, bank, t, bi)
                        t3 = DV.add(lambda e, v=v, w=w: e.tensor_tensor(v, v, w, ALU.mult), toks, t2)
                        tmps.done(tj, t3)
                    else:
                        t3 = DV.add(lambda e, v=v, bank=bank: e.tensor_tensor(v, v, bank, ALU.mult), t, t2)
                        banks.done(bi, t3)
                    q = base + 2 * j + c
                    pready[q] = pair(P, q, t3, v, pfree[q])
                    tmps.done(ti, *pready[q])
            if h == 2:
                h_read()
            for i in range(4):
                extra(3)
                nd, vd = next_tile(tag + "d", (h, i))
                rd = form_a(vd[0], n, P, pready, base=base, wide=i == 0)
                tile_used(nd)
                for c in range(2):
                    bi, bank, t = rd[c]
                    banks.done(bi, add_x(2 * i + c, bank, t, 1.0 if kind == "conv" else 0.5))
                    if h == 2 and tag != "s3":
                        if after:
                            h_pair(2 * i + c, after, after_base)
                        stats(2 * i + c)
            for q in range(16):
                pfree[q] = [(PE.sem, PE.n)] if base <= q < base + 8 else pfree[q]

    pfree = [[] for _ in range(16)]
    RF = M[:, 6, :]

    def conv(cc, bank, t, bi):
        ti, tv, was = tmps.take()
        v = tv[:, 16:528]
        t1 = AC.add(lambda e: e.activation(v, bank, ACT.Identity, bias=convp(-1, cc), scale=convp(2, cc)), t, was)
        t2 = DV.add(lambda e: e.scalar_tensor_tensor(v[:, 1:T], bank[:, 0:T - 1], convp(1, cc), v[:, 1:T], ALU.mult,
                                                     ALU.add), t1)
        t3 = DV.add(lambda e: e.scalar_tensor_tensor(v[:, 2:T], bank[:, 0:T - 2], convp(0, cc), v[:, 2:T], ALU.mult,
                                                     ALU.add), t2)
        banks.done(bi, t3)
        return v, [t3], ti

    extras = []

    def extra(n):
        for _ in range(n):
            if extras:
                extras.pop(0)()

    BND = [LOWEST] + [float(b) for b in bucket_bounds()]

    def bias_consts():
        rows = Z[:, 0:128].rearrange("p (n k) -> p n k", n=4)
        was = bstate["t"]
        for k in range(32):
            t = PO.add(lambda e, k=k: e.memset(rows[:, :, k:k + 1], BND[k]), was)
        t1 = DV.add(lambda e: e.tensor_tensor(Z[:, 0:128], Z[:, 0:128], ident[:, :], ALU.mult), t, was)
        t1 = DV.add(lambda e: e.tensor_reduce(lo, Z[:, 0:128], AX.X, ALU.add), t1)
        tz = PO.add(lambda e: e.memset(rb2[:, 16:32], 0.0))
        rb = a["rel_bias_2"]
        for n in range(4):
            SP.dma(cs["rb"], rb2[32 * n:32 * n + 32, 0:16], rb)
            t = SP.dma(cs["rb"], rb2[32 * n + 1:32 * n + 32, 16:32], rb[0:31, :], tz)
        bstate["rb"] = t
        for n in range(4):
            SP.dma(cs["pos2"], pki[32 * n:32 * n + 32, 0:255],
                   PS[1 + 128 * n:256 + 128 * n].rearrange("(o n) -> o n", o=1).broadcast_to([32, 255]),
                   bstate["pos"])
            t = SP.dma(cs["pos2"], pki[32 * n:32 * n + 32, 256:384],
                       PS[128 + 128 * n:256 + 128 * n].rearrange("(o n) -> o n", o=1).broadcast_to([32, 128]))
        bstate["pki"] = t

    def bias_table():
        d = rb2[:, 32:48]
        t = bstate["rb"]
        t = DV.add(lambda e: e.tensor_tensor(d, rb2[:, 0:16], rb2[:, 16:32], ALU.subtract), t)
        for j in range(3):
            part = drb3[:, :].rearrange("p (h j) -> p h j", j=3)[:, :, j]
            t = DV.add(lambda e, part=part: e.tensor_copy(part, d), t)
            if j < 2:
                t = DV.add(lambda e, part=part: e.tensor_tensor(d, d, part, ALU.subtract), t)
        bstate["drb"] = t
        t = bstate["pki"]
        DV.add(lambda e: e.tensor_copy(pkf[:, 0:255], pki[:, 0:255]), t)
        bstate["pk"] = DV.add(lambda e: e.tensor_copy(pkf[:, 256:384], pki[:, 256:384]), t)
        bstate["t"] = bstate["t"] + [bstate["pk"]]

    def plan_bias():
        acc = Z[:, :].rearrange("p (h n u) -> p h n u", h=16, n=4)
        GU = 32
        Gv = M[:, 0:4, :].rearrange("p a b -> p (a b)").bitcast(BF16).rearrange("p (q u) -> p q u", q=128)
        pk_t = pkf[:, :]
        for ch in range(4):
            def compare(ch=ch):
                keys = bass.AP(pk_t.tensor, pk_t.offset + GU * ch, [list(pk_t.ap[0]), [1, 128], [1, GU]])
                qs = pkf[:, 256:384].unsqueeze(2).broadcast_to([128, 128, GU])
                bstate["G"] = DV.add(lambda e: e.scalar_tensor_tensor(Gv, keys, lo, qs, ALU.add, ALU.is_le),
                                     bstate["pk"], bstate.get("gread"), bstate["t"], bstate["mfree"])
            extras.append(compare)
            for n in range(4):
                for v in range(4):
                    def step(ch=ch, n=n, v=v):
                        bi, bank, was = banks.take()
                        PE.wait(was, bstate["G"], bstate["drb"])
                        rows = slice(32 * n, 32 * n + 32)
                        for w in range(8):
                            t = PE.add(lambda e, w=w: e.matmul(bank[:, 48 * w:48 * w + 48], Gv[rows, :, 8 * v + w],
                                                               drb3[rows, :], start=True, stop=True))
                        bstate["gread"] = t
                        src = bank[:, 0:384].rearrange("p (u h j) -> p h u j", u=8, j=3)
                        t = DV.add(lambda e: e.tensor_reduce(acc[:, :, n, 8 * v:8 * v + 8], src, AX.X, ALU.add),
                                   t, bstate.get("bw"), bstate["t"])
                        banks.done(bi, t)
                        bstate["acc"] = t
                    extras.append(step)

            def write(ch=ch):
                for h in range(16):
                    dst = bass.AP(BS.tensor, h * 4 * 128 * 256 + 1 + GU * ch, [[257, 128], [128 * 256, 4], [1, GU]])
                    bstate["bw"] = SP.dma(cs["bw"], dst, acc[:, h, :, :], bstate["acc"], bstate["fill"])
            extras.append(write)

    for i in range(2):
        load_tile()
    tx = SP.dma(cs["x"], M[:, 0:7, :].rearrange("p a b -> p (a b)")[:, 0:3072].rearrange("p (n d) -> p n d", n=3),
                a["x"][0, 0:384, :].rearrange("(n p) d -> p n d", p=128))
    tx = SP.dma(cs["x"], Z[:, 0:1024], a["x"][0, 384:512, :])
    t_par = parameters()
    xm = M[:, 0:6, :].rearrange("p a b -> p (a b)").rearrange("p (n d) -> p n d", n=3)
    for c in range(8):
        bi, bank, was = banks.take()
        PE.wait(was, tx, t_const)
        for n in range(4):
            src = xm[:, n, 128 * c:128 * c + 128] if n < 3 else Z[:, 128 * c:128 * c + 128]
            t = PE.add(lambda e, n=n, src=src, bank=bank: e.transpose(bank[:, 128 * n:128 * n + 128], src, ident[:, :]))
        xt[c] = [DV.add(lambda e, c=c, bank=bank: e.tensor_copy(X[:, c, :], bank), t)]
        banks.done(bi, *xt[c])
        stats(c)
    t_x_in = t
    wsp = Z[:, 0:1024].rearrange("p (h s) -> p h s", h=8)
    bsp = Z[:, 1024:2048].rearrange("p (h t) -> p h t", h=8)
    t_ws = SP.dma(cs["ws"], wsp, a["w_spatial"][0].rearrange("h t s -> t h s"), t_x_in)
    t_ws = SP.dma(cs["ws"], Z[:, 1024:2048],
                  flat(a["b_spatial"]).rearrange("(o n) -> o n", o=1).broadcast_to([128, 1024]))
    pos = flat(a["positions_2"])
    SP.wait(t_const)
    SP.dma(cs["sm"], smi[:, :], pos.rearrange("(n p) -> p n", p=128))
    SP.dma(cs["sm"], sinkc, a["a_sinks_2"].broadcast_to([128, 16]))
    for k, (name, w, d) in enumerate((("a_q_gain_2", 64, gq_a), ("a_k_gain_2", 64, gk_a))):
        gcol = flat(a[name]).rearrange("(n o) -> n o", o=1)
        SP.dma(cs["sm"], d[0:64, :], gcol)
        SP.dma(cs["sm"], d[64:128, :], gcol)
    for name, d, row in (("b_q_gain_2", gq_b, grow_q), ("b_k_gain_2", gk_b, grow_k)):
        SP.dma(cs["sm"], d[0:64, :], flat(a[name]).rearrange("(n o) -> n o", o=1)[0:64, :])
        t_sm = SP.dma(cs["sm"], row, a[name][:, 64:96].broadcast_to([128, 32]))
    SP.dma(cs["pscr"], PS[0:128], pos[0:128])
    bstate["pos"] = SP.dma(cs["pscr"], PS[128:640], pos)
    t_g1 = t_sm
    bstate["posf"] = t_posf = DV.add(lambda e: e.tensor_copy(posf, smi[:, :]), t_sm)

    def trig():
        TWO_PI = 2 * math.pi
        c1 = float(np.float32(6.28125))
        c2 = float(np.float32(TWO_PI - c1))
        c3 = float(np.float32(TWO_PI - c1 - c2))
        MAGIC = 12582912.0
        ang, kk, r, t_ = rope[:, 0, :], rope[:, 1, :], rope[:, 2, :], rope[:, 3, :]
        sn, cn = rope[:, 4, :], rope[:, 5, :]
        tk = None
        DV.wait(t_const, t_posf, t_sm)
        for n in range(4):
            tk = DV.add(lambda e, n=n: e.tensor_scalar(ang[:, 16 * n:16 * n + 16], invf, posf[:, n:n + 1], None,
                                                       ALU.mult))
        tk = DV.add(lambda e: e.tensor_scalar(kk, ang, 1.0 / TWO_PI, None, ALU.mult), tk)
        tk = DV.add(lambda e: e.tensor_scalar(kk, kk, MAGIC, None, ALU.add), tk)
        tk = DV.add(lambda e: e.tensor_scalar(kk, kk, -MAGIC, None, ALU.add), tk)
        tk = DV.add(lambda e: e.scalar_tensor_tensor(r, kk, -c1, ang, ALU.mult, ALU.add), tk)
        tk = DV.add(lambda e: e.scalar_tensor_tensor(r, kk, -c2, r, ALU.mult, ALU.add), tk)
        tk = DV.add(lambda e: e.scalar_tensor_tensor(r, kk, -c3, r, ALU.mult, ALU.add), tk)
        PI = float(np.nextafter(np.float32(math.pi), np.float32(0)))
        tk = DV.add(lambda e: e.tensor_scalar(r, r, PI, -PI, ALU.min, ALU.max), tk)
        ts = AC.add(lambda e: e.activation(sn, r, ACT.Sin), tk)
        tk = DV.add(lambda e: e.tensor_scalar(t_, r, -1.0, None, ALU.mult), tk)
        tk = DV.add(lambda e: e.tensor_tensor(t_, t_, r, ALU.max), tk)
        tk = DV.add(lambda e: e.tensor_scalar(t_, t_, -1.0, math.pi / 2, ALU.mult, ALU.add), tk)
        tc = AC.add(lambda e: e.activation(cn, t_, ACT.Sin), tk)
        DV.wait(ts, tc)

    def tables():
        sn, cn = rope[:, 4, :], rope[:, 5, :]
        tk = None
        for row, base in ((grow_q, 0), (grow_k, 4)):
            dst = ropt[:, base:base + 4, :]
            for j, (g, tr) in enumerate(((0, cn), (16, sn), (16, cn), (0, sn))):
                for n in range(4):
                    tk = DV.add(lambda e, j=j, g=g, tr=tr, n=n, dst=dst, row=row: e.tensor_tensor(
                        dst[:, j, 16 * n:16 * n + 16], tr[:, 16 * n:16 * n + 16], row[:, g:g + 16], ALU.mult))
        return tk



    split_tile()
    load_tile()
    split_tile()
    load_tile()
    DV.wait(t_par)
    norm("mix_norm")
    trig()
    t_rope = tables()

    for g in range(4):
        w = 2 << g
        n, v = next_tile("pool", g)
        r = form_a(v[0], 8, H, hready)
        tile_used(n)
        for c in range(2):
            bi, bank, t = r[c]
            i0, z0, w0 = tmps.take()
            i1, z1, w1 = tmps.take()
            i2, z2, w2 = tmps.take()
            tz = AC.add(lambda e, z0=z0, bank=bank: e.activation(z0[:, 16:528], bank, ACT.Copy), t, w0)
            src, dsts = z0, [z1, z2]
            tk, k, q = tz, 1, 0
            while k < w:
                d = dsts[q % 2]
                tk = DV.add(lambda e, d=d, src=src, k=k: e.tensor_tensor(d[:, 16:528], src[:, 16:528],
                                                                         src[:, 16 - k:528 - k], ALU.add),
                            tk, w1, w2)
                src, k, q = d, 2 * k, q + 1
            tk = DV.add(lambda e, s=src, w=w: e.scalar_tensor_tensor(s[:, 16:16 + w], s[:, 16:16 + w], float(w),
                                                                     rinv[:, 0:w], ALU.mult, ALU.mult), tk)
            tk = DV.add(lambda e, s=src, w=w, z0=z0: e.scalar_tensor_tensor(s[:, 16:528], s[:, 16:528], 1.0 / w,
                                                                            z0[:, 16:528], ALU.mult, ALU.subtract), tk)
            banks.done(bi, tz)
            q = 2 * g + c
            pready[q] = pair(P, q, tk, src[:, 16:528])
            for i in (i0, i1, i2):
                tmps.done(i, *pready[q])
    n, v = next_tile("wpool", 0)
    wh, wl = v[0]
    for g in range(4):
        r = form_a((wh[:, 2 * g:2 * g + 2, :], wl[:, 2 * g:2 * g + 2, :]), 2, P, pready, base=2 * g)
        for c in range(2):
            bi, bank, t = r[c]
            q = 8 + 2 * g + c
            s = gain("pool_scale", 2 * g + c)
            h = AC.add(lambda e, q=q, bank=bank, s=s: e.activation(Ph[:, q, :], bank, ACT.Copy, scale=s), t)
            l = DV.add(lambda e, q=q, bank=bank, s=s: e.scalar_tensor_tensor(
                Pl[:, q, :], bank, s, f(Ph[:, q, :]), ALU.mult, ALU.subtract), h)
            pready[q] = [h, l]
            banks.done(bi, h, l)
    tile_used(n)
    t_pool = r[1][2]

    def gated(ta, tg, src, ready, base, finish):
        for i in range(4):
            na, va = next_tile(ta, i)
            ra = form_a(va[0], 8, src, ready, base=base)
            tile_used(na)
            ng, vg = next_tile(tg, i)
            rg = form_a(vg[0], 8, H, hready)
            tile_used(ng)
            for c in range(2):
                bg, bankg, tgk = rg[c]
                ba, banka, tak = ra[c]
                ti, tv, was = tmps.take()
                v = tv[:, 16:528]
                s = AC.add(lambda e, v=v, b=bankg: e.activation(v, b, ACT.Sigmoid), tgk, was)
                banks.done(bg, s)
                t = finish(2 * i + c, v, banka, [s, tak])
                banks.done(ba, t)
                tmps.done(ti, t)

    mt = [None] * 8

    def fin_a(c, v, bank, toks):
        mt[c] = DV.add(lambda e: e.tensor_tensor(M[:, c, :], v, bank, ALU.mult), *toks)
        return mt[c]

    gated("wa", "ga", P, pready, 8, fin_a)
    t_free8 = (PE.sem, PE.n)

    vh, vl = (W[:, 0:8, :].rearrange("p a b -> p (a b)").rearrange("p (n d) -> p n d", n=4) for W in (Ph, Pl))
    ssv = small[:, 0:16].rearrange("p (n i) -> p n i", n=4)
    vtok = []
    for i in range(4):
        n, v = next_tile("v", i)
        wh, wl = v[0]
        for half in range(2):
            bi, bank, was = banks.take()
            PE.wait(was)
            for q in range(2):
                b = 2 * half + q
                for k in range(8):
                    t = mm3(bank[:, 256 * q:256 * q + 256], Hh[:, k, 128 * b:128 * b + 128],
                            Hl[:, k, 128 * b:128 * b + 128], wh[:, k, :], wl[:, k, :], k == 0, k == 7)
            ti, tv, w0 = tmps.take()
            tj, tw, w1 = tmps.take()
            vv, ww = tv[:, 16:528], tw[:, 16:528]
            tg = AC.add(lambda e, vv=vv, bank=bank: e.activation(vv, bank, ACT.Gelu), t, w0)
            banks.done(bi, tg)
            hh = vh[:, 2 * half:2 * half + 2, 256 * i:256 * i + 256]
            ll = vl[:, 2 * half:2 * half + 2, 256 * i:256 * i + 256]
            v3 = vv.rearrange("p (q d) -> p q d", q=2)
            h = AC.add(lambda e, hh=hh, v3=v3: e.activation(hh, v3, ACT.Copy), tg, t_pool)
            l = DV.add(lambda e, ll=ll, v3=v3, hh=hh: e.tensor_tensor(ll, v3, f(hh), ALU.subtract), h)
            for q in range(2):
                s = AC.add(lambda e, q=q, i=i, half=half, vv=vv, ww=ww: e.activation(
                    ww[:, 256 * q:256 * q + 256], vv[:, 256 * q:256 * q + 256], ACT.Square,
                    accum_out=ssv[:, 2 * half + q, i:i + 1]), tg, w1)
            vtok += [h, l]
            tmps.done(ti, l, s)
            tmps.done(tj, s)
        tile_used(n)
    ssum, rv = small[:, 16:20], small[:, 24:28]
    t = DV.add(lambda e: e.tensor_reduce(ssum, ssv, AX.X, ALU.add), s)
    t_rv = rsqrt_small(rv, ssum, 1024, t)

    t_m = PO.add(lambda e: e.affine_select(out=wsp, in_=wsp, compare_op=ALU.is_ge, fill=0.0, base=0,
                                           pattern=[[0, 8], [-1, 128]], channel_multiplier=1), t_ws)
    for half in range(2):
        bi, bank, was = banks.take()
        PE.wait(was, t_m)
        for q in range(4):
            t = PE.add(lambda e, q=q, half=half, bank=bank: e.transpose(bank[:, 128 * q:128 * q + 128],
                                                                        wsp[:, 4 * half + q, :], ident[:, :]))
        t_wsT = DV.add(lambda e, half=half, bank=bank: e.tensor_copy(Z[:, 512 * half:512 * half + 512], bank), t)
        banks.done(bi, t_wsT)

    ws_free = [None]

    def ws_pair(h, t_mixed):
        ti, tv, was = tmps.take()
        tt = tv[:, 16:528]
        for q in range(4):
            ts = DV.add(lambda e: e.tensor_scalar(tt[:, 128 * q:128 * q + 128], wsp[:, h, :], rv[:, q:q + 1], None,
                                                  ALU.mult), t_wsT, t_rv, was)
        th = AC.add(lambda e: e.activation(WS[:, 0, :], tt, ACT.Copy), ts, t_mixed)
        tl = DV.add(lambda e: e.tensor_tensor(WS[:, 1, :], tt, f(WS[:, 0, :]), ALU.subtract), th, t_mixed)
        tmps.done(ti, tl)
        return [th, tl]

    def mix(h, tws, ui, uu, tu):
        bj, bk, was = banks.take()
        PE.wait(was, tws, vtok)
        for q in range(4):
            sl = slice(128 * q, 128 * q + 128)
            hc = slice(128 * h, 128 * h + 128)
            t = mm3(bk[:, sl], vh[:, q, hc], vl[:, q, hc], WS[:, 0, sl], WS[:, 1, sl], True, True)
        tm, z2, w2 = tmps.take()
        mx = z2[:, 16:528]
        bb = bsp[:, h, :].unsqueeze(1).broadcast_to([128, 4, 128])
        t1 = DV.add(lambda e: e.scalar_tensor_tensor(
            mx.rearrange("p (n t) -> p n t", n=4), bk.rearrange("p (n t) -> p n t", n=4), gain("sgu_norm", h), bb,
            ALU.mult, ALU.add), t, w2)
        banks.done(bj, t1)
        t2 = DV.add(lambda e: e.tensor_tensor(mx, mx, uu, ALU.mult), t1, tu)
        pready[8 + h] = pair(P, 8 + h, t2, mx, t_free8)
        utmps.done(ui, t2)
        tmps.done(tm, *pready[8 + h])
        return t

    utmps = tmps.part(1)
    tws = ws_pair(0, None)
    before = None
    for i in range(4):
        n, v = next_tile("u", i)
        for c in range(2):
            h = 2 * i + c
            bi, bank, t = form_a((v[0][0][:, :, 128 * c:128 * c + 128], v[0][1][:, :, 128 * c:128 * c + 128]), 8, H,
                                 hready, m=1)[0]
            if c == 1:
                tile_used(n)
            if before is not None:
                t_mix = mix(h - 1, tws, *before)
                tws = ws_pair(h, t_mix)
            ui, uv, uw = utmps.take()
            uu = uv[:, 16:528]
            tu = AC.add(lambda e: e.activation(uu, bank, ACT.Gelu), t, uw)
            banks.done(bi, tu)
            before = (ui, uu, tu)
    mix(7, tws, *before)
    tmps.join(utmps)
    bstate["t"] = [(DV.sem, DV.n), (PE.sem, PE.n), (AC.sem, AC.n)]
    t_vused = (PE.sem, PE.n)

    def fin_b(c, v, bank, toks):
        t = DV.add(lambda e: e.tensor_tensor(v, v, bank, ALU.mult), *toks)
        t2 = DV.add(lambda e: e.tensor_tensor(M[:, c, :], M[:, c, :], v, ALU.add), t, mt[c])
        pready[c] = pair(P, c, t2, M[:, c, :], t_vused)
        return t2

    gated("wb", "gb", P, pready, 8, fin_b)
    h_read()
    for i in range(4):
        n, v = next_tile("wo", i)
        r = form_a(v[0], 8, P, pready)
        tile_used(n)
        for c in range(2):
            bi, bank, t = r[c]
            banks.done(bi, add_x(2 * i + c, bank, t, 1.0))
            h_pair(2 * i + c, "ffn_norm")
            stats(2 * i + c)
    for q in range(16):
        pfree[q] = [(PE.sem, PE.n)]

    t_f = DV.add(lambda e: e.memset(M[:, 0:2, :], NEG), (PE.sem, PE.n), (AC.sem, AC.n), (DV.sem, DV.n))
    def fill(h):
        bstate["fill"] = SP.dma(cs["fill"], BS[h].rearrange("n p s -> p n s"),
                                M[:, 0:2, :].rearrange("p a b -> p (a b)").rearrange("p (n s) -> p n s", n=4), t_f)

    for h in range(16):
        extras.append(lambda h=h: fill(h))
    extras.insert(4, bias_consts)
    extras.insert(10, bias_table)
    norm_begin(RF, now())
    ffn("f", "conv", "ple_norm")
    t_RF = (DV.sem, DV.n)
    norm_begin(Z[:, 1024:1536], bstate["t"])

    pm = M[:, 4:6, :].rearrange("p a b -> p (a b)").rearrange("p (n d) -> p n d", n=4)
    t_p = SP.dma(cs["p"], pm, a["p"][0, 0].rearrange("(n p) d -> p n d", p=128), bstate["t"])
    for c in range(2):
        bi, bank, was = banks.take()
        PE.wait(was, t_p)
        for n in range(4):
            t = PE.add(lambda e, n=n, c=c, bank=bank: e.transpose(bank[:, 128 * n:128 * n + 128],
                                                                  pm[:, n, 128 * c:128 * c + 128], ident[:, :]))
        pready[c] = pair(P, c, t, bank, pfree[c])
        banks.done(bi, *pready[c])
    t_pm = (PE.sem, PE.n)
    n, v = next_tile("ple", 0)
    for c in range(8):
        r = form_a(v[0], 2, P, pready, m=1, kw=c)
        bi, bank, t = r[0]
        mt[c] = AC.add(lambda e, c=c, bank=bank: e.activation(M[:, c, :], bank, ACT.Copy), t, t_pm, t_RF, bstate["fill"])
        banks.done(bi, mt[c])
    tile_used(n)
    for q in range(16):
        pfree[q] = [(PE.sem, PE.n)]
    for i in range(4):
        extra(1)
        n, v = next_tile("pg", i)
        r = form_a(v[0], 8, H, hready, scaled=Z[:, 1024:1536])
        tile_used(n)
        for c in range(2):
            cc = 2 * i + c
            bi, bank, t = r[c]
            ti, tv, was = tmps.take()
            v_ = tv[:, 16:528]
            s = AC.add(lambda e, v=v_, b=bank: e.activation(v, b, ACT.Sigmoid), t, was)
            banks.done(bi, s)
            t1 = DV.add(lambda e, v=v_, cc=cc: e.tensor_tensor(v, v, M[:, cc, :], ALU.mult), s, mt[cc])
            t2 = DV.add(lambda e, v=v_, cc=cc: e.tensor_tensor(X[:, cc, :], X[:, cc, :], v, ALU.add), t1, xt[cc])
            xt[cc] = [t2]
            tmps.done(ti, t2)
            stats(cc)
    h_read()
    bi, bank, tr = rstd()
    for c in range(8):
        xt[c] = [DV.add(lambda e, c=c, bank=bank: e.scalar_tensor_tensor(
            X[:, c, :], X[:, c, :], gain("final_norm", c), bank, ALU.mult, ALU.mult), tr, xt[c])]
        if c == 7:
            banks.done(bi, *xt[c])
        h_pair(c, "ffn_norm1_2")
        stats(c)

    def mul3(o, x, y):
        return lambda e: e.tensor_tensor(o, x, y, ALU.mult)

    def scaled_pair(dst, rows, bank, t, scale, *was):
        h = AC.add(lambda e: e.activation(dst[0], bank, ACT.Copy, scale=scale), t, *was)
        l = DV.add(lambda e: e.scalar_tensor_tensor(dst[1], bank, scale, f(dst[0]), ALU.mult, ALU.subtract), h, *was)
        return [h, l]

    def turn(src, rows):
        bi, bank, was = banks.take()
        PE.wait(was)
        for n in range(4):
            t = PE.add(lambda e, n=n: e.transpose(bank[0:rows, 128 * n:128 * n + 128], src(n), ident[:, :]))
        return bi, bank, t

    def proj_b(W, c0, w, n_t, b0, stride, K, src=H, ring=None):
        bi, bank, was = (ring or banks).take()
        PE.wait(was)
        for q in range(n_t):
            b = b0 + q
            for k in range(K):
                PE.wait(src[2][k])
                t = mm3(bank[:, stride * q:stride * q + w], src[0][:, k, 128 * b:128 * b + 128],
                        src[1][:, k, 128 * b:128 * b + 128], W[0][:, k, c0:c0 + w], W[1][:, k, c0:c0 + w],
                        k == 0, k == K - 1)
        norm_step()
        return bi, bank, t

    def out_partial(name, src, bases, ready, free, ring, after=None):
        units = [(j, c) for j in range(4) for c in range(8)]
        held = {}

        def run(n):
            for j, c in units[:n]:
                base = bases[j % len(bases)]
                if c == 0:
                    held[j] = next_tile(name, j, 1)
                nn, v = held[j]
                bi, bank, t = form_a(v[0], 2, src, ready, base=base, m=1, kw=c, ring=ring)[0]
                ring.done(bi, add_x(c, bank, t, 1.0))
                if j == 3:
                    if after:
                        h_pair(c, *after)
                    stats(c)
                if c == 7:
                    tile_used(nn)
                    free[base - bases[0]] = [t]
                    free[base - bases[0] + 1] = [t]
            del units[:n]
        return run

    def mflat(a0, a1):
        return M[:, a0:a1, :].rearrange("p a b -> p (a b)")

    def attend_a():
        free0 = now()
        qt = mflat(0, 2).rearrange("p (n d) -> p n d", n=4)
        SS = [mflat(2, 4).rearrange("p (n s) -> p n s", n=4), mflat(4, 6).rearrange("p (n s) -> p n s", n=4)]
        kd = mflat(6, 8).rearrange("p (n g u d) -> p n g u d", n=4, g=2, u=2)
        BR = [Z[:, 0:1024].rearrange("p (n s) -> p n s", n=4), Z[:, 1024:2048].rearrange("p (n s) -> p n s", n=4)]
        vA = [W[:, 2, :].rearrange("p (n d) -> p n d", n=4) for W in P]
        QT = [(Ph[:, 3, :], Pl[:, 3, :]), (WS[:, 0, :], WS[:, 1, :]), (Ph[:, 12, :], Pl[:, 12, :]),
              (Ph[:, 13, :], Pl[:, 13, :])]
        t_neg = [PO.add(lambda e, b=b: e.memset(b[:, 0, 0:128], NEG), bstate["bw"], free0) for b in BR]
        Hs = (Hh, Hl, hready)
        AC.wait(free0)
        DV.wait(free0)

        n_, v_ = next_tile("akv", 0)
        ssk, rk = small[:, 0:8], small[:, 8:16]
        got = []
        vt = []
        for half in range(2):
            bi, bank, t = proj_b(v_[0], 0, 256, 2, 2 * half, 256, 8, Hs)
            bv = bank.rearrange("p (n g d) -> p n g d", n=2, g=4)
            ti, tv, was = tmps.take()
            sq = tv[:, 16:272].rearrange("p (n g d) -> p n g d", n=2, g=2)
            for q in range(2):
                t1 = AC.add(lambda e: e.activation(sq[:, q], bv[:, q, 0:2, :], ACT.Square,
                                                   scale=rs4[:, 2 * half + q:2 * half + q + 1]), t, was, nstate["rst"])
            t2 = DV.add(lambda e, half=half, tv=tv: e.tensor_reduce(
                ssk[:, 4 * half:4 * half + 4], tv[:, 16:272].rearrange("p (m d) -> p m d", d=64), AX.X, ALU.add), t1)
            tmps.done(ti, t2)
            b3 = bank.rearrange("p (n d) -> p n d", n=2)[:, :, 128:256]
            for q in range(2):
                n, r = 2 * half + q, rs4[:, 2 * half + q:2 * half + q + 1]
                h = AC.add(lambda e: e.activation(vA[0][:, n, :], b3[:, q, :], ACT.Copy, scale=r), t)
            for q in range(2):
                n, r = 2 * half + q, rs4[:, 2 * half + q:2 * half + q + 1]
                l = DV.add(lambda e: e.scalar_tensor_tensor(vA[1][:, n, :], b3[:, q, :], r, f(vA[0][:, n, :]),
                                                            ALU.mult, ALU.subtract), h)
            vt += [h, l]
            got.append((bi, bv, t))
        tile_used(n_)
        tr = rsqrt_small(rk, ssk, 64, t2)
        rk4 = rk.rearrange("p (n g) -> p n g", n=4)
        tr = DV.add(lambda e: e.tensor_tensor(rk4, rk4, rs4.unsqueeze(2).broadcast_to([128, 4, 2]), ALU.mult), tr)
        for half in range(2):
            bi, bv, t = got[half]
            for u in range(2):
                tk = DV.add(lambda e, half=half, u=u, bv=bv: e.tensor_tensor(
                    kd[:, 2 * half:2 * half + 2, :, u, :], bv[:, :, 0:2, :],
                    rk4[:, 2 * half:2 * half + 2, :].unsqueeze(3).broadcast_to([128, 2, 2, 64]), ALU.mult), tr)
            banks.done(bi, tk, *vt)
        KT = []
        for g in range(2):
            PE.wait(tk)
            bi, bank, t = turn(lambda n, g=g: kd[:, n, g, :, :].rearrange("p u d -> p (u d)"), 128)
            kt = (Ph[:, g, :], Pl[:, g, :])
            toks = scaled_pair(kt, 128, bank, t, gk_a)
            banks.done(bi, *toks)
            KT.append((kt, toks))

        sfree = [[], []]
        bfree = [[], []]
        pt_free = [[], []]
        heads = {}
        ssq, rq = small[:, 16:32], small[:, 32:48]
        q_t = {}
        aq = {}

        def q_unit(g, b):
            if b == 0:
                aq[g] = next_tile("aq", g, 1)
            n_, v_ = aq[g]
            bi, bank, t = proj_b(v_[0], 0, 256, 1, b, 256, 8, Hs)
            ti, tv, was = tmps.take()
            sq = tv[:, 16:272]
            t1 = AC.add(lambda e: e.activation(sq, bank[:, 0:256], ACT.Square, scale=rs4[:, b:b + 1]), t, was)
            t2 = DV.add(lambda e: e.tensor_reduce(ssq[:, 4 * b:4 * b + 4], sq.rearrange("p (m d) -> p m d", d=64),
                                                  AX.X, ALU.add), t1)
            tmps.done(ti, t2)
            t3 = AC.add(lambda e: e.activation(qt[:, b, :], bank[:, 0:256], ACT.Copy, scale=rs4[:, b:b + 1]), t,
                        bstate.get("qt_read"))
            banks.done(bi, t1, t3)
            q_t[g, b] = [t2, t3]
            if b == 3:
                tile_used(n_)

        def q_turn(g):
            tr = rsqrt_small(rq, ssq, 64, *[q_t[g, b] for b in range(4)])
            qv = qt.rearrange("p n (m d) -> p (n m) d", d=64)
            tk = DV.add(lambda e: e.tensor_tensor(qv, qv, rq.unsqueeze(2).broadcast_to([128, 16, 64]), ALU.mult), tr)
            for hp in range(2):
                PE.wait(tk)
                bi, bank, t = turn(lambda n: qt[:, n, 128 * hp:128 * hp + 128], 128)
                slot = 2 * (g % 2) + hp
                toks = scaled_pair(QT[slot], 128, bank, t, gq_a, qfree[slot])
                banks.done(bi, *toks)
                heads[2 * g + hp] = (QT[slot], toks)
            bstate["qt_read"] = t

        def load_bias(h):
            b = BR[h % 2]
            SP.dma(cs[f"bs{h % 2}"], b[:, 1:4, :], BS[h, 1:4].rearrange("n q s -> q n s"), bfree[h % 2], t_neg,
                   bstate["bw"])
            return SP.dma(cs[f"bs{h % 2}"], b[:, 0, 128:256], BS[h, 0, :, 128:256], bfree[h % 2])

        bias_t = {0: load_bias(0), 1: load_bias(1)}

        def scores(h):
            r, c = h % 2, h // 2
            qv, qtok = heads[c]
            kt, ktok = KT[h // 8]
            rows = slice(64 * r, 64 * r + 64)
            PE.wait(qtok, ktok)
            S = SS[h % 2]
            bt = bias_t[h]
            for m in range(2):
                bi, bank, was = banks.take()
                PE.wait(was)
                for n in (2 * m, 2 * m + 1):
                    o = 256 * (n % 2)
                    ql = [x[rows, 128 * n:128 * n + 128] for x in qv]
                    if n == 0:
                        for z in range(2):
                            t = mm3(bank[:, 128 * z:128 * z + 128], ql[0], ql[1], kt[0][rows, 0:128],
                                    kt[1][rows, 0:128], True, True)
                    else:
                        ks = slice(128 * (n - 1), 128 * (n + 1))
                        t = mm3(bank[:, o:o + 256], ql[0], ql[1], kt[0][rows, ks], kt[1][rows, ks], True, True)
                t1 = DV.add(lambda e: e.scalar_tensor_tensor(
                    S[:, 2 * m:2 * m + 2, :], bank.rearrange("p (n s) -> p n s", n=2), 0.125,
                    BR[h % 2][:, 2 * m:2 * m + 2, :], ALU.mult, ALU.add), t, bt, sfree[h % 2], t_neg)
                banks.done(bi, t1)
            bfree[h % 2] = [t1]
            if r == 1:
                qfree[c % 4] = [t]
            if h + 2 < 16:
                bias_t[h + 2] = load_bias(h + 2)
            x = 16 * (h % 3)
            mx, nm, sm_, es = (small[:, 48 + x + 4 * i:52 + x + 4 * i] for i in range(4))
            t2 = DV.add(lambda e: e.tensor_reduce(mx, S, AX.X, ALU.max), t1)
            t3 = DV.add(lambda e: e.tensor_scalar(nm, mx, sinkc[:, h:h + 1], -1.0, ALU.max, ALU.mult), t2)
            for n in range(4):
                t4 = AC.add(lambda e: e.activation(S[:, n, :], S[:, n, :], ACT.Exp, bias=nm[:, n:n + 1],
                                                   accum_out=sm_[:, n:n + 1]), t3)
            return AC.add(lambda e: e.activation(es, nm, ACT.Exp, bias=sinkc[:, h:h + 1]), t4)

        def turns(h, te):
            S = SS[h % 2]
            slot = 4 + 2 * (h % 2)
            toks = []
            for m in range(2):
                bi, bank, was = banks.take()
                PE.wait(was, te)
                for i in range(4):
                    b = 4 * m + i
                    t = PE.add(lambda e: e.transpose(bank[:, 128 * i:128 * i + 128],
                                                     S[:, b // 2, 128 * (b % 2):128 * (b % 2) + 128], ident[:, :]))
                pr = pair(P, slot + m, t, bank, pt_free[h % 2])
                banks.done(bi, *pr)
                toks += pr
            sfree[h % 2] = [t]
            return toks

        oslot = {}

        def values(h, toks):
            slot = 4 + 2 * (h % 2)
            kv = h // 8
            bi, bank, was = banks.take()
            PE.wait(was, toks, vt)
            for n in range(4):
                js = [j for j in (n - 1, n) if j >= 0]
                for j in js:
                    b = 2 * n + (j - n + 1)
                    c, o = slot + b // 4, 128 * (b % 4)
                    t = mm3(bank[:, 64 * n:64 * n + 64], Ph[:, c, o:o + 128], Pl[:, c, o:o + 128],
                            vA[0][:, j, 64 * kv:64 * kv + 64], vA[1][:, j, 64 * kv:64 * kv + 64],
                            j == js[0], j == n)
            pt_free[h % 2] = [t]
            x = 16 * (h % 3)
            sm_, es = small[:, 56 + x:60 + x], small[:, 60 + x:64 + x]
            t1 = DV.add(lambda e: e.tensor_tensor(sm_, sm_, es, ALU.add), toks)
            t1 = DV.add(lambda e: e.reciprocal(sm_, sm_), t1)
            if h % 2 == 0:
                oslot[h // 2] = otmps.take()
            oi, ov, ow = oslot[h // 2]
            ot = ov[:, 16:528].rearrange("p (n d) -> p n d", n=4)
            r = 64 * (h % 2)
            t2 = DV.add(lambda e: e.tensor_tensor(ot[:, :, r:r + 64],
                                                  bank[:, 0:256].rearrange("p (n d) -> p n d", n=4),
                                                  sm_.unsqueeze(2).broadcast_to([128, 4, 64]), ALU.mult), t1, t, ow)
            banks.done(bi, t2)
            if h % 2:
                c = h // 2
                PE.wait(t2)
                bi, bank, t = turn(lambda n: ot[:, n, :], 128)
                otmps.done(oi, t)
                q = 8 + c % 4
                pready[q] = pair(P, q, t, bank, ofree[c % 4])
                banks.done(bi, *pready[q])

        qfree = [[] for _ in range(4)]
        ofree = [[] for _ in range(4)]
        otmps = tmps.part(1)
        for b in range(4):
            q_unit(0, b)
        q_turn(0)
        exps, pts = {}, {}
        out_units = out_partial("ao", P, [8, 10], pready, ofree, banks, ("ffn_norm2_2", 0))
        for i in range(16 + 2):
            g = i // 4
            if i == 12:
                h_read()
            if i < 16:
                exps[i] = scores(i)
            if g < 3:
                q_unit(g + 1, i % 4)
            if i >= 6:
                out_units(2)
            if 1 <= i <= 16:
                pts[i - 1] = turns(i - 1, exps[i - 1])
            if i >= 2:
                values(i - 2, pts[i - 2])
            if g < 3 and i % 4 == 3:
                q_turn(g + 1)
        out_units(32)
        tmps.join(otmps)
        for q in range(16):
            pfree[q] = now()

    def attend_b():
        free0 = now()
        AC.wait(free0)
        DV.wait(free0)
        PO.wait(free0)
        Hs = (Hh, Hl, hready)
        cq = mflat(0, 2).rearrange("p (n d) -> p n d", n=4)
        ck = mflat(2, 3).rearrange("p (n d) -> p n d", n=4)
        kr = krt[:, :].rearrange("p (n d) -> p n d", n=4)
        ssq, ssc = small[:, 0:4], small[:, 4:8]
        rq, rc = small[:, 8:12], small[:, 12:16]
        nq, vq = next_tile("bq", 0)
        got, gok = [], []
        for half in range(2):
            bi, bank, t = proj_b(vq[0], 0, 256, 2, 2 * half, 256, 8, Hs)
            ti, tv, was = tmps.take()
            for q in range(2):
                t1 = AC.add(lambda e, q=q, half=half, tv=tv, bank=bank: e.activation(
                    tv[:, 16 + 256 * q:272 + 256 * q], bank[:, 256 * q:256 * q + 256], ACT.Square,
                    scale=rs4[:, 2 * half + q:2 * half + q + 1],
                    accum_out=ssq[:, 2 * half + q:2 * half + q + 1]), t, was, nstate["rst"])
            tmps.done(ti, t1)
            got.append((bi, bank, t))
        t_q = t1
        tile_used(nq)
        nk, vk = next_tile("bkv", 0)
        for half in range(2):
            bi, bank, t = proj_b(vk[0], 0, 160, 2, 2 * half, 160, 8, Hs)
            ti, tv, was = tmps.take()
            for q in range(2):
                AC.add(lambda e, q=q, half=half, tv=tv, bank=bank: e.activation(
                    tv[:, 16 + 160 * q:144 + 160 * q], bank[:, 160 * q:160 * q + 128], ACT.Square,
                    scale=rs4[:, 2 * half + q:2 * half + q + 1],
                    accum_out=ssc[:, 2 * half + q:2 * half + q + 1]), t, was)
                AC.add(lambda e, q=q, half=half, tv=tv, bank=bank: e.activation(
                    tv[:, 144 + 160 * q:176 + 160 * q], bank[:, 160 * q + 128:160 * q + 160], ACT.Square,
                    scale=rs4[:, 2 * half + q:2 * half + q + 1],
                    accum_out=kr2[:, 2 * half + q:2 * half + q + 1]))
                t1 = AC.add(lambda e, q=q, half=half, bank=bank: e.activation(
                    kr[:, 2 * half + q, :], bank[:, 160 * q + 128:160 * q + 160], ACT.Copy,
                    scale=rs4[:, 2 * half + q:2 * half + q + 1]))
            tmps.done(ti, t1)
            gok.append((bi, bank, t))
        tile_used(nk)
        t_kr = t1
        ta = rsqrt_small(rq, ssq, 256, t_q)
        tb = rsqrt_small(rc, ssc, 128, t1)
        ta = DV.add(mul3(rq, rq, rs4), ta)
        tb = DV.add(mul3(rc, rc, rs4), tb)
        for half in range(2):
            for (bi, bank, t), w, wd, dst, r in ((got[half], 256, 256, cq, rq), (gok[half], 160, 128, ck, rc)):
                for q in range(2):
                    n = 2 * half + q
                    tk = DV.add(lambda e, q=q, n=n, w=w, wd=wd, dst=dst, r=r, bank=bank: e.tensor_scalar(
                        dst[:, n, :], bank[:, w * q:w * q + wd], r[:, n:n + 1], None, ALU.mult), ta, tb)
                banks.done(bi, tk, t_kr)
        PE.wait(tk)
        t_cn = tk
        cready = []
        for c in range(3):
            srcv = (lambda n, c=c: cq[:, n, 128 * c:128 * c + 128]) if c < 2 else (lambda n: ck[:, n, :])
            bi, bank, t = turn(srcv, 128)
            s = gain("b_q_norm_2", c) if c < 2 else gain("b_kv_norm_2", 0)
            toks = scaled_pair((Ph[:, c, :], Pl[:, c, :]), 128, bank, t, s)
            banks.done(bi, *toks)
            cready.append(toks)
        t_c = t
        Cq = (Ph, Pl, cready)
        Ck = (Ph[:, 2:3, :], Pl[:, 2:3, :], cready[2:3])

        qts = [x.rearrange("p (n h d) -> p n h d", n=4, h=2) for x in (mflat(0, 3)[:, 0:768], mflat(0, 3)[:, 768:1536])]
        kts = [x.rearrange("p (n h d) -> p n h d", n=4, h=2) for x in (mflat(3, 6)[:, 0:768], mflat(3, 6)[:, 768:1536])]
        ots = [M[:, 6 + i, :].rearrange("p (n d) -> p n d", n=4) for i in range(2)]
        vBs = [[W[:, 3 + i, :].rearrange("p (n h d) -> p n h d", n=4, h=2) for W in P] for i in range(2)]
        QK = [((Ph[:, 5, :], Pl[:, 5, :]), (Ph[:, 6, :], Pl[:, 6, :])),
              ((Ph[:, 7, :], Pl[:, 7, :]), (Ph[:, 8, :], Pl[:, 8, :]))]
        ER = Ring([Z[:, 512 * i:512 * i + 512] for i in range(4)])
        PT = Ring([9, 10, 11, 12])
        sc = 96 ** -0.5
        qkfree = [[], []]
        tread, vread, oread = [[t_c], [t_c]], [[], []], [[], []]
        bg = {}
        qkv_t = {}

        def prep_unit(g, u):
            if u == 0 and g % 2 == 0:
                bg[g // 2] = next_tile("bg", g // 2, 1)
            n_, v_ = bg[g // 2]
            x, half = g % 2, u % 2
            ss = small[:, 16 * x + 8 * (u // 2) + 4 * half:16 * x + 8 * (u // 2) + 4 * half + 4]
            ti, tv, was = tmps.take()
            tb = slice(2 * half, 2 * half + 2)
            if u < 2:
                bi, bank, t = proj_b(v_[0], 192 * x, 192, 2, 2 * half, 256, 2, Cq, banks2)
                src = bank.rearrange("p (n d) -> p n d", n=2)[:, :, 0:192]
                sq = tv[:, 16:400]
                t1 = AC.add(lambda e: e.activation(sq.rearrange("p (n d) -> p n d", n=2), src, ACT.Square), t, was)
                t2 = DV.add(lambda e: e.tensor_reduce(ss, sq.rearrange("p (m d) -> p m d", m=4), AX.X, ALU.add), t1,
                            rdone.get(g - 2))
                t3 = AC.add(lambda e: e.activation(qts[x][:, tb, :, :].rearrange("p n h d -> p n (h d)"), src,
                                                   ACT.Copy), t, tread[x])
                banks2.done(bi, t1, t3)
            else:
                bi, bank, t = proj_b(v_[1], 256 * x, 256, 2, 2 * half, 256, 1, Ck, banks2)
                bv = bank.rearrange("p (m d) -> p m d", m=4)
                sq = tv[:, 16:272].rearrange("p (m d) -> p m d", m=4)
                t1 = AC.add(lambda e: e.activation(sq, bv[:, :, 0:64], ACT.Square), t, was)
                t2 = DV.add(lambda e: e.tensor_reduce(ss, sq, AX.X, ALU.add), t1, rdone.get(g - 2))
                b4 = bank.rearrange("p (n h d) -> p n h d", n=2, h=2)
                t3 = AC.add(lambda e: e.activation(kts[x][:, tb, :, 0:64], b4[:, :, :, 0:64], ACT.Copy), t, tread[x])
                vh_, vl_ = vBs[x][0][:, tb, :, :], vBs[x][1][:, tb, :, :]
                h = AC.add(lambda e: e.activation(vh_, b4[:, :, :, 64:128], ACT.Copy), t, vread[x])
                l = DV.add(lambda e: e.tensor_tensor(vl_, b4[:, :, :, 64:128], f(vh_), ALU.subtract), h, vread[x])
                banks2.done(bi, t1, t3, h, l)
                qkv_t[g, 4 + half] = [h, l]
            tmps.done(ti, t2)
            qkv_t[g, u] = [t2, t3]
            if u == 3 and g % 2 == 1:
                tile_used(n_)

        rdone = {-2: t_cn, -1: t_cn}

        def prep_end(g):
            x = g % 2
            qt, kt = qts[x], kts[x]
            ss, r = small[:, 16 * x:16 * x + 16], small[:, 32 + 16 * x:48 + 16 * x]
            wait = [qkv_t[g, u] for u in range(4)]
            t = DV.add(lambda e: e.tensor_tensor(ss[:, 8:16].rearrange("p (n h) -> p n h", n=4),
                                                 ss[:, 8:16].rearrange("p (n h) -> p n h", n=4),
                                                 kr2.unsqueeze(2).broadcast_to([128, 4, 2]), ALU.add), wait)
            tr = rsqrt_small(r, ss, 96, t, tread[x])
            rdone[g] = tr
            rq, rk = r[:, 0:8], r[:, 8:16]
            qf = qt.rearrange("p n h d -> p (n h) d")
            kf = kt.rearrange("p n h d -> p (n h) d")
            tq = DV.add(lambda e: e.tensor_tensor(qf, qf, rq.unsqueeze(2).broadcast_to([128, 8, 96]), ALU.mult), tr)
            PO.add(lambda e: e.tensor_tensor(kt[:, :, :, 64:96], kr.unsqueeze(2).broadcast_to([128, 4, 2, 32]),
                                             rk.rearrange("p (n h) -> p n h", n=4).unsqueeze(3)
                                             .broadcast_to([128, 4, 2, 32]), ALU.mult), tr, t_kr, tread[x])
            tk = PO.add(lambda e: e.tensor_tensor(kf[:, :, 0:64], kf[:, :, 0:64],
                                                  rk.unsqueeze(2).broadcast_to([128, 8, 64]), ALU.mult), tr)
            done = []
            for E, tens, base, t0, tmp in ((DV, qt, 0, tq, rt[0]), (PO, kt, 4, tk, rt[1])):
                tmp = [tmp[:, 128 * i:128 * i + 128].rearrange("p (n h d) -> p n h d", n=4, h=2) for i in range(4)]
                a1, a2 = tens[:, :, :, 64:80], tens[:, :, :, 80:96]
                tab = [ropt[:, base + j, :].rearrange("p (n d) -> p n d", n=4).unsqueeze(2)
                       .broadcast_to([128, 4, 2, 16]) for j in range(4)]
                for o, i, j in ((0, a1, 0), (1, a2, 1), (2, a2, 2), (3, a1, 3)):
                    t = E.add(mul3(tmp[o], i, tab[j]), t0, t_rope, rtfree[base // 4])
                E.add(lambda e: e.tensor_tensor(a1, tmp[0], tmp[1], ALU.subtract), t)
                t = E.add(lambda e: e.tensor_tensor(a2, tmp[2], tmp[3], ALU.add), t)
                rtfree[base // 4] = t
                done.append(t)
            return done

        rtfree = [free0, free0]
        rtm = tmps.part(2)
        rt = [v[:, 16:528] for v in rtm.views]

        def head_qk(h, done):
            x, hl, s = (h // 2) % 2, h % 2, h % 2
            PE.wait(done)
            res = []
            for src, dst, gcol in ((qts[x], QK[s][0], gq_b), (kts[x], QK[s][1], gk_b)):
                bi, bank, t = turn(lambda n: src[:, n, hl, :], 96)
                toks = scaled_pair([d[0:96, :] for d in dst], 96, bank[0:96, :], t, gcol[0:96, :], qkfree[s], t_g1)
                banks.done(bi, *toks)
                res += toks
            if hl == 1:
                tread[x] = [t]
            return res

        def scores(h, n, ready):
            s = h % 2
            (qh, ql), (kh, kl) = QK[s]
            L = 128 * (n + 1)
            bi, bank, was = banks.take()
            PE.wait(was, ready)
            qs = slice(128 * n, 128 * n + 128)
            PE.add(lambda e: e.matmul(bank[:, 0:L], ql[0:96, qs], kh[0:96, 0:L], start=True, stop=False), signal=False)
            PE.add(lambda e: e.matmul(bank[:, 0:L], qh[0:96, qs], kl[0:96, 0:L], start=False, stop=False),
                   signal=False)
            PE.add(lambda e: e.matmul(bank[:, 0:L], qh[0:96, qs], kh[0:96, 0:L], start=False, stop=False),
                   signal=False)
            t = PE.add(lambda e: e.matmul(bank[:, 128 * n:L], identb[:, :], maskb[:, :], start=False, stop=True))
            if n == 3:
                qkfree[s] = [t]
            x = (h % 4) * 4 + n
            mx = mneg[:, x:x + 1]
            nm = mneg[:, 16 + x:17 + x]
            t1 = DV.add(lambda e: e.tensor_reduce(mx, bank[:, 0:L], AX.X, ALU.max), t)
            t1 = DV.add(lambda e: e.tensor_scalar(nm, mx, -sc, None, ALU.mult), t1)
            ei, E, w = ER.take()
            y = (h % 8) * 4 + n
            t2 = AC.add(lambda e: e.activation(E[:, 0:L], bank[:, 0:L], ACT.Exp, bias=nm, scale=sc,
                                               accum_out=sums[:, y:y + 1]), t1, w)
            banks.done(bi, t2)
            return ei, E, t2

        def turns(n, ei, E, te):
            L = 128 * (n + 1)
            bi, bank, was = banks.take()
            PE.wait(was, te)
            for j in range(n + 1):
                t = PE.add(lambda e: e.transpose(bank[:, 128 * j:128 * j + 128], E[:, 128 * j:128 * j + 128],
                                                 ident[:, :]))
            ER.done(ei, t)
            pi, slot, w = PT.take()
            hh = AC.add(lambda e: e.activation(Ph[:, slot, 0:L], bank[:, 0:L], ACT.Copy), t, w)
            ll = DV.add(lambda e: e.tensor_tensor(Pl[:, slot, 0:L], bank[:, 0:L], f(Ph[:, slot, 0:L]), ALU.subtract),
                        hh, w)
            banks.done(bi, hh, ll)
            return pi, slot, [hh, ll]

        obank = {}

        def values(h, n, pi, slot, toks, vts):
            x, hl = (h // 2) % 2, h % 2
            if n == 0:
                obank[h] = obanks.take()
            bi, bank, was = obank[h]
            PE.wait(was, toks, vts)
            for j in range(n + 1):
                sl = slice(128 * j, 128 * j + 128)
                t = mm3(bank[:, 64 * n:64 * n + 64], Ph[:, slot, sl], Pl[:, slot, sl], vBs[x][0][:, j, hl, :],
                        vBs[x][1][:, j, hl, :], j == 0, j == n)
            PT.done(pi, t)
            if n < 3:
                return
            y = (h % 8) * 4
            t1 = DV.add(lambda e: e.reciprocal(sums[:, y:y + 4], sums[:, y:y + 4]), toks)
            t2 = DV.add(lambda e: e.tensor_tensor(ots[x][:, :, 64 * hl:64 * hl + 64],
                                                  bank[:, 0:256].rearrange("p (n d) -> p n d", n=4),
                                                  sums[:, y:y + 4].unsqueeze(2).broadcast_to([128, 4, 64]),
                                                  ALU.mult), t1, t, oread[x])
            obanks.done(bi, t2)
            if hl == 1:
                vread[x] = [t]
                c = h // 2
                PE.wait(t2)
                bi, bank, t = turn(lambda n: ots[x][:, n, :], 128)
                oread[x] = [t]
                oready[c] = pair(H, c, t, bank)
                banks.done(bi, *oready[c])

        obanks = banks.part(1)
        banks2 = banks.part(2)

        def units(g):
            yield lambda: prep_unit(g, 0)
            yield lambda: prep_unit(g, 1)
            yield lambda: prep_unit(g, 2)
            yield lambda: prep_unit(g, 3)
            yield lambda: ready.update({g: prep_end(g)})

        ready = {}
        out_units = out_partial("bo", H, [0, 2, 4, 6], oready, [[] for _ in range(8)], banks2)
        for u in units(0):
            u()
        items = [(h, n) for h in range(16) for n in range(4)]
        sco, tur, qk = {}, {}, {0: head_qk(0, ready[0])}
        LT, LV = 2, 4
        STEPS = (1, 1, 0, 0, 1, 2, 0, 0)
        queue = []
        for i in range(len(items) + LV):
            if i < len(items):
                h, n = items[i]
                if n == 0 and h % 2 == 0 and h // 2 < 7:
                    queue = list(units(h // 2 + 1))
                sco[i] = scores(h, n, qk[h])
                for _ in range(STEPS[i % 8]):
                    if queue:
                        queue.pop(0)()
                if n == 2 and h % 2 == 0:
                    qk[h + 1] = head_qk(h + 1, ready[h // 2])
                if n == 3 and h % 2 == 1 and h < 15:
                    qk[h + 1] = head_qk(h + 1, ready[h // 2 + 1])
            if i >= 16 + LV + 1 and (i - LV) % 2 == 0:
                out_units(1)
            if i >= LT and i - LT < len(items):
                tur[i - LT] = turns(items[i - LT][1], *sco.pop(i - LT))
            if i >= LV:
                h, n = items[i - LV]
                g = h // 2
                values(h, n, *tur.pop(i - LV), [qkv_t[g, 4], qkv_t[g, 5]])
        out_units(32)
        banks.join(banks2)
        banks.join(obanks)
        tmps.join(rtm)
        for q in range(16):
            pfree[q] = now()

    oready = [[] for _ in range(8)]

    bstate["mfree"] = now()
    bstate["t"] = now()
    plan_bias()
    norm_begin(RF, now())
    ffn("s0", "glu", "mix_norm_2", 0)
    while extras:
        extra(1)
    norm_begin_rows()
    attend_a()
    norm_begin(RF, now())
    ffn("s1", "glu", "ffn_norm1_2", 8)
    norm_begin(RF, now())
    ffn("s2", "glu", "mix_norm_2", 8)
    norm_begin_rows()
    attend_b()
    h_read()
    for c in range(8):
        h_pair(c, "ffn_norm2_2", 8)
    norm_begin(RF, now())
    ffn("s3", "glu")

    om = M[:, :, :].rearrange("p a b -> p (a b)").rearrange("p (n d) -> p n d", n=4)
    t_free = [(AC.sem, AC.n), (PE.sem, PE.n), (DV.sem, DV.n)]
    for n in range(4):
        for half in range(2):
            bi, bank, was = banks.take()
            PE.wait(was)
            for q in range(4):
                c = 4 * half + q
                t = PE.add(lambda e, n=n, c=c, q=q, bank=bank: e.transpose(
                    bank[:, 128 * q:128 * q + 128], X[:, c, 128 * n:128 * n + 128], ident[:, :]), xt[c])
            eng, put = ((DV, lambda e, o, b: e.tensor_copy(o, b)),
                        (AC, lambda e, o, b: e.activation(o, b, ACT.Copy)))[half]
            t1 = eng.add(lambda e, n=n, half=half, bank=bank, put=put: put(e, om[:, n, 512 * half:512 * half + 512],
                                                                           bank), t, t_free)
            banks.done(bi, t1)
            t_out = SP.dma(cs["out"], out[0, 128 * n:128 * n + 128, 512 * half:512 * half + 512],
                           om[:, n, 512 * half:512 * half + 512], t1)
    SP.wait(t_out, bstate["bw"], bstate.get("fill"), bstate["pos"])


INS = ['x', 'p', 'mix_norm', 'w_in', 'w_pool', 'pool_scale', 'sgu_norm', 'w_spatial', 'b_spatial', 'w_branch_a',
       'w_branch_b', 'w_out', 'ffn_norm', 'w_up', 'conv_w', 'conv_b', 'w_down', 'ple_norm', 'w_ple_gate', 'w_ple',
       'final_norm', 'positions_2', 'rel_bias_2', 'ffn_norm1_2', 'ffn1_wg_2', 'ffn1_wu_2', 'ffn1_wd_2', 'mix_norm_2',
       'ffn_norm2_2', 'ffn2_wg_2', 'ffn2_wu_2', 'ffn2_wd_2', 'a_w_in_2', 'a_q_gain_2', 'a_k_gain_2', 'a_sinks_2',
       'a_w_out_2', 'b_w_in_2', 'b_q_norm_2', 'b_kv_norm_2', 'b_w_uq_2', 'b_w_ukv_2', 'b_q_gain_2', 'b_k_gain_2',
       'b_w_out_2']


def kernel(**inputs):
    import numpy as _np
    import concourse.bacc as _bacc
    from concourse import mybir as _mybir
    from concourse.bass_utils import run_bass_kernel_spmd as _run

    nc = _bacc.Bacc("TRN2", target_bir_lowering=False, num_devices=1, dynamic_dma_scratch_size=1024)
    arrays, args = {}, {}
    for name in INS:
        v = _np.ascontiguousarray(inputs[name])
        arrays[f"in_{name}"] = v
        args[name] = nc.dram_tensor(f"in_{name}", v.shape, _mybir.dt.from_np(v.dtype), kind="ExternalInput").ap()
    out = nc.dram_tensor("out_0", (1, T, D), F32, kind="ExternalOutput").ap()
    program(nc, args, out)
    r = _run(nc, [arrays], core_ids=[0])
    return r.results[0]["out_0"]
```

```python
import math
from contextlib import ExitStack

import numpy as np
import concourse.bass as bass
from concourse import mybir

F32 = mybir.dt.float32
F32R = mybir.dt.float32r
BF16 = mybir.dt.bfloat16
I32 = mybir.dt.int32
ALU = mybir.AluOpType
ACT = mybir.ActivationFunctionType
AX = mybir.AxisListType

T, D, DFF = 512, 1024, 2816
EPS = 1e-6
NEG = -1e30
AH, BH = 16, 16
ROPE_HALF = 16
LOWEST = -3.0e38


def bucket_bounds():
    def bucket(n):
        if n < 16:
            return n
        return min(31, 16 + int(math.log(n / 16) / math.log(8) * 16))
    return [min(n for n in range(200) if bucket(n) >= k) for k in range(1, 32)]


class Queue:

    def __init__(self, engine, sem):
        self.e, self.sem, self.n, self.seen = engine, sem, 0, {}

    def wait(self, *after):
        for tok in after:
            if tok is None:
                continue
            if isinstance(tok, list):
                self.wait(*tok)
                continue
            sem, v = tok
            if self.seen.get(sem.name, 0) < v:
                self.seen[sem.name] = v
                self.e.wait_ge(sem, v)

    def add(self, fn, *after, signal=True):
        self.wait(*after)
        ins = fn(self.e)
        if not signal:
            return None
        self.n += 1
        ins.then_inc(self.sem, 1)
        return (self.sem, self.n)

    def dma(self, sem, out, in_, *after):
        self.wait(*after)
        sem[1] += 16
        self.e.dma_start(out, in_).then_inc(sem[0], 16)
        return (sem[0], sem[1])


class Ring:

    def __init__(self, views):
        self.views, self.free, self.i = views, [[] for _ in views], -1

    def take(self):
        self.i = (self.i + 1) % len(self.views)
        assert self.free[self.i] is not None
        was, self.free[self.i] = self.free[self.i], None
        return self.i, self.views[self.i], was

    def part(self, k):
        other = Ring(self.views[-k:])
        other.free = self.free[-k:]
        self.views, self.free, self.i = self.views[:-k], self.free[:-k], -1
        return other

    def join(self, other):
        self.views, self.free = self.views + other.views, self.free + other.free

    def done(self, i, *toks):
        self.free[i] = (self.free[i] or []) + [t for t in toks if t is not None]


def program(nc, a, out):
    ctx = ExitStack()
    with ctx:
        build(nc, a, out, ctx)


def build(nc, a, out, ctx):
    def sb(name, shape, dt=F32):
        return ctx.enter_context(nc.sbuf_tensor(name, shape, dt))

    def sem(name):
        return ctx.enter_context(nc.semaphore(name))

    ctx.enter_context(nc.allow_non_contiguous_dma(reason="a few short columns"))
    PE, AC, DV, PO, SP = (Queue(e, sem(n)) for e, n in ((nc.tensor, "s_pe"), (nc.scalar, "s_act"), (nc.vector, "s_dve"),
                                                        (nc.gpsimd, "s_pool"), (nc.sync, "s_sp")))

    X = sb("X", [128, 8, T])
    Hh, Hl = sb("Hh", [128, 8, T], F32R), sb("Hl", [128, 8, T], F32R)
    Ph, Pl = sb("Ph", [128, 16, T], F32R), sb("Pl", [128, 16, T], F32R)
    M = sb("M", [128, 8, T])
    RAW = sb("RAW", [128, 2, 2048])
    Wh, Wl = sb("Wh", [128, 3, 2048], F32R), sb("Wl", [128, 3, 2048], F32R)
    NT = 4
    TMP = sb("TMP", [128, NT, 528])
    Z = sb("Z", [128, 2048])
    WS = sb("WS", [128, 2, T], F32R)
    ident, ones = sb("ident", [128, 128]), sb("ones", [128, 128])
    identb, maskb = sb("identb", [128, 128], BF16), sb("maskb", [128, 128], BF16)
    P0, P1, P2 = sb("P0", [128, 99]), sb("P1", [128, 88]), sb("P2", [128, 88])
    rb2 = sb("rb2", [128, 48])
    drb3 = sb("drb3", [128, 48], BF16)
    pki = sb("pki", [128, 384], I32)
    pkf = sb("pkf", [128, 384])
    krt = sb("krt", [128, 128])
    rope = M[:, 5, :].rearrange("p (a b) -> p a b", a=8)
    sm = sb("sm", [128, 320])
    ropt = sb("ropt", [128, 8, 64])
    smi = sb("smi", [128, 4], I32)

    BANK = [ctx.enter_context(nc.psum_tensor(f"bank{i}", [128, 512], F32)) for i in range(8)]
    banks = Ring([b[:, :] for b in BANK])

    eps = sm[:, 0:1]
    posf = sm[:, 1:5]
    gq_a, gk_a, gq_b, gk_b = sm[:, 5:6], sm[:, 6:7], sm[:, 7:8], sm[:, 8:9]
    rinv = sm[:, 16:32]
    sinkc = sm[:, 32:48]
    invf = sm[:, 48:64]
    grow_q, grow_k = sm[:, 64:96], sm[:, 96:128]
    st4, rs4 = sm[:, 128:132], sm[:, 132:136]
    kr2 = sm[:, 136:140]
    lo = sm[:, 9:10]
    mneg, sums, small = sm[:, 160:192], sm[:, 192:224], sm[:, 224:320]

    cs = {n: [sem("d_" + n), 0] for n in ("x", "x2", "par", "par1", "par2", "sm", "pos", "pos2", "rb", "ws", "p", "fill",
                                         "bw", "out", "bs0", "bs1", "pscr")}
    raws = [[sem(f"d_raw{i}"), 0] for i in range(2)]

    BS = nc.dram_tensor("bias_scratch", (16, 4, 128, 256), F32, kind="Internal").ap()
    PS = nc.dram_tensor("pos_scratch", (T + 128,), I32, kind="Internal").ap()

    def f(ap):
        return ap.bitcast(F32)

    def consts():
        z = PO.add(lambda e: e.memset(ident[:, :], 0.0))
        o = PO.add(lambda e: e.memset(ones[:, :], 1.0))
        PO.add(lambda e: e.memset(eps, EPS))
        PO.add(lambda e: e.memset(gq_b, 1.0))
        PO.add(lambda e: e.memset(gk_b, 1.0))
        tid = PO.add(lambda e: e.affine_select(out=ident[:, :], in_=ident[:, :], compare_op=ALU.not_equal, fill=1.0,
                                               base=0, pattern=[[-1, 128]], channel_multiplier=1), z)
        b0 = PO.add(lambda e: e.memset(identb[:, :], 0.0))
        PO.add(lambda e: e.affine_select(out=identb[:, :], in_=identb[:, :], compare_op=ALU.not_equal, fill=1.0,
                                         base=0, pattern=[[-1, 128]], channel_multiplier=1), b0)
        b1 = PO.add(lambda e: e.memset(maskb[:, :], 0.0))
        tmb = PO.add(lambda e: e.affine_select(out=maskb[:, :], in_=maskb[:, :], compare_op=ALU.is_ge, fill=NEG,
                                               base=0, pattern=[[-1, 128]], channel_multiplier=1), b1)
        for t in range(16):
            PO.add(lambda e, t=t: e.memset(rinv[:, t:t + 1], float(np.float32(1.0) / np.float32(t + 1))))
            PO.add(lambda e, t=t: e.memset(invf[:, t:t + 1],
                                           float(np.float32(10000.0) ** np.float32(-2.0 * t / 32))))
        tc = PO.add(lambda e: e.memset(TMP[:, :, 0:16], 0.0))
        return tc

    t_const = consts()

    PARS = [("mix_norm", 8), ("pool_scale", 8), ("sgu_norm", 8), ("ffn_norm", 8), ("ple_norm", 8), ("final_norm", 8),
            ("ffn_norm1_2", 16), ("mix_norm_2", 16), ("ffn_norm2_2", 16), ("b_q_norm_2", 2), ("b_kv_norm_2", 1)]
    col = {}
    stage = M[:, 7, :]

    def flat(ap):
        n = len(ap.shape)
        if n == 1:
            return ap
        names = "abcd"[:n]
        return ap.rearrange(" ".join(names) + " -> (" + " ".join(names) + ")")

    def parameters():
        r = 0
        tok = None
        for name, n in PARS:
            col[name] = r
            tok = SP.dma(cs["par"], stage[r:r + n, 0:128], flat(a[name]).rearrange("(c p) -> c p", p=128))
            r += n
        cb = flat(a["conv_b"]).rearrange("(c p) -> c p", p=128)
        cw = a["conv_w"][0].rearrange("k (c p) -> (k c) p", p=128)
        SP.dma(cs["par"], stage[0:44, 128:256], cb)
        SP.dma(cs["par"], stage[44:88, 128:256], cw[0:44, :])
        tok = SP.dma(cs["par"], stage[0:88, 256:384], cw[44:132, :])
        bi, bank, was = banks.take()
        PE.wait(was, t_const, tok)
        for i, (n, d) in enumerate(((99, P0), (88, P1), (88, P2))):
            tk = PE.add(lambda e, i=i, n=n: e.transpose(bank[:, 128 * i:128 * i + n], stage[0:n, 128 * i:128 * i + 128],
                                                        ident[0:n, 0:n]))
        for i, (n, d) in enumerate(((99, P0), (88, P1), (88, P2))):
            t = DV.add(lambda e, i=i, n=n, d=d: e.tensor_copy(d[:, :], bank[:, 128 * i:128 * i + n]), tk)
        banks.done(bi, t)
        return t

    def gain(name, c, base=0):
        return P0[:, col[name] + base + c:col[name] + base + c + 1]

    def convp(k, c):
        r = 44 * (k + 1) + c
        return P1[:, r:r + 1] if r < 88 else P2[:, r - 88:r - 87]

    tiles = []

    def square(src, k, c0, w=256):
        return [(0, k, w, src[:, c0:c0 + w])]

    def rows4(src, i):
        return [(0, 2, 1024, src[256 * i:256 * i + 256, :])]

    def plan():
        win = a["w_in"][0]
        for i in range(4):
            tiles.append(("pool", i, square(win, 8, 256 * i)))
        tiles.append(("ga", 0, square(win, 8, 3072)))
        tiles.append(("wpool", 0, [(0, 8, 256, a["w_pool"][0].rearrange("g c d -> (g c) d"))]))
        for i in range(4):
            if i:
                tiles.append(("ga", i, square(win, 8, 3072 + 256 * i)))
            tiles.append(("wa", i, square(a["w_branch_a"][0], 8, 256 * i)))
        for i in range(4):
            tiles.append(("v", i, square(win, 8, 2048 + 256 * i)))
        for i in range(4):
            tiles.append(("u", i, square(win, 8, 1024 + 256 * i)))
        for i in range(4):
            tiles.append(("gb", i, square(win, 8, 4096 + 256 * i)))
            tiles.append(("wb", i, square(a["w_branch_b"][0], 8, 256 * i)))
        for i in range(4):
            tiles.append(("wo", i, square(a["w_out"][0], 8, 256 * i)))
        plan_ffn("f", a["w_up"][0], a["w_up"][0], DFF, a["w_down"][0])
        tiles.append(("ple", 0, [(0, 2, 1024, a["w_ple"][0])]))
        for i in range(4):
            tiles.append(("pg", i, square(a["w_ple_gate"][0], 8, 256 * i)))
        plan_ffn("s0", a["ffn1_wg_2"][0], a["ffn1_wu_2"][0], 0, a["ffn1_wd_2"][0])
        wi = a["a_w_in_2"][0]
        tiles.append(("akv", 0, square(wi, 8, 1024)))
        for name, i in (("aq", 0), ("aq", 1), ("aq", 2), ("ao", 0), ("aq", 3), ("ao", 1), ("ao", 2), ("ao", 3)):
            tiles.append((name, i, square(wi, 8, 256 * i) if name == "aq" else rows4(a["a_w_out_2"][0], i)))
        plan_ffn("s1", a["ffn2_wg_2"][0], a["ffn2_wu_2"][0], 0, a["ffn2_wd_2"][0])
        plan_ffn("s2", a["ffn1_wg_2"][1], a["ffn1_wu_2"][1], 0, a["ffn1_wd_2"][1])
        wi = a["b_w_in_2"][0]
        tiles.append(("bq", 0, square(wi, 8, 0)))
        tiles.append(("bkv", 0, square(wi, 8, 256, 160)))
        for name, g in (("bg", 0), ("bg", 1), ("bo", 0), ("bg", 2), ("bo", 1), ("bg", 3), ("bo", 2), ("bo", 3)):
            tiles.append((name, g, rows4(a["b_w_out_2"][0], g) if name == "bo" else
                          [(0, 2, 384, a["b_w_uq_2"][0][:, 384 * g:384 * g + 384]),
                           (768, 1, 512, a["b_w_ukv_2"][0][:, 512 * g:512 * g + 512])]))
        plan_ffn("s3", a["ffn2_wg_2"][1], a["ffn2_wu_2"][1], 0, a["ffn2_wd_2"][1])

    THIRDS = ((0, 8), (8, 8), (16, 6))

    def plan_ffn(tag, wa, wb, off, wd):
        for h, (c0, n) in enumerate(THIRDS):
            for j in range(n // 2):
                tiles.append((tag + "a", (h, j), square(wa, 8, 128 * c0 + 256 * j)))
                tiles.append((tag + "b", (h, j), square(wb, 8, off + 128 * c0 + 256 * j)))
            for i in range(4):
                tiles.append((tag + "d", (h, i), [(0, n, 256, wd[128 * c0:128 * (c0 + n), 256 * i:256 * i + 256])]))

    plan()
    NW = len(tiles)
    landed, halves, split, used = {}, {}, {}, {}
    state = {"dma": 0, "split": 0, "use": 0, "low": DV}

    def size(n):
        return max(o + k * w for o, k, w, _ in tiles[n][2])

    def load_tile():
        n = state["dma"]
        if n >= NW:
            return
        state["dma"] += 1
        for o, k, w, src in tiles[n][2]:
            dst = RAW[:, n % 2, o:o + k * w].rearrange("p (k w) -> p k w", k=k)
            landed[n] = SP.dma(raws[n % 2], dst, src.rearrange("(k p) w -> p k w", p=128), split.get(n - 2))

    def split_tile():
        n = state["split"]
        if n >= NW:
            return
        state["split"] += 1
        s, z = n % 3, size(n)
        parts = [(0, z // 2), (z // 2, z)]
        ta = [AC.add(lambda e, x=x, y=y: e.activation(Wh[:, s, x:y], RAW[:, n % 2, x:y], ACT.Copy),
                     landed[n], used.get(n - 3)) for x, y in parts]
        td = [state["low"].add(lambda e, x=x, y=y: e.tensor_tensor(Wl[:, s, x:y], RAW[:, n % 2, x:y], f(Wh[:, s, x:y]),
                                                         ALU.subtract), t, used.get(n - 3))
              for (x, y), t in zip(parts, ta)]
        split[n] = td

    def next_tile(name, i, ahead=2):
        n = state["use"]
        assert tiles[n][0:2] == (name, i), (tiles[n][0:2], name, i)
        state["use"] += 1
        assert n + ahead - 3 < 0 or n + ahead - 3 in used
        while state["split"] <= min(n + ahead, NW - 1):
            split_tile()
            load_tile()
        s = n % 3
        views = []
        for o, k, w, _ in tiles[n][2]:
            views.append(tuple(W[:, s, o:o + k * w].rearrange("p (k w) -> p k w", k=k) for W in (Wh, Wl)))
        PE.wait(split[n])
        return n, views

    def tile_used(n):
        used[n] = (PE.sem, PE.n)

    def mm3(o, lh, ll, rh, rl, start, stop):
        PE.add(lambda e: e.matmul(o, ll, rh, start=start, stop=False), signal=False)
        PE.add(lambda e: e.matmul(o, lh, rl, start=False, stop=False), signal=False)
        return PE.add(lambda e: e.matmul(o, lh, rh, start=False, stop=stop), signal=stop)

    hready = [[] for _ in range(8)]
    pready = [[] for _ in range(16)]

    def form_a(views, K, src, ready, base=0, m=2, kw=0, ring=None, scaled=None,
               wide=False):
        res = []
        wh, wl = views
        if wide:
            got = [(ring or banks).take() for _ in range(m)]
            last = [None] * m
            for k0, k1 in ((0, K - 2), (K - 2, K)):
                for c in range(m):
                    PE.wait(got[c][2])
                    cc = slice((kw + c) * 128, (kw + c + 1) * 128)
                    for k in range(k0, k1):
                        PE.wait(ready[base + k])
                        last[c] = mm3(got[c][1], wh[:, k, cc], wl[:, k, cc], src[0][:, base + k, :],
                                      src[1][:, base + k, :], k == 0, k == K - 1)
            return [(got[c][0], got[c][1], last[c]) for c in range(m)]
        for c in range(m):
            bi, bank, was = (ring or banks).take()
            PE.wait(was)
            for k in range(K):
                PE.wait(ready[base + k])
                cc = slice((kw + c) * 128, (kw + c + 1) * 128)
                t = mm3(bank, wh[:, k, cc], wl[:, k, cc], src[0][:, base + k, :], src[1][:, base + k, :],
                        k == 0, k == K - 1)
            res.append((bi, bank, t))
            norm_step()
        return res if scaled is None else scale_banks(res, scaled)

    def scale_banks(res, R):
        assert nstate["R"]
        return [(bi, bank, DV.add(lambda e: e.tensor_tensor(bank, bank, R, ALU.mult), t, nstate["R"]))
                for bi, bank, t in res]

    def norm_step():
        if nstate["todo"]:
            nstate["todo"].pop(0)()

    H, P = (Hh, Hl), (Ph, Pl)

    def pair(dst, c, src_tok, view, *was):
        h = AC.add(lambda e: e.activation(dst[0][:, c, :], view, ACT.Copy), src_tok, *was)
        l = DV.add(lambda e: e.tensor_tensor(dst[1][:, c, :], view, f(dst[0][:, c, :]), ALU.subtract), h, *was)
        return [h, l]

    xt = [[] for _ in range(8)]
    SQ = TMP[:, NT - 1, 16:528]
    SQ2 = Z[:, 512:1024]
    tmps = Ring([TMP[:, i, :] for i in range(NT - 1)])
    bstate = {"nt": None}
    nstate = {"sq": None, "read": [], "rs": None, "todo": [], "R": None, "hread": None, "rst": None, "sq2": None}

    nt = sb("nt", [128, 32])

    def rsqrt_small(dst, src, n, *after):
        w = dst.shape[1]
        v, u = nt[:, 0:w], nt[:, 16:16 + w]
        t = DV.add(lambda e: e.tensor_scalar(v, src, 1.0 / n, EPS, ALU.mult, ALU.add), bstate["nt"], *after)
        t = DV.add(lambda e: e.tensor_scalar(u.bitcast(I32), v.bitcast(I32), 1, None, ALU.logical_shift_right), t)
        t = DV.add(lambda e: e.tensor_scalar(dst.bitcast(I32), u.bitcast(I32), -1.0, float(0x5F3759DF), ALU.mult,
                                             ALU.add), t)
        for _ in range(3):
            t = DV.add(lambda e: e.tensor_tensor(u, dst, dst, ALU.mult), t)
            t = DV.add(lambda e: e.scalar_tensor_tensor(u, u, -0.5, v, ALU.mult, ALU.mult), t)
            t = DV.add(lambda e: e.scalar_tensor_tensor(dst, u, 1.5, dst, ALU.add, ALU.mult), t)
        bstate["nt"] = t
        return t

    def stats(c):
        if c == 0:
            nstate["sq"] = AC.add(lambda e: e.activation(SQ, X[:, c, :], ACT.Square), xt[c], nstate["read"])
            xt[c] = xt[c] + [nstate["sq"]]
            return
        ti, tv, was = tmps.take()
        v = tv[:, 16:528]
        s = AC.add(lambda e: e.activation(v, X[:, c, :], ACT.Square), xt[c], was)
        xt[c] = xt[c] + [s]
        nstate["sq"] = PO.add(lambda e: e.tensor_tensor(SQ, SQ, v, ALU.add), s, nstate["sq"])
        tmps.done(ti, nstate["sq"])

    def stats2(c, g):
        if c == 0:
            nstate["sq2"] = AC.add(lambda e: e.activation(SQ2, X[:, c, :], ACT.Square, scale=g), xt[c], bstate["t"])
            xt[c] = xt[c] + [nstate["sq2"]]
            return
        ti, tv, was = tmps.take()
        v = tv[:, 16:528]
        s = AC.add(lambda e: e.activation(v, X[:, c, :], ACT.Square, scale=g), xt[c], was)
        xt[c] = xt[c] + [s]
        nstate["sq2"] = PO.add(lambda e: e.tensor_tensor(SQ2, SQ2, v, ALU.add), s, nstate["sq2"])
        tmps.done(ti, nstate["sq2"])

    def h_pair(c, name, base=0, g=None):
        g = gain(name, c, base) if g is None else g
        h = AC.add(lambda e: e.activation(Hh[:, c, :], X[:, c, :], ACT.Copy, scale=g), xt[c], nstate["hread"])
        l = DV.add(lambda e: e.scalar_tensor_tensor(Hl[:, c, :], X[:, c, :], g, f(Hh[:, c, :]), ALU.mult,
                                                    ALU.subtract), h, nstate["hread"])
        xt[c] = xt[c] + [h]
        hready[c] = [h, l]

    def h_read():
        nstate["hread"] = (PE.sem, PE.n)

    def rs_columns():
        bi, bank, was = banks.take()
        PE.wait(was, nstate["sq"])
        for n in range(4):
            t = PE.add(lambda e, n=n: e.matmul(bank[:, n:n + 1], SQ[:, 128 * n:128 * n + 128], ones[:, 0:1],
                                               start=True, stop=True))
        nstate["read"] = [t]
        t3 = rsqrt_small(rs4, bank[:, 0:4], D, t, nstate["rs"])
        banks.done(bi, t3)
        return t3

    def rs_diagonal(t3, col4=None):
        src = rs4 if col4 is None else col4
        ti, tv, w2 = tmps.take()
        v = tv[:, 16:528]
        DV.wait(t3)
        for n in range(4):
            t4 = DV.add(lambda e, n=n: e.tensor_scalar(v[:, 128 * n:128 * n + 128], ident[:, :], src[:, n:n + 1], None,
                                                       ALU.mult), w2)
        nstate["rs"] = t4
        return ti, v, t4

    def rs_spread(ti, v, t4):
        bi, bank, was = banks.take()
        PE.wait(was)
        t5 = PE.add(lambda e: e.matmul(bank, ones[:, :], v, start=True, stop=True), t4)
        tmps.done(ti, t5)
        return bi, bank, t5

    def norm_begin(R, *was, steps=(0, 1)):
        part = {}

        def first():
            part["d"] = rs_diagonal(rs_columns())

        def second():
            bi, bank, t = rs_spread(*part["d"])
            nstate["R"] = AC.add(lambda e: e.activation(R, bank, ACT.Copy), t, *was)
            banks.done(bi, nstate["R"])
        nstate["rs"], nstate["R"] = now(), None
        nstate["todo"] = [lambda: None] * (steps[1] + 1)
        nstate["todo"][steps[0]], nstate["todo"][steps[1]] = first, second

    def norm_begin_twice(R, *was):
        r1, m2 = small[:, 88:92], small[:, 92:96]
        part = {}

        def first():
            bi, bank, free = banks.take()
            PE.wait(free, nstate["sq"], nstate["sq2"])
            for i, q in enumerate((SQ, SQ2)):
                for n in range(4):
                    t = PE.add(lambda e: e.matmul(bank[:, 4 * i + n:4 * i + n + 1], q[:, 128 * n:128 * n + 128],
                                                  ones[:, 0:1], start=True, stop=True))
            nstate["read"] = [t]
            bstate["t"] = bstate["t"] + [t]
            t = rsqrt_small(r1, bank[:, 0:4], D, t)
            t = DV.add(lambda e: e.tensor_tensor(m2, r1, r1, ALU.mult), t)
            t = DV.add(lambda e: e.tensor_tensor(m2, bank[:, 4:8], m2, ALU.mult), t)
            banks.done(bi, t)
            t = rsqrt_small(rs4, m2, D, t, nstate["rs"])
            part["r1"] = t
            part["d"] = rs_diagonal(DV.add(lambda e: e.tensor_tensor(rs4, rs4, r1, ALU.mult), t))

        def second():
            bi, bank, t = rs_spread(*part["d"])
            nstate["R"] = AC.add(lambda e: e.activation(R, bank, ACT.Copy), t, *was)
            banks.done(bi, nstate["R"])

        def third():
            bi, bank, t = rs_spread(*rs_diagonal(part["r1"], r1))
            for c in range(8):
                t = DV.add(lambda e: e.scalar_tensor_tensor(X[:, c, :], X[:, c, :], gain("final_norm", c), bank,
                                                            ALU.mult, ALU.mult), t, xt[c])
                xt[c] = [t]
            banks.done(bi, t)
        nstate["rs"], nstate["R"] = now(), None
        nstate["todo"] = [first, second, lambda: None, lambda: None, lambda: None, third]

    def norm_begin_rows():
        def first():
            nstate["rst"] = rs_columns()
        nstate["rs"] = now()
        nstate["todo"] = [first]

    def now():
        return [(q.sem, q.n) for q in (PE, AC, DV, PO) if q.n]

    def add_x(c, bank, tok, factor):
        t = DV.add(lambda e: e.scalar_tensor_tensor(X[:, c, :], bank, factor, X[:, c, :], ALU.mult, ALU.add),
                   tok, xt[c])
        xt[c] = [t]
        return t

    def ffn(tag, kind, after=None, after_base=0, mid=None):
        for h, (c0, n) in enumerate(THIRDS):
            base = 8 * (h % 2)
            for j in range(n // 2):
                begins = (h, j) == (0, 0)
                if not begins:
                    extra(4)
                na, va = next_tile(tag + "a", (h, j), 1 if begins else 2)
                ra = form_a(va[0], 8, H, hready, scaled=None if begins else RF)
                tile_used(na)
                if begins:
                    nb, vb = next_tile(tag + "b", (h, j))
                    rb = form_a(vb[0], 8, H, hready)
                    tile_used(nb)
                    ra = scale_banks(ra, RF)
                acts = []
                for c in range(2):
                    cc = c0 + 2 * j + c
                    bi, bank, t = ra[c]
                    if kind == "conv":
                        v, toks, ti = conv(cc, bank, t, bi)
                        t2 = AC.add(lambda e, v=v: e.activation(v, v, ACT.Gelu), toks)
                        acts.append((v, t2, ti))
                    else:
                        ti, tv, was = tmps.take()
                        v = tv[:, 16:528]
                        t2 = AC.add(lambda e, v=v, bank=bank: e.activation(v, bank, ACT.Silu), t, was)
                        banks.done(bi, t2)
                        acts.append((v, t2, ti))
                if begins:
                    rb = scale_banks(rb, RF)
                else:
                    nb, vb = next_tile(tag + "b", (h, j), 1 if kind == "conv" and j == n // 2 - 1 else 2)
                    rb = form_a(vb[0], 8, H, hready, scaled=RF)
                    tile_used(nb)
                for c in range(2):
                    cc = c0 + 2 * j + c
                    bi, bank, t = rb[c]
                    v, t2, ti = acts[c]
                    if kind == "conv":
                        w, toks, tj = conv(22 + cc, bank, t, bi)
                        t3 = DV.add(lambda e, v=v, w=w: e.tensor_tensor(v, v, w, ALU.mult), toks, t2)
                        tmps.done(tj, t3)
                    else:
                        t3 = DV.add(lambda e, v=v, bank=bank: e.tensor_tensor(v, v, bank, ALU.mult), t, t2)
                        banks.done(bi, t3)
                    q = base + 2 * j + c
                    pready[q] = pair(P, q, t3, v, pfree[q])
                    tmps.done(ti, *pready[q])
            if h == 2:
                h_read()
                nstate["mfree"] = now()
            for i in range(4):
                extra(4)
                if tag == "s3" and h == 2 and i:
                    out_tile(i - 1)
                if mid and (h, i) == (2, 2):
                    mid()
                nd, vd = next_tile(tag + "d", (h, i))
                rd = form_a(vd[0], n, P, pready, base=base, wide=i == 0)
                tile_used(nd)
                for c in range(2):
                    bi, bank, t = rd[c]
                    banks.done(bi, add_x(2 * i + c, bank, t, 1.0 if kind == "conv" else 0.5))
                    if h == 2 and tag != "s3":
                        if after:
                            h_pair(2 * i + c, after, after_base)
                        stats(2 * i + c)
            for q in range(16):
                pfree[q] = [(PE.sem, PE.n)] if base <= q < base + 8 else pfree[q]

    pfree = [[] for _ in range(16)]
    RF = M[:, 6, :]

    def out_tile(i):
        om = M[:, 2 * i:2 * i + 2, :].rearrange("p a b -> p (a b)").rearrange("p (n d) -> p n d", n=4)
        eng = ((DV, lambda e, o, b: e.tensor_copy(o, b)), (AC, lambda e, o, b: e.activation(o, b, ACT.Copy)))
        toks = []
        for c, (E, put) in enumerate(eng):
            bi, bank, was = banks.take()
            PE.wait(was, xt[2 * i + c])
            for n in range(4):
                t = PE.add(lambda e: e.transpose(bank[:, 128 * n:128 * n + 128],
                                                 X[:, 2 * i + c, 128 * n:128 * n + 128], ident[:, :]))
            toks.append(E.add(lambda e: put(e, om[:, :, 128 * c:128 * c + 128],
                                            bank.rearrange("p (n d) -> p n d", n=4)), t, nstate["mfree"]))
            banks.done(bi, toks[-1])
        bstate["out"] = SP.dma(cs["out"], out[0, :, 256 * i:256 * i + 256].rearrange("(n p) d -> p n d", p=128), om,
                               toks)

    def conv(cc, bank, t, bi):
        ti, tv, was = tmps.take()
        v = tv[:, 16:528]
        t1 = AC.add(lambda e: e.activation(v, bank, ACT.Identity, bias=convp(-1, cc), scale=convp(2, cc)), t, was)
        t2 = DV.add(lambda e: e.scalar_tensor_tensor(v[:, 1:T], bank[:, 0:T - 1], convp(1, cc), v[:, 1:T], ALU.mult,
                                                     ALU.add), t1)
        t3 = DV.add(lambda e: e.scalar_tensor_tensor(v[:, 2:T], bank[:, 0:T - 2], convp(0, cc), v[:, 2:T], ALU.mult,
                                                     ALU.add), t2)
        banks.done(bi, t3)
        return v, [t3], ti

    extras = []

    def extra(n):
        for _ in range(n):
            if extras:
                extras.pop(0)()

    BND = [LOWEST] + [float(b) for b in bucket_bounds()]

    def bias_consts():
        rows = Z[:, 0:128].rearrange("p (n k) -> p n k", n=4)
        was = bstate["t"]
        for k in range(32):
            t = PO.add(lambda e, k=k: e.memset(rows[:, :, k:k + 1], BND[k]), was)
        t1 = DV.add(lambda e: e.tensor_tensor(Z[:, 0:128], Z[:, 0:128], ident[:, :], ALU.mult), t, was)
        t1 = DV.add(lambda e: e.tensor_reduce(lo, Z[:, 0:128], AX.X, ALU.add), t1)
        tz = PO.add(lambda e: e.memset(rb2[:, 16:32], 0.0))
        rb = a["rel_bias_2"]
        for n in range(4):
            SP.dma(cs["rb"], rb2[32 * n:32 * n + 32, 0:16], rb)
            t = SP.dma(cs["rb"], rb2[32 * n + 1:32 * n + 32, 16:32], rb[0:31, :], tz)
        bstate["rb"] = t
        for n in range(4):
            SP.dma(cs["pos2"], pki[32 * n:32 * n + 32, 0:255],
                   PS[1 + 128 * n:256 + 128 * n].rearrange("(o n) -> o n", o=1).broadcast_to([32, 255]),
                   bstate["pos"])
            t = SP.dma(cs["pos2"], pki[32 * n:32 * n + 32, 256:384],
                       PS[128 + 128 * n:256 + 128 * n].rearrange("(o n) -> o n", o=1).broadcast_to([32, 128]))
        bstate["pki"] = t

    def bias_table():
        d = rb2[:, 32:48]
        t = bstate["rb"]
        t = DV.add(lambda e: e.tensor_tensor(d, rb2[:, 0:16], rb2[:, 16:32], ALU.subtract), t)
        for j in range(3):
            part = drb3[:, :].rearrange("p (h j) -> p h j", j=3)[:, :, j]
            t = DV.add(lambda e, part=part: e.tensor_copy(part, d), t)
            if j < 2:
                t = DV.add(lambda e, part=part: e.tensor_tensor(d, d, part, ALU.subtract), t)
        bstate["drb"] = t
        t = bstate["pki"]
        DV.add(lambda e: e.tensor_copy(pkf[:, 0:255], pki[:, 0:255]), t)
        bstate["pk"] = DV.add(lambda e: e.tensor_copy(pkf[:, 256:384], pki[:, 256:384]), t)
        bstate["t"] = bstate["t"] + [bstate["pk"]]

    def plan_bias():
        acc = Z[:, :].rearrange("p (h n u) -> p h n u", h=16, n=4)
        GU = 32
        Gv = M[:, 0:4, :].rearrange("p a b -> p (a b)").bitcast(BF16).rearrange("p (q u) -> p q u", q=128)
        pk_t = pkf[:, :]
        for ch in range(4):
            def compare(ch=ch):
                keys = bass.AP(pk_t.tensor, pk_t.offset + GU * ch, [list(pk_t.ap[0]), [1, 128], [1, GU]])
                qs = pkf[:, 256:384].unsqueeze(2).broadcast_to([128, 128, GU])
                bstate["G"] = DV.add(lambda e: e.scalar_tensor_tensor(Gv, keys, lo, qs, ALU.add, ALU.is_le),
                                     bstate["pk"], bstate.get("gread"), bstate["t"], bstate["mfree"])
            extras.append(compare)
            extras.extend([lambda: None] * 3)
            for n in range(4):
                for v in range(4):
                    def step(ch=ch, n=n, v=v):
                        bi, bank, was = banks.take()
                        PE.wait(was, bstate["G"], bstate["drb"])
                        rows = slice(32 * n, 32 * n + 32)
                        for w in range(8):
                            t = PE.add(lambda e, w=w: e.matmul(bank[:, 48 * w:48 * w + 48], Gv[rows, :, 8 * v + w],
                                                               drb3[rows, :], start=True, stop=True))
                        bstate["gread"] = t
                        src = bank[:, 0:384].rearrange("p (u h j) -> p h u j", u=8, j=3)
                        t = DV.add(lambda e: e.tensor_reduce(acc[:, :, n, 8 * v:8 * v + 8], src, AX.X, ALU.add),
                                   t, bstate.get("bw"), bstate["t"])
                        banks.done(bi, t)
                        bstate["acc"] = t
                    extras.append(step)

            def write(ch=ch):
                for h in range(16):
                    dst = bass.AP(BS.tensor, h * 4 * 128 * 256 + 1 + GU * ch, [[257, 128], [128 * 256, 4], [1, GU]])
                    bstate["bw"] = SP.dma(cs["bw"], dst, acc[:, h, :, :], bstate["acc"], bstate["fill"])
            extras.append(write)

    xm = M[:, 0:6, :].rearrange("p a b -> p (a b)").rearrange("p (n d) -> p n d", n=3)
    tx = []
    for half, cx in enumerate((cs["x"], cs["x2"])):
        sl = slice(512 * half, 512 * half + 512)
        SP.dma(cx, xm[:, :, sl], a["x"][0, 0:384, sl].rearrange("(n p) d -> p n d", p=128))
        tx.append(SP.dma(cx, Z[:, sl], a["x"][0, 384:512, sl]))
    load_tile()
    t_par = parameters()
    load_tile()
    for c in range(8):
        bi, bank, was = banks.take()
        PE.wait(was, tx[c // 4], t_const)
        for n in range(4):
            src = xm[:, n, 128 * c:128 * c + 128] if n < 3 else Z[:, 128 * c:128 * c + 128]
            t = PE.add(lambda e, n=n, src=src, bank=bank: e.transpose(bank[:, 128 * n:128 * n + 128], src, ident[:, :]))
        if c % 2:
            xt[c] = [AC.add(lambda e: e.activation(X[:, c, :], bank, ACT.Copy), t)]
        else:
            xt[c] = [DV.add(lambda e: e.tensor_copy(X[:, c, :], bank), t)]
        banks.done(bi, *xt[c])
    split_tile()
    load_tile()
    AC.wait(t_par)
    for c in range(8):
        h_pair(c, "mix_norm")
    for c in range(8):
        stats(c)
    t_x_in = t
    R0 = ropt[:, :, :].rearrange("p a b -> p (a b)")
    norm_begin(R0, steps=(1, 3))
    wsp = Z[:, 0:1024].rearrange("p (h s) -> p h s", h=8)
    bsp = Z[:, 1024:2048].rearrange("p (h t) -> p h t", h=8)
    t_ws = SP.dma(cs["ws"], wsp, a["w_spatial"][0].rearrange("h t s -> t h s"), t_x_in)
    t_ws = SP.dma(cs["ws"], Z[:, 1024:2048],
                  flat(a["b_spatial"]).rearrange("(o n) -> o n", o=1).broadcast_to([128, 1024]))
    pos = flat(a["positions_2"])
    SP.wait(t_const)
    SP.dma(cs["sm"], smi[:, :], pos.rearrange("(n p) -> p n", p=128))
    SP.dma(cs["sm"], sinkc, a["a_sinks_2"].broadcast_to([128, 16]))
    for k, (name, w, d) in enumerate((("a_q_gain_2", 64, gq_a), ("a_k_gain_2", 64, gk_a))):
        gcol = flat(a[name]).rearrange("(n o) -> n o", o=1)
        SP.dma(cs["sm"], d[0:64, :], gcol)
        SP.dma(cs["sm"], d[64:128, :], gcol)
    for name, d, row in (("b_q_gain_2", gq_b, grow_q), ("b_k_gain_2", gk_b, grow_k)):
        SP.dma(cs["sm"], d[0:64, :], flat(a[name]).rearrange("(n o) -> n o", o=1)[0:64, :])
        t_sm = SP.dma(cs["sm"], row, a[name][:, 64:96].broadcast_to([128, 32]))
    SP.dma(cs["pscr"], PS[0:128], pos[0:128])
    bstate["pos"] = SP.dma(cs["pscr"], PS[128:640], pos)
    t_g1 = t_sm

    def trig(was):
        TWO_PI = 2 * math.pi
        c1 = float(np.float32(6.28125))
        c2 = float(np.float32(TWO_PI - c1))
        c3 = float(np.float32(TWO_PI - c1 - c2))
        MAGIC = 12582912.0
        ang, kk, r, t_ = rope[:, 0, :], rope[:, 1, :], rope[:, 2, :], rope[:, 3, :]
        sn, cn = rope[:, 4, :], rope[:, 5, :]
        tk = None
        DV.wait(t_const, t_sm, was)
        tp = DV.add(lambda e: e.tensor_copy(posf, smi[:, :]))
        DV.wait(tp)
        for n in range(4):
            tk = DV.add(lambda e, n=n: e.tensor_scalar(ang[:, 16 * n:16 * n + 16], invf, posf[:, n:n + 1], None,
                                                       ALU.mult))
        tk = DV.add(lambda e: e.tensor_scalar(kk, ang, 1.0 / TWO_PI, None, ALU.mult), tk)
        tk = DV.add(lambda e: e.tensor_scalar(kk, kk, MAGIC, None, ALU.add), tk)
        tk = DV.add(lambda e: e.tensor_scalar(kk, kk, -MAGIC, None, ALU.add), tk)
        tk = DV.add(lambda e: e.scalar_tensor_tensor(r, kk, -c1, ang, ALU.mult, ALU.add), tk)
        tk = DV.add(lambda e: e.scalar_tensor_tensor(r, kk, -c2, r, ALU.mult, ALU.add), tk)
        tk = DV.add(lambda e: e.scalar_tensor_tensor(r, kk, -c3, r, ALU.mult, ALU.add), tk)
        PI = float(np.nextafter(np.float32(math.pi), np.float32(0)))
        tk = DV.add(lambda e: e.tensor_scalar(r, r, PI, -PI, ALU.min, ALU.max), tk)
        ts = AC.add(lambda e: e.activation(sn, r, ACT.Sin), tk)
        tk = DV.add(lambda e: e.tensor_scalar(t_, r, -1.0, None, ALU.mult), tk)
        tk = DV.add(lambda e: e.tensor_tensor(t_, t_, r, ALU.max), tk)
        tk = DV.add(lambda e: e.tensor_scalar(t_, t_, -1.0, math.pi / 2, ALU.mult, ALU.add), tk)
        tc = AC.add(lambda e: e.activation(cn, t_, ACT.Sin), tk)
        DV.wait(ts, tc)

    def tables():
        sn, cn = rope[:, 4, :], rope[:, 5, :]
        tk = None
        for row, base in ((grow_q, 0), (grow_k, 4)):
            dst = ropt[:, base:base + 4, :]
            for j, (g, tr) in enumerate(((0, cn), (16, sn), (16, cn), (0, sn))):
                for n in range(4):
                    tk = DV.add(lambda e, j=j, g=g, tr=tr, n=n, dst=dst, row=row: e.tensor_tensor(
                        dst[:, j, 16 * n:16 * n + 16], tr[:, 16 * n:16 * n + 16], row[:, g:g + 16], ALU.mult))
        return tk




    rp = {}
    for g in range(4):
        w = 2 << g
        for gg in {0: (0, 1), 1: ()}.get(g, (g,)):
            n, v = next_tile("pool", gg, 1 if gg == 0 else 2)
            rp[gg] = form_a(v[0], 8, H, hready)
            tile_used(n)
        r = scale_banks(rp[g], R0)
        for c in range(2):
            bi, bank, t = r[c]
            i0, z0, w0 = tmps.take()
            i1, z1, w1 = tmps.take()
            i2, z2, w2 = tmps.take()
            tz = AC.add(lambda e, z0=z0, bank=bank: e.activation(z0[:, 16:528], bank, ACT.Copy), t, w0)
            src, dsts = z0, [z1, z2]
            tk, k, q = tz, 1, 0
            while k < w:
                d = dsts[q % 2]
                tk = DV.add(lambda e, d=d, src=src, k=k: e.tensor_tensor(d[:, 16:528], src[:, 16:528],
                                                                         src[:, 16 - k:528 - k], ALU.add),
                            tk, w1, w2)
                src, k, q = d, 2 * k, q + 1
            tk = DV.add(lambda e, s=src, w=w: e.scalar_tensor_tensor(s[:, 16:16 + w], s[:, 16:16 + w], float(w),
                                                                     rinv[:, 0:w], ALU.mult, ALU.mult), tk)
            tk = DV.add(lambda e, s=src, w=w, z0=z0: e.scalar_tensor_tensor(s[:, 16:528], s[:, 16:528], 1.0 / w,
                                                                            z0[:, 16:528], ALU.mult, ALU.subtract), tk)
            banks.done(bi, tz)
            q = 2 * g + c
            pready[q] = pair(P, q, tk, src[:, 16:528])
            for i in (i0, i1, i2):
                tmps.done(i, *pready[q])
    def gate_tile(tg, i, ring=None):
        ng, vg = next_tile(tg, i)
        rg = form_a(vg[0], 8, H, hready, ring=ring)
        tile_used(ng)
        return rg

    held = banks.part(2)
    ga0 = gate_tile("ga", 0, held)
    n, v = next_tile("wpool", 0)
    wh, wl = v[0]
    for g in range(4):
        r = form_a((wh[:, 2 * g:2 * g + 2, :], wl[:, 2 * g:2 * g + 2, :]), 2, P, pready, base=2 * g)
        for c in range(2):
            bi, bank, t = r[c]
            q = 8 + 2 * g + c
            s = gain("pool_scale", 2 * g + c)
            h = AC.add(lambda e, q=q, bank=bank, s=s: e.activation(Ph[:, q, :], bank, ACT.Copy, scale=s), t)
            l = DV.add(lambda e, q=q, bank=bank, s=s: e.scalar_tensor_tensor(
                Pl[:, q, :], bank, s, f(Ph[:, q, :]), ALU.mult, ALU.subtract), h)
            pready[q] = [h, l]
            banks.done(bi, h, l)
    tile_used(n)
    t_pool = r[1][2]

    def gated(ta, tg, src, ready, base, finish, gate=None):
        for i in range(4):
            if gate is None:
                gate = gate_tile(tg, i)
            rg, gate = scale_banks(gate, R0), None
            na, va = next_tile(ta, i)
            ra = form_a(va[0], 8, src, ready, base=base)
            tile_used(na)
            for c in range(2):
                bg, bankg, tgk = rg[c]
                ba, banka, tak = ra[c]
                ti, tv, was = tmps.take()
                v = tv[:, 16:528]
                s = AC.add(lambda e, v=v, b=bankg: e.activation(v, b, ACT.Sigmoid), tgk, was)
                banks.done(bg, s)
                t = finish(2 * i + c, v, banka, [s, tak])
                banks.done(ba, t)
                tmps.done(ti, t)

    mt = [None] * 8

    def fin_a(c, v, bank, toks):
        mt[c] = DV.add(lambda e: e.tensor_tensor(M[:, c, :], v, bank, ALU.mult), *toks)
        return mt[c]

    banks.join(held)
    ga0 = [(len(banks.views) - 2 + bi, bank, t) for bi, bank, t in ga0]
    gated("wa", "ga", P, pready, 8, fin_a, ga0)
    t_free8 = (PE.sem, PE.n)

    vh, vl = (W[:, 0:8, :].rearrange("p a b -> p (a b)").rearrange("p (n d) -> p n d", n=4) for W in (Ph, Pl))
    ssv = small[:, 0:16].rearrange("p (n i) -> p n i", n=4)
    vtok = []
    for i in range(4):
        n, v = next_tile("v", i)
        wh, wl = v[0]
        for half in range(2):
            bi, bank, was = banks.take()
            PE.wait(was)
            for q in range(2):
                b = 2 * half + q
                for k in range(8):
                    t = mm3(bank[:, 256 * q:256 * q + 256], Hh[:, k, 128 * b:128 * b + 128],
                            Hl[:, k, 128 * b:128 * b + 128], wh[:, k, :], wl[:, k, :], k == 0, k == 7)
            ti, tv, w0 = tmps.take()
            tj, tw, w1 = tmps.take()
            vv, ww = tv[:, 16:528], tw[:, 16:528]
            for q in range(2):
                tg = AC.add(lambda e: e.activation(vv[:, 256 * q:256 * q + 256], bank[:, 256 * q:256 * q + 256],
                                                   ACT.Gelu, scale=rs4[:, 2 * half + q:2 * half + q + 1]), t, w0)
            banks.done(bi, tg)
            hh = vh[:, 2 * half:2 * half + 2, 256 * i:256 * i + 256]
            ll = vl[:, 2 * half:2 * half + 2, 256 * i:256 * i + 256]
            v3 = vv.rearrange("p (q d) -> p q d", q=2)
            h = AC.add(lambda e, hh=hh, v3=v3: e.activation(hh, v3, ACT.Copy), tg, t_pool)
            l = DV.add(lambda e, ll=ll, v3=v3, hh=hh: e.tensor_tensor(ll, v3, f(hh), ALU.subtract), h)
            for q in range(2):
                s = AC.add(lambda e, q=q, i=i, half=half, vv=vv, ww=ww: e.activation(
                    ww[:, 256 * q:256 * q + 256], vv[:, 256 * q:256 * q + 256], ACT.Square,
                    accum_out=ssv[:, 2 * half + q, i:i + 1]), tg, w1)
            vtok += [h, l]
            tmps.done(ti, l, s)
            tmps.done(tj, s)
        tile_used(n)
    ssum, rv = small[:, 16:20], small[:, 24:28]
    t = DV.add(lambda e: e.tensor_reduce(ssum, ssv, AX.X, ALU.add), s)
    t_rv = rsqrt_small(rv, ssum, 1024, t)

    t_m = PO.add(lambda e: e.affine_select(out=wsp, in_=wsp, compare_op=ALU.is_ge, fill=0.0, base=0,
                                           pattern=[[0, 8], [-1, 128]], channel_multiplier=1), t_ws)
    for half in range(2):
        bi, bank, was = banks.take()
        PE.wait(was, t_m)
        for q in range(4):
            t = PE.add(lambda e, q=q, half=half, bank=bank: e.transpose(bank[:, 128 * q:128 * q + 128],
                                                                        wsp[:, 4 * half + q, :], ident[:, :]))
        t_wsT = DV.add(lambda e, half=half, bank=bank: e.tensor_copy(Z[:, 512 * half:512 * half + 512], bank), t)
        banks.done(bi, t_wsT)

    ws_free = [None]

    def ws_pair(h, t_mixed):
        ti, tv, was = tmps.take()
        tt = tv[:, 16:528]
        for q in range(4):
            ts = DV.add(lambda e: e.tensor_scalar(tt[:, 128 * q:128 * q + 128], wsp[:, h, :], rv[:, q:q + 1], None,
                                                  ALU.mult), t_wsT, t_rv, was)
        th = AC.add(lambda e: e.activation(WS[:, 0, :], tt, ACT.Copy), ts, t_mixed)
        tl = DV.add(lambda e: e.tensor_tensor(WS[:, 1, :], tt, f(WS[:, 0, :]), ALU.subtract), th, t_mixed)
        tmps.done(ti, tl)
        return [th, tl]

    def mix(h, tws, ui, uu, tu):
        bj, bk, was = banks.take()
        PE.wait(was, tws, vtok)
        for q in range(4):
            sl = slice(128 * q, 128 * q + 128)
            hc = slice(128 * h, 128 * h + 128)
            t = mm3(bk[:, sl], vh[:, q, hc], vl[:, q, hc], WS[:, 0, sl], WS[:, 1, sl], True, True)
        tm, z2, w2 = tmps.take()
        mx = z2[:, 16:528]
        bb = bsp[:, h, :].unsqueeze(1).broadcast_to([128, 4, 128])
        t1 = DV.add(lambda e: e.scalar_tensor_tensor(
            mx.rearrange("p (n t) -> p n t", n=4), bk.rearrange("p (n t) -> p n t", n=4), gain("sgu_norm", h), bb,
            ALU.mult, ALU.add), t, w2)
        banks.done(bj, t1)
        t2 = DV.add(lambda e: e.tensor_tensor(mx, mx, uu, ALU.mult), t1, tu)
        pready[8 + h] = pair(P, 8 + h, t2, mx, t_free8)
        utmps.done(ui, t2)
        tmps.done(tm, *pready[8 + h])
        return t

    utmps = tmps.part(1)
    tws = ws_pair(0, None)
    before = None
    for i in range(4):
        n, v = next_tile("u", i)
        for c in range(2):
            h = 2 * i + c
            bi, bank, t = form_a((v[0][0][:, :, 128 * c:128 * c + 128], v[0][1][:, :, 128 * c:128 * c + 128]), 8, H,
                                 hready, m=1, scaled=R0)[0]
            if c == 1:
                tile_used(n)
            if before is not None:
                t_mix = mix(h - 1, tws, *before)
                tws = ws_pair(h, t_mix)
            ui, uv, uw = utmps.take()
            uu = uv[:, 16:528]
            tu = AC.add(lambda e: e.activation(uu, bank, ACT.Gelu), t, uw)
            banks.done(bi, tu)
            before = (ui, uu, tu)
    mix(7, tws, *before)
    tmps.join(utmps)
    bstate["t"] = [(DV.sem, DV.n), (PE.sem, PE.n), (AC.sem, AC.n)]
    t_vused = (PE.sem, PE.n)

    def fin_b(c, v, bank, toks):
        t = DV.add(lambda e: e.tensor_tensor(v, v, bank, ALU.mult), *toks)
        t2 = DV.add(lambda e: e.tensor_tensor(M[:, c, :], M[:, c, :], v, ALU.add), t, mt[c])
        pready[c] = pair(P, c, t2, M[:, c, :], t_vused)
        return t2

    gated("wb", "gb", P, pready, 8, fin_b)
    h_read()
    for i in range(4):
        n, v = next_tile("wo", i)
        r = form_a(v[0], 8, P, pready)
        tile_used(n)
        for c in range(2):
            bi, bank, t = r[c]
            banks.done(bi, add_x(2 * i + c, bank, t, 1.0))
            h_pair(2 * i + c, "ffn_norm")
            stats(2 * i + c)
    for q in range(16):
        pfree[q] = [(PE.sem, PE.n)]

    t_f = DV.add(lambda e: e.memset(M[:, 0:2, :], NEG), (PE.sem, PE.n), (AC.sem, AC.n), (DV.sem, DV.n))
    def fill(h):
        bstate["fill"] = SP.dma(cs["fill"], BS[h].rearrange("n p s -> p n s"),
                                M[:, 0:2, :].rearrange("p a b -> p (a b)").rearrange("p (n s) -> p n s", n=4), t_f)

    for h in range(16):
        extras.append(lambda h=h: fill(h))
    extras.insert(4, bias_consts)
    extras.insert(10, bias_table)
    norm_begin(RF, now())
    pm = M[:, 4:6, :].rearrange("p a b -> p (a b)").rearrange("p (n d) -> p n d", n=4)
    t_mix = now()

    def load_p():
        bstate["p"] = SP.dma(cs["p"], pm, a["p"][0, 0].rearrange("(n p) d -> p n d", p=128), t_mix)

    def turn_p():
        for c in range(2):
            bi, bank, was = banks.take()
            PE.wait(was, bstate["p"])
            for n in range(4):
                t = PE.add(lambda e: e.transpose(bank[:, 128 * n:128 * n + 128], pm[:, n, 128 * c:128 * c + 128],
                                                 ident[:, :]))
            pready[14 + c] = pair(P, 14 + c, t, bank, pfree[14 + c])
            banks.done(bi, *pready[14 + c])
        bstate["pm"] = t

    extras.append(load_p)
    ffn("f", "conv", "ple_norm", mid=turn_p)
    t_pm = bstate["pm"]
    t_RF = (DV.sem, DV.n)
    norm_begin(Z[:, 1024:1536], bstate["t"], steps=(2, 6))

    n, v = next_tile("ple", 0)
    for c in range(8):
        r = form_a(v[0], 2, P, pready, base=14, m=1, kw=c)
        bi, bank, t = r[0]
        mt[c] = AC.add(lambda e, c=c, bank=bank: e.activation(M[:, c, :], bank, ACT.Copy), t, t_pm, t_RF, bstate["fill"])
        banks.done(bi, mt[c])
    tile_used(n)
    for q in range(16):
        pfree[q] = [(PE.sem, PE.n)]
    gg = small[:, 80:88]
    t_gg = DV.add(lambda e: e.tensor_tensor(gg, P0[:, col["final_norm"]:col["final_norm"] + 8],
                                            P0[:, col["ffn_norm1_2"]:col["ffn_norm1_2"] + 8], ALU.mult))
    AC.wait(t_gg)
    DV.wait(t_gg)

    def gate_x(cc, bi, bank, t):
        ti, tv, was = tmps.take()
        v = tv[:, 16:528]
        s = AC.add(lambda e: e.activation(v, bank, ACT.Sigmoid), t, was)
        banks.done(bi, s)
        t1 = DV.add(lambda e: e.tensor_tensor(v, v, M[:, cc, :], ALU.mult), s, mt[cc])
        t2 = DV.add(lambda e: e.tensor_tensor(X[:, cc, :], X[:, cc, :], v, ALU.add), t1, xt[cc])
        xt[cc] = [t2]
        tmps.done(ti, t2)
        stats(cc)
        stats2(cc, gain("final_norm", cc))

    for i in range(4):
        n, v = next_tile("pg", i, 1 if i == 3 else 2)
        r = form_a(v[0], 8, H, hready, scaled=Z[:, 1024:1536])
        tile_used(n)
        gate_x(2 * i, *r[0])
        if i == 3:
            h_read()
            for c in range(5):
                h_pair(c, None, g=gg[:, c:c + 1])
        gate_x(2 * i + 1, *r[1])
    for c in range(5, 8):
        h_pair(c, None, g=gg[:, c:c + 1])

    def mul3(o, x, y):
        return lambda e: e.tensor_tensor(o, x, y, ALU.mult)

    def scaled_pair(dst, rows, bank, t, scale, *was):
        h = AC.add(lambda e: e.activation(dst[0], bank, ACT.Copy, scale=scale), t, *was)
        l = DV.add(lambda e: e.scalar_tensor_tensor(dst[1], bank, scale, f(dst[0]), ALU.mult, ALU.subtract), h, *was)
        return [h, l]

    def turn(src, rows):
        bi, bank, was = banks.take()
        PE.wait(was)
        for n in range(4):
            t = PE.add(lambda e, n=n: e.transpose(bank[0:rows, 128 * n:128 * n + 128], src(n), ident[:, :]))
        return bi, bank, t

    def proj_b(W, c0, w, n_t, b0, stride, K, src=H, ring=None):
        bi, bank, was = (ring or banks).take()
        PE.wait(was)
        for q in range(n_t):
            b = b0 + q
            for k in range(K):
                PE.wait(src[2][k])
                t = mm3(bank[:, stride * q:stride * q + w], src[0][:, k, 128 * b:128 * b + 128],
                        src[1][:, k, 128 * b:128 * b + 128], W[0][:, k, c0:c0 + w], W[1][:, k, c0:c0 + w],
                        k == 0, k == K - 1)
        norm_step()
        return bi, bank, t

    def out_partial(name, src, bases, ready, free, ring, after=None, late=8):
        units = [(j, c) for j in range(4) for c in range(8)]
        held = {}

        def run(n):
            for j, c in units[:n]:
                base = bases[j % len(bases)]
                if c == 0:
                    held[j] = next_tile(name, j, 1)
                nn, v = held[j]
                bi, bank, t = form_a(v[0], 2, src, ready, base=base, m=1, kw=c, ring=ring)[0]
                ring.done(bi, add_x(c, bank, t, 1.0))
                if j == 3:
                    if after:
                        h_pair(c, *after)
                    if c < late:
                        stats(c)
                if c == 7:
                    tile_used(nn)
                    free[base - bases[0]] = [t]
                    free[base - bases[0] + 1] = [t]
            del units[:n]
        return run

    def mflat(a0, a1):
        return M[:, a0:a1, :].rearrange("p a b -> p (a b)")

    def attend_a():
        free0 = now()
        qt = mflat(0, 2).rearrange("p (n d) -> p n d", n=4)
        SS = [mflat(2, 4).rearrange("p (n s) -> p n s", n=4), mflat(4, 6).rearrange("p (n s) -> p n s", n=4),
              mflat(6, 8).rearrange("p (n s) -> p n s", n=4)]
        kd = mflat(6, 8).rearrange("p (n g u d) -> p n g u d", n=4, g=2, u=2)
        BR = [Z[:, 0:1024].rearrange("p (n s) -> p n s", n=4), Z[:, 1024:2048].rearrange("p (n s) -> p n s", n=4)]
        vA = [W[:, 2, :].rearrange("p (n d) -> p n d", n=4) for W in P]
        QT = [(Ph[:, 3, :], Pl[:, 3, :]), (WS[:, 0, :], WS[:, 1, :]), (Ph[:, 12, :], Pl[:, 12, :]),
              (Ph[:, 13, :], Pl[:, 13, :])]
        t_neg = [PO.add(lambda e, b=b: e.memset(b[:, 0, 0:128], NEG), bstate["bw"], free0) for b in BR]
        Hs = (Hh, Hl, hready)
        AC.wait(free0)
        DV.wait(free0)

        n_, v_ = next_tile("akv", 0)
        ssk, rk = small[:, 0:8], small[:, 8:16]
        got = []
        vt = []
        for half in range(2):
            bi, bank, t = proj_b(v_[0], 0, 256, 2, 2 * half, 256, 8, Hs)
            bv = bank.rearrange("p (n g d) -> p n g d", n=2, g=4)
            ti, tv, was = tmps.take()
            sq = tv[:, 16:272].rearrange("p (n g d) -> p n g d", n=2, g=2)
            for q in range(2):
                t1 = AC.add(lambda e: e.activation(sq[:, q], bv[:, q, 0:2, :], ACT.Square,
                                                   scale=rs4[:, 2 * half + q:2 * half + q + 1]), t, was, nstate["rst"])
            t2 = DV.add(lambda e, half=half, tv=tv: e.tensor_reduce(
                ssk[:, 4 * half:4 * half + 4], tv[:, 16:272].rearrange("p (m d) -> p m d", d=64), AX.X, ALU.add), t1)
            tmps.done(ti, t2)
            b3 = bank.rearrange("p (n d) -> p n d", n=2)[:, :, 128:256]
            for q in range(2):
                n, r = 2 * half + q, rs4[:, 2 * half + q:2 * half + q + 1]
                h = AC.add(lambda e: e.activation(vA[0][:, n, :], b3[:, q, :], ACT.Copy, scale=r), t)
            for q in range(2):
                n, r = 2 * half + q, rs4[:, 2 * half + q:2 * half + q + 1]
                l = DV.add(lambda e: e.scalar_tensor_tensor(vA[1][:, n, :], b3[:, q, :], r, f(vA[0][:, n, :]),
                                                            ALU.mult, ALU.subtract), h)
            vt += [h, l]
            got.append((bi, bv, t))
        tile_used(n_)
        tr = rsqrt_small(rk, ssk, 64, t2)
        rk4 = rk.rearrange("p (n g) -> p n g", n=4)
        tr = DV.add(lambda e: e.tensor_tensor(rk4, rk4, rs4.unsqueeze(2).broadcast_to([128, 4, 2]), ALU.mult), tr)
        for half in range(2):
            bi, bv, t = got[half]
            for u in range(2):
                tk = DV.add(lambda e, half=half, u=u, bv=bv: e.tensor_tensor(
                    kd[:, 2 * half:2 * half + 2, :, u, :], bv[:, :, 0:2, :],
                    rk4[:, 2 * half:2 * half + 2, :].unsqueeze(3).broadcast_to([128, 2, 2, 64]), ALU.mult), tr)
            banks.done(bi, tk, *vt)
        t_kd = tk
        sfree = [[], [], []]
        bfree = [[], []]
        pt_free = [[], []]
        heads = {}
        ssq, rq = small[:, 16:32], small[:, 32:48]
        q_t = {}
        aq = {}

        def q_unit(g, b):
            if b == 0:
                aq[g] = next_tile("aq", g, 1)
            n_, v_ = aq[g]
            bi, bank, t = proj_b(v_[0], 0, 256, 1, b, 256, 8, Hs)
            ti, tv, was = tmps.take()
            sq = tv[:, 16:272]
            t1 = AC.add(lambda e: e.activation(sq, bank[:, 0:256], ACT.Square, scale=rs4[:, b:b + 1]), t, was)
            t2 = DV.add(lambda e: e.tensor_reduce(ssq[:, 4 * b:4 * b + 4], sq.rearrange("p (m d) -> p m d", d=64),
                                                  AX.X, ALU.add), t1)
            tmps.done(ti, t2)
            t3 = AC.add(lambda e: e.activation(qt[:, b, :], bank[:, 0:256], ACT.Copy, scale=rs4[:, b:b + 1]), t,
                        bstate.get("qt_read"))
            banks.done(bi, t1, t3)
            q_t[g, b] = [t2, t3]
            if b == 3:
                tile_used(n_)

        def q_norm(g):
            tr = rsqrt_small(rq, ssq, 64, *[q_t[g, b] for b in range(4)])
            qv = qt.rearrange("p n (m d) -> p (n m) d", d=64)
            tk = DV.add(lambda e: e.tensor_tensor(qv, qv, rq.unsqueeze(2).broadcast_to([128, 16, 64]), ALU.mult), tr)
            q_t[g] = tk

        def q_turn(g):
            for hp in range(2):
                PE.wait(q_t[g])
                bi, bank, t = turn(lambda n: qt[:, n, 128 * hp:128 * hp + 128], 128)
                slot = 2 * (g % 2) + hp
                toks = scaled_pair(QT[slot], 128, bank, t, gq_a, qfree[slot])
                banks.done(bi, *toks)
                heads[2 * g + hp] = (QT[slot], toks)
            bstate["qt_read"] = t

        def load_bias(h):
            b = BR[h % 2]
            SP.dma(cs[f"bs{h % 2}"], b[:, 1:4, :], BS[h, 1:4].rearrange("n q s -> q n s"), bfree[h % 2], t_neg,
                   bstate["bw"])
            return SP.dma(cs[f"bs{h % 2}"], b[:, 0, 128:256], BS[h, 0, :, 128:256], bfree[h % 2])

        bias_t = {0: load_bias(0), 1: load_bias(1)}

        def scores(h):
            r, c = h % 2, h // 2
            qv, qtok = heads[c]
            kt, ktok = KT[h // 8]
            rows = slice(64 * r, 64 * r + 64)
            PE.wait(qtok, ktok)
            S = SS[h % 3]
            bt = bias_t[h]
            for m in range(2):
                bi, bank, was = banks.take()
                PE.wait(was)
                for n in (2 * m, 2 * m + 1):
                    o = 256 * (n % 2)
                    ql = [x[rows, 128 * n:128 * n + 128] for x in qv]
                    if n == 0:
                        for z in range(2):
                            t = mm3(bank[:, 128 * z:128 * z + 128], ql[0], ql[1], kt[0][rows, 0:128],
                                    kt[1][rows, 0:128], True, True)
                    else:
                        ks = slice(128 * (n - 1), 128 * (n + 1))
                        t = mm3(bank[:, o:o + 256], ql[0], ql[1], kt[0][rows, ks], kt[1][rows, ks], True, True)
                t1 = DV.add(lambda e: e.scalar_tensor_tensor(
                    S[:, 2 * m:2 * m + 2, :], bank.rearrange("p (n s) -> p n s", n=2), 0.125,
                    BR[h % 2][:, 2 * m:2 * m + 2, :], ALU.mult, ALU.add), t, bt, sfree[h % 3], t_neg)
                banks.done(bi, t1)
            bfree[h % 2] = [t1]
            if r == 1:
                qfree[c % 4] = [t]
            if h + 2 < 16:
                bias_t[h + 2] = load_bias(h + 2)
            x = 16 * (h % 4)
            mx, nm, sm_, es = (sm[:, 160 + x + 4 * i:164 + x + 4 * i] for i in range(4))
            t2 = DV.add(lambda e: e.tensor_reduce(mx, S, AX.X, ALU.max), t1)
            t3 = DV.add(lambda e: e.tensor_scalar(nm, mx, sinkc[:, h:h + 1], -1.0, ALU.max, ALU.mult), t2)
            for n in range(4):
                t4 = AC.add(lambda e: e.activation(S[:, n, :], S[:, n, :], ACT.Exp, bias=nm[:, n:n + 1],
                                                   accum_out=sm_[:, n:n + 1]), t3)
            return AC.add(lambda e: e.activation(es, nm, ACT.Exp, bias=sinkc[:, h:h + 1]), t4)

        def turns(h, te):
            S = SS[h % 3]
            slot = 4 + 2 * (h % 2)
            toks = []
            for m in range(2):
                bi, bank, was = banks.take()
                PE.wait(was, te)
                for i in range(4):
                    b = 4 * m + i
                    t = PE.add(lambda e: e.transpose(bank[:, 128 * i:128 * i + 128],
                                                     S[:, b // 2, 128 * (b % 2):128 * (b % 2) + 128], ident[:, :]))
                pr = pair(P, slot + m, t, bank, pt_free[h % 2])
                banks.done(bi, *pr)
                toks += pr
            sfree[h % 3] = [t]
            return toks

        oslot = {}

        def values(h, toks):
            slot = 4 + 2 * (h % 2)
            kv = h // 8
            bi, bank, was = banks.take()
            PE.wait(was, toks, vt)
            for n in range(4):
                js = [j for j in (n - 1, n) if j >= 0]
                for j in js:
                    b = 2 * n + (j - n + 1)
                    c, o = slot + b // 4, 128 * (b % 4)
                    t = mm3(bank[:, 64 * n:64 * n + 64], Ph[:, c, o:o + 128], Pl[:, c, o:o + 128],
                            vA[0][:, j, 64 * kv:64 * kv + 64], vA[1][:, j, 64 * kv:64 * kv + 64],
                            j == js[0], j == n)
            pt_free[h % 2] = [t]
            x = 16 * (h % 4)
            sm_, es = sm[:, 168 + x:172 + x], sm[:, 172 + x:176 + x]
            t1 = DV.add(lambda e: e.tensor_tensor(sm_, sm_, es, ALU.add), toks)
            t1 = DV.add(lambda e: e.reciprocal(sm_, sm_), t1)
            if h % 2 == 0:
                oslot[h // 2] = otmps.take()
            oi, ov, ow = oslot[h // 2]
            ot = ov[:, 16:528].rearrange("p (n d) -> p n d", n=4)
            r = 64 * (h % 2)
            t2 = DV.add(lambda e: e.tensor_tensor(ot[:, :, r:r + 64],
                                                  bank[:, 0:256].rearrange("p (n d) -> p n d", n=4),
                                                  sm_.unsqueeze(2).broadcast_to([128, 4, 64]), ALU.mult), t1, t, ow)
            banks.done(bi, t2)
            if h % 2:
                later.append(lambda: o_turn(h // 2, oi, ot, t2))

        def o_turn(c, oi, ot, t2):
            PE.wait(t2)
            bi, bank, t = turn(lambda n: ot[:, n, :], 128)
            otmps.done(oi, t)
            q = 8 + c % 4
            pready[q] = pair(P, q, t, bank, ofree[c % 4])
            banks.done(bi, *pready[q])

        later = []

        qfree = [[] for _ in range(4)]
        ofree = [[] for _ in range(4)]
        otmps = tmps.part(1)
        for b in range(4):
            q_unit(0, b)
        q_norm(0)
        KT = []
        for g in range(2):
            PE.wait(t_kd)
            bi, bank, t = turn(lambda n, g=g: kd[:, n, g, :, :].rearrange("p u d -> p (u d)"), 128)
            kt = (Ph[:, g, :], Pl[:, g, :])
            toks = scaled_pair(kt, 128, bank, t, gk_a)
            banks.done(bi, *toks)
            KT.append((kt, toks))
        t_kt = t
        q_turn(0)
        exps, pts = {}, {}
        LT, LV = 1, 2
        out_units = out_partial("ao", P, [8, 10], pready, ofree, banks, ("ffn_norm2_2", 0))
        sfree[2] = [t_kt]
        for i in range(16 + LV):
            g = i // 4
            if i == 12:
                h_read()
            if i < 16:
                exps[i] = scores(i)
            while later:
                later.pop()()
            if g < 3:
                for b in ((0, 1), (2,), (3,), ())[i % 4]:
                    q_unit(g + 1, b)
                if i % 4 == 2:
                    q_norm(g + 1)
            if i >= LV + 4:
                out_units(2)
            if LT <= i < 16 + LT:
                pts[i - LT] = turns(i - LT, exps[i - LT])
            if i >= LV:
                values(i - LV, pts[i - LV])
            if g < 3 and i % 4 == 3:
                q_turn(g + 1)
        while later:
            later.pop()()
        out_units(32)
        tmps.join(otmps)
        for q in range(16):
            pfree[q] = now()

    def attend_b():
        free0 = now()
        AC.wait(free0)
        DV.wait(free0)
        PO.wait(free0)
        Hs = (Hh, Hl, hready)
        cq = mflat(0, 2).rearrange("p (n d) -> p n d", n=4)
        ck = mflat(2, 3).rearrange("p (n d) -> p n d", n=4)
        kr = krt[:, :].rearrange("p (n d) -> p n d", n=4)
        ssq, ssc = small[:, 0:4], small[:, 4:8]
        rq, rc = small[:, 8:12], small[:, 12:16]
        nq, vq = next_tile("bq", 0)
        got, gok = [], []
        for half in range(2):
            bi, bank, t = proj_b(vq[0], 0, 256, 2, 2 * half, 256, 8, Hs)
            ti, tv, was = tmps.take()
            for q in range(2):
                t1 = AC.add(lambda e, q=q, half=half, tv=tv, bank=bank: e.activation(
                    tv[:, 16 + 256 * q:272 + 256 * q], bank[:, 256 * q:256 * q + 256], ACT.Square,
                    scale=rs4[:, 2 * half + q:2 * half + q + 1],
                    accum_out=ssq[:, 2 * half + q:2 * half + q + 1]), t, was, nstate["rst"])
            tmps.done(ti, t1)
            got.append((bi, bank, t))
        t_q = t1
        tile_used(nq)
        nk, vk = next_tile("bkv", 0)
        for half in range(2):
            bi, bank, t = proj_b(vk[0], 0, 160, 2, 2 * half, 160, 8, Hs)
            ti, tv, was = tmps.take()
            for q in range(2):
                AC.add(lambda e, q=q, half=half, tv=tv, bank=bank: e.activation(
                    tv[:, 16 + 160 * q:144 + 160 * q], bank[:, 160 * q:160 * q + 128], ACT.Square,
                    scale=rs4[:, 2 * half + q:2 * half + q + 1],
                    accum_out=ssc[:, 2 * half + q:2 * half + q + 1]), t, was)
                AC.add(lambda e, q=q, half=half, tv=tv, bank=bank: e.activation(
                    tv[:, 144 + 160 * q:176 + 160 * q], bank[:, 160 * q + 128:160 * q + 160], ACT.Square,
                    scale=rs4[:, 2 * half + q:2 * half + q + 1],
                    accum_out=kr2[:, 2 * half + q:2 * half + q + 1]))
                t1 = AC.add(lambda e, q=q, half=half, bank=bank: e.activation(
                    kr[:, 2 * half + q, :], bank[:, 160 * q + 128:160 * q + 160], ACT.Copy,
                    scale=rs4[:, 2 * half + q:2 * half + q + 1]))
            tmps.done(ti, t1)
            gok.append((bi, bank, t))
        tile_used(nk)
        t_kr = t1
        cready = []

        def latent(parts, w, wd, dst, r, ss, t_ss):
            t_r = rsqrt_small(r, ss, wd, t_ss)
            t_r = DV.add(mul3(r, r, rs4), t_r)
            for half, (bi, bank, t) in enumerate(parts):
                for q in range(2):
                    n = 2 * half + q
                    tk = DV.add(lambda e: e.tensor_scalar(dst[:, n, :], bank[:, w * q:w * q + wd], r[:, n:n + 1], None,
                                                          ALU.mult), t_r)
                banks.done(bi, tk, t_kr)
            return tk

        def latent_turn(dst, chunks, tk):
            PE.wait(tk)
            for i, (c, g) in enumerate(chunks):
                bi, bank, t = turn(lambda n: dst[:, n, 128 * i:128 * i + 128], 128)
                toks = scaled_pair((Ph[:, c, :], Pl[:, c, :]), 128, bank, t, g)
                banks.done(bi, *toks)
                cready.append(toks)
            return t

        tq_ = latent(got, 256, 256, cq, rq, ssq, t_q)
        tk_ = latent(gok, 160, 128, ck, rc, ssc, t_kr)
        t_cn = tk_
        latent_turn(cq, [(0, gain("b_q_norm_2", 0)), (1, gain("b_q_norm_2", 1))], tq_)
        t = latent_turn(ck, [(2, gain("b_kv_norm_2", 0))], tk_)
        t_c = t
        Cq = (Ph, Pl, cready)
        Ck = (Ph[:, 2:3, :], Pl[:, 2:3, :], cready[2:3])

        qts = [x.rearrange("p (n h d) -> p n h d", n=4, h=2) for x in (mflat(0, 3)[:, 0:768], mflat(0, 3)[:, 768:1536])]
        kts = [x.rearrange("p (n h d) -> p n h d", n=4, h=2) for x in (mflat(3, 6)[:, 0:768], mflat(3, 6)[:, 768:1536])]
        ots = [M[:, 6 + i, :].rearrange("p (n d) -> p n d", n=4) for i in range(2)]
        vBs = [[W[:, 3 + i, :].rearrange("p (n h d) -> p n h d", n=4, h=2) for W in P] for i in range(2)]
        QK = [((Ph[:, 5, :], Pl[:, 5, :]), (Ph[:, 6, :], Pl[:, 6, :])),
              ((Ph[:, 7, :], Pl[:, 7, :]), (Ph[:, 8, :], Pl[:, 8, :]))]
        ER = Ring([Z[:, 512 * i:512 * i + 512] for i in range(4)])
        PT = Ring([9, 10, 11, 12])
        sc = 96 ** -0.5
        qkfree = [[], []]
        tread, vread, oread = [[t_c], [t_c]], [[], []], [[], []]
        bg = {}
        qkv_t = {}

        def prep_unit(g, u):
            if u == 0 and g % 2 == 0:
                bg[g // 2] = next_tile("bg", g // 2, 1)
            n_, v_ = bg[g // 2]
            x, half = g % 2, u % 2
            ss = small[:, 16 * x + 8 * (u // 2) + 4 * half:16 * x + 8 * (u // 2) + 4 * half + 4]
            ti, tv, was = tmps.take()
            tb = slice(2 * half, 2 * half + 2)
            if u < 2:
                bi, bank, t = proj_b(v_[0], 192 * x, 192, 2, 2 * half, 256, 2, Cq, banks2)
                src = bank.rearrange("p (n d) -> p n d", n=2)[:, :, 0:192]
                sq = tv[:, 16:400]
                t1 = AC.add(lambda e: e.activation(sq.rearrange("p (n d) -> p n d", n=2), src, ACT.Square), t, was)
                t2 = DV.add(lambda e: e.tensor_reduce(ss, sq.rearrange("p (m d) -> p m d", m=4), AX.X, ALU.add), t1,
                            rdone.get(g - 2))
                t3 = AC.add(lambda e: e.activation(qts[x][:, tb, :, :].rearrange("p n h d -> p n (h d)"), src,
                                                   ACT.Copy), t, tread[x])
                banks2.done(bi, t1, t3)
            else:
                bi, bank, t = proj_b(v_[1], 256 * x, 256, 2, 2 * half, 256, 1, Ck, banks2)
                bv = bank.rearrange("p (m d) -> p m d", m=4)
                sq = tv[:, 16:272].rearrange("p (m d) -> p m d", m=4)
                t1 = AC.add(lambda e: e.activation(sq, bv[:, :, 0:64], ACT.Square), t, was)
                t2 = DV.add(lambda e: e.tensor_reduce(ss, sq, AX.X, ALU.add), t1, rdone.get(g - 2))
                b4 = bank.rearrange("p (n h d) -> p n h d", n=2, h=2)
                t3 = AC.add(lambda e: e.activation(kts[x][:, tb, :, 0:64], b4[:, :, :, 0:64], ACT.Copy), t, tread[x])
                vh_, vl_ = vBs[x][0][:, tb, :, :], vBs[x][1][:, tb, :, :]
                h = AC.add(lambda e: e.activation(vh_, b4[:, :, :, 64:128], ACT.Copy), t, vread[x])
                l = DV.add(lambda e: e.tensor_tensor(vl_, b4[:, :, :, 64:128], f(vh_), ALU.subtract), h, vread[x])
                banks2.done(bi, t1, t3, h, l)
                qkv_t[g, 4 + half] = [h, l]
            tmps.done(ti, t2)
            qkv_t[g, u] = [t2, t3]
            if u == 3 and g % 2 == 1:
                tile_used(n_)

        rdone = {-2: t_cn, -1: t_cn}
        scaled = {}

        def prep_norm(g):
            x = g % 2
            ss, r = small[:, 16 * x:16 * x + 16], small[:, 32 + 16 * x:48 + 16 * x]
            wait = [qkv_t[g, u] for u in range(4)]
            t = DV.add(lambda e: e.tensor_tensor(ss[:, 8:16].rearrange("p (n h) -> p n h", n=4),
                                                 ss[:, 8:16].rearrange("p (n h) -> p n h", n=4),
                                                 kr2.unsqueeze(2).broadcast_to([128, 4, 2]), ALU.add), wait)
            tr = rsqrt_small(r, ss, 96, t, tread[x])
            rdone[g] = tr

        def prep_scale(g):
            x = g % 2
            qt, kt = qts[x], kts[x]
            r, tr = small[:, 32 + 16 * x:48 + 16 * x], rdone[g]
            rq, rk = r[:, 0:8], r[:, 8:16]
            qf = qt.rearrange("p n h d -> p (n h) d")
            kf = kt.rearrange("p n h d -> p (n h) d")
            tq = DV.add(lambda e: e.tensor_tensor(qf, qf, rq.unsqueeze(2).broadcast_to([128, 8, 96]), ALU.mult), tr)
            PO.add(lambda e: e.tensor_tensor(kt[:, :, :, 64:96], kr.unsqueeze(2).broadcast_to([128, 4, 2, 32]),
                                             rk.rearrange("p (n h) -> p n h", n=4).unsqueeze(3)
                                             .broadcast_to([128, 4, 2, 32]), ALU.mult), tr, t_kr, tread[x])
            tk = PO.add(lambda e: e.tensor_tensor(kf[:, :, 0:64], kf[:, :, 0:64],
                                                  rk.unsqueeze(2).broadcast_to([128, 8, 64]), ALU.mult), tr)
            scaled[g] = tq, tk

        def prep_turn(g):
            x = g % 2
            qt, kt = qts[x], kts[x]
            tq, tk = scaled[g]
            done = []
            for E, tens, base, t0, tmp in ((DV, qt, 0, tq, rt[0]), (PO, kt, 4, tk, rt[1])):
                tmp = [tmp[:, 128 * i:128 * i + 128].rearrange("p (n h d) -> p n h d", n=4, h=2) for i in range(4)]
                a1, a2 = tens[:, :, :, 64:80], tens[:, :, :, 80:96]
                tab = [ropt[:, base + j, :].rearrange("p (n d) -> p n d", n=4).unsqueeze(2)
                       .broadcast_to([128, 4, 2, 16]) for j in range(4)]
                for o, i, j in ((0, a1, 0), (1, a2, 1), (2, a2, 2), (3, a1, 3)):
                    t = E.add(mul3(tmp[o], i, tab[j]), t0, bstate["rope"], rtfree[base // 4])
                E.add(lambda e: e.tensor_tensor(a1, tmp[0], tmp[1], ALU.subtract), t)
                t = E.add(lambda e: e.tensor_tensor(a2, tmp[2], tmp[3], ALU.add), t)
                rtfree[base // 4] = t
                done.append(t)
            return done

        rtfree = [free0, free0]
        rtm = tmps.part(2)
        rt = [v[:, 16:528] for v in rtm.views]

        def head_qk(h, done):
            x, hl, s = (h // 2) % 2, h % 2, h % 2
            PE.wait(done)
            res = []
            for src, dst, gcol in ((qts[x], QK[s][0], gq_b), (kts[x], QK[s][1], gk_b)):
                bi, bank, t = turn(lambda n: src[:, n, hl, :], 96)
                toks = scaled_pair([d[0:96, :] for d in dst], 96, bank[0:96, :], t, gcol[0:96, :], qkfree[s], t_g1)
                banks.done(bi, *toks)
                res += toks
            if hl == 1:
                tread[x] = [t]
            return res

        def scores(h, n, ready):
            s = h % 2
            (qh, ql), (kh, kl) = QK[s]
            L = 128 * (n + 1)
            bi, bank, was = banks.take()
            PE.wait(was, ready)
            qs = slice(128 * n, 128 * n + 128)
            PE.add(lambda e: e.matmul(bank[:, 0:L], ql[0:96, qs], kh[0:96, 0:L], start=True, stop=False), signal=False)
            PE.add(lambda e: e.matmul(bank[:, 0:L], qh[0:96, qs], kl[0:96, 0:L], start=False, stop=False),
                   signal=False)
            PE.add(lambda e: e.matmul(bank[:, 0:L], qh[0:96, qs], kh[0:96, 0:L], start=False, stop=False),
                   signal=False)
            t = PE.add(lambda e: e.matmul(bank[:, 128 * n:L], identb[:, :], maskb[:, :], start=False, stop=True))
            if n == 3:
                qkfree[s] = [t]
            x = (h % 4) * 4 + n
            mx = mneg[:, x:x + 1]
            nm = mneg[:, 16 + x:17 + x]
            t1 = DV.add(lambda e: e.tensor_reduce(mx, bank[:, 0:L], AX.X, ALU.max), t)
            t1 = DV.add(lambda e: e.tensor_scalar(nm, mx, -sc, None, ALU.mult), t1)
            ei, E, w = ER.take()
            y = (h % 8) * 4 + n
            t2 = AC.add(lambda e: e.activation(E[:, 0:L], bank[:, 0:L], ACT.Exp, bias=nm, scale=sc,
                                               accum_out=sums[:, y:y + 1]), t1, w)
            banks.done(bi, t2)
            return ei, E, t2

        def turns(n, ei, E, te):
            L = 128 * (n + 1)
            bi, bank, was = banks.take()
            PE.wait(was, te)
            for j in range(n + 1):
                t = PE.add(lambda e: e.transpose(bank[:, 128 * j:128 * j + 128], E[:, 128 * j:128 * j + 128],
                                                 ident[:, :]))
            ER.done(ei, t)
            pi, slot, w = PT.take()
            hh = AC.add(lambda e: e.activation(Ph[:, slot, 0:L], bank[:, 0:L], ACT.Copy), t, w)
            ll = DV.add(lambda e: e.tensor_tensor(Pl[:, slot, 0:L], bank[:, 0:L], f(Ph[:, slot, 0:L]), ALU.subtract),
                        hh, w)
            banks.done(bi, hh, ll)
            return pi, slot, [hh, ll]

        obank = {}

        def values(h, n, pi, slot, toks, vts):
            x, hl = (h // 2) % 2, h % 2
            if n == 0:
                obank[h] = obanks.take()
            bi, bank, was = obank[h]
            PE.wait(was, toks, vts)
            for j in range(n + 1):
                sl = slice(128 * j, 128 * j + 128)
                t = mm3(bank[:, 64 * n:64 * n + 64], Ph[:, slot, sl], Pl[:, slot, sl], vBs[x][0][:, j, hl, :],
                        vBs[x][1][:, j, hl, :], j == 0, j == n)
            PT.done(pi, t)
            if n < 3:
                return
            y = (h % 8) * 4
            t1 = DV.add(lambda e: e.reciprocal(sums[:, y:y + 4], sums[:, y:y + 4]), toks)
            t2 = DV.add(lambda e: e.tensor_tensor(ots[x][:, :, 64 * hl:64 * hl + 64],
                                                  bank[:, 0:256].rearrange("p (n d) -> p n d", n=4),
                                                  sums[:, y:y + 4].unsqueeze(2).broadcast_to([128, 4, 64]),
                                                  ALU.mult), t1, t, oread[x])
            obanks.done(bi, t2)
            if hl == 1:
                vread[x] = [t]
                later.append(lambda: o_turn(h // 2, x, t2))

        def o_turn(c, x, t2):
            PE.wait(t2)
            bi, bank, t = turn(lambda n: ots[x][:, n, :], 128)
            oread[x] = [t]
            oready[c] = pair(H, c, t, bank)
            banks.done(bi, *oready[c])

        later = []

        obanks = banks.part(1)
        banks2 = banks.part(2)

        def units(g):
            yield lambda: prep_unit(g, 0)
            yield lambda: prep_unit(g, 1)
            yield lambda: prep_unit(g, 2)
            yield lambda: prep_unit(g, 3)
            yield lambda: prep_norm(g)
            yield lambda: prep_scale(g)
            yield lambda: ready.update({g: prep_turn(g)})

        ready = {}
        out_units = out_partial("bo", H, [0, 2, 4, 6], oready, [[] for _ in range(8)], banks2, late=5)
        first, second = list(units(0)), list(units(1))
        for u in first[0:5] + second[0:4] + first[5:7]:
            u()
        items = [(h, n) for h in range(16) for n in range(4)]
        sco, tur, qk = {}, {}, {0: head_qk(0, ready[0])}
        LT, LV = 2, 3
        STEPS = (1, 1, 0, 1, 1, 1, 2, 0)
        queue = []
        for i in range(len(items) + LV):
            if i < len(items):
                h, n = items[i]
                if n == 0 and h % 2 == 0 and h // 2 < 7:
                    queue = list(units(h // 2 + 1)) if h else second[4:7]
                sco[i] = scores(h, n, qk[h])
            while later:
                later.pop()()
            if i < len(items):
                for _ in range(STEPS[i % 8]):
                    if queue:
                        queue.pop(0)()
                if n == 2 and h % 2 == 0:
                    qk[h + 1] = head_qk(h + 1, ready[h // 2])
                if n == 3 and h % 2 == 1 and h < 15:
                    qk[h + 1] = head_qk(h + 1, ready[h // 2 + 1])
            if i >= 16 + LV + 1 and (i - LV) % 2 == 0:
                out_units(1)
            if i >= LT and i - LT < len(items):
                tur[i - LT] = turns(items[i - LT][1], *sco.pop(i - LT))
            if i >= LV:
                h, n = items[i - LV]
                g = h // 2
                values(h, n, *tur.pop(i - LV), [qkv_t[g, 4], qkv_t[g, 5]])
        while later:
            later.pop()()
        out_units(32)
        banks.join(banks2)
        banks.join(obanks)
        tmps.join(rtm)
        for q in range(16):
            pfree[q] = now()

    oready = [[] for _ in range(8)]

    bstate["mfree"] = now()
    bstate["t"] = now()
    plan_bias()
    norm_begin_twice(RF, now())
    ffn("s0", "glu", "mix_norm_2", 0)
    while extras:
        extra(1)
    norm_begin_rows()
    state["low"] = PO
    attend_a()
    state["low"] = DV
    t_aa = now()
    extras.append(lambda: trig(t_aa))
    extras.append(lambda: bstate.update(rope=tables()))
    norm_begin(RF, now())
    ffn("s1", "glu", "ffn_norm1_2", 8)
    norm_begin(RF, now())
    ffn("s2", "glu", "mix_norm_2", 8)
    norm_begin_rows()
    state["low"] = PO
    attend_b()
    state["low"] = DV
    h_read()
    for c in range(8):
        h_pair(c, "ffn_norm2_2", 8)
    for c in range(5, 8):
        stats(c)
    norm_begin(RF, now(), steps=(1, 3))
    ffn("s3", "glu")

    out_tile(3)
    SP.wait(bstate["out"], bstate["bw"], bstate.get("fill"), bstate["pos"])


INS = ['x', 'p', 'mix_norm', 'w_in', 'w_pool', 'pool_scale', 'sgu_norm', 'w_spatial', 'b_spatial', 'w_branch_a',
       'w_branch_b', 'w_out', 'ffn_norm', 'w_up', 'conv_w', 'conv_b', 'w_down', 'ple_norm', 'w_ple_gate', 'w_ple',
       'final_norm', 'positions_2', 'rel_bias_2', 'ffn_norm1_2', 'ffn1_wg_2', 'ffn1_wu_2', 'ffn1_wd_2', 'mix_norm_2',
       'ffn_norm2_2', 'ffn2_wg_2', 'ffn2_wu_2', 'ffn2_wd_2', 'a_w_in_2', 'a_q_gain_2', 'a_k_gain_2', 'a_sinks_2',
       'a_w_out_2', 'b_w_in_2', 'b_q_norm_2', 'b_kv_norm_2', 'b_w_uq_2', 'b_w_ukv_2', 'b_q_gain_2', 'b_k_gain_2',
       'b_w_out_2']


def kernel(**inputs):
    import numpy as _np
    import concourse.bacc as _bacc
    from concourse import mybir as _mybir
    from concourse.bass_utils import run_bass_kernel_spmd as _run

    nc = _bacc.Bacc("TRN2", target_bir_lowering=False, num_devices=1, dynamic_dma_scratch_size=1024)
    arrays, args = {}, {}
    for name in INS:
        v = _np.ascontiguousarray(inputs[name])
        arrays[f"in_{name}"] = v
        args[name] = nc.dram_tensor(f"in_{name}", v.shape, _mybir.dt.from_np(v.dtype), kind="ExternalInput").ap()
    out = nc.dram_tensor("out_0", (1, T, D), F32, kind="ExternalOutput").ap()
    program(nc, args, out)
    r = _run(nc, [arrays], core_ids=[0])
    return r.results[0]["out_0"]
```
